# Optimizing a Trainium2 kernel written in Bass

```python
import math
import jax
import jax.numpy as jnp
from jax import lax
import numpy as np

D_MODEL = 1024
BATCH = 1
SEQ = 512
DEPTH = 1
DEC_BATCH = 1
DEC_SEQ = 64
PAST_LEN = 512

CHUNK = 64
N_META = 16
POOL_WINDOWS = (2, 4, 8, 16)
N_POOL_GROUPS = 4
POOL_WIDTH = D_MODEL // 2
POOL_GROUP = POOL_WIDTH // N_POOL_GROUPS
POOL_STATE = max(POOL_WINDOWS) - 1
SB_HEADS = 8
SB_HEAD_DIM = 64
SB_WIDTH = SB_HEADS * SB_HEAD_DIM
Q_BLOCK = 128
N_GROUPS = 4
EXPERTS_PER_GROUP = 8
N_EXPERTS = N_GROUPS * EXPERTS_PER_GROUP
TOP_K = 2
D_EXPERT = D_MODEL // 2
MOE_BLOCK = 256
NORM_EPS = 1e-6
IN_SPLITS = (POOL_WIDTH, POOL_WIDTH + SB_WIDTH, POOL_WIDTH + 2 * SB_WIDTH,
             POOL_WIDTH + 3 * SB_WIDTH, POOL_WIDTH + 3 * SB_WIDTH + D_MODEL)
IN_WIDTH = POOL_WIDTH + 3 * SB_WIDTH + 2 * D_MODEL

kernel_name = 'hybrid_pool_stickbreak_hmoe_step'

def rms_norm(x, g):
    xf = x.astype(jnp.float32)
    y = xf * lax.rsqrt(jnp.mean(xf * xf, axis=-1, keepdims=True) + NORM_EPS)
    return (y * g.astype(jnp.float32)).astype(x.dtype)

def multiscale_pool(u, prefix, offset, pool_mix, pool_scale):
    b, n, _ = u.shape
    uf = u.astype(jnp.float32)
    ext = jnp.concatenate([prefix.astype(jnp.float32), uf], axis=1)
    cs = jnp.concatenate([jnp.zeros_like(ext[:, :1]), jnp.cumsum(ext, axis=1)], axis=1)
    hi = cs[:, POOL_STATE + 1:POOL_STATE + 1 + n]
    t = jnp.arange(n)
    groups = []
    for gi, w in enumerate(POOL_WINDOWS):
        c0, c1 = gi * POOL_GROUP, (gi + 1) * POOL_GROUP
        lo = cs[:, POOL_STATE + 1 - w:POOL_STATE + 1 - w + n, c0:c1]
        cnt = jnp.minimum(w, t + 1 + offset).astype(jnp.float32)[None, :, None]
        groups.append((hi[..., c0:c1] - lo) / cnt - uf[..., c0:c1])
    pooled = jnp.stack(groups, axis=2)
    mixed = jnp.einsum('bngc,gcd->bngd', pooled, pool_mix.astype(jnp.float32))
    return (mixed.reshape(b, n, POOL_WIDTH) * pool_scale.astype(jnp.float32)).astype(u.dtype)

def stick_breaking_block(q, qpos, k, v, kpos):
    z = jnp.einsum('bqhd,bkhd->bhqk', q, k) * (SB_HEAD_DIM ** -0.5)
    mask = kpos[None, :] < qpos[:, None]
    log_keep = jnp.where(mask, jax.nn.log_sigmoid(-z), 0.0)
    after = lax.cumsum(log_keep, axis=3, reverse=True) - log_keep
    a = jnp.where(mask, jnp.exp(jax.nn.log_sigmoid(z) + after), 0.0)
    return jnp.einsum('bhqk,bkhd->bqhd', a, v)

def stick_breaking_prompt(q, k, v):
    b, n = q.shape[:2]
    nb = -(-n // Q_BLOCK)
    pad = nb * Q_BLOCK - n
    qb = jnp.pad(q.astype(jnp.float32), ((0, 0), (0, pad), (0, 0), (0, 0)))
    qb = qb.reshape(b, nb, Q_BLOCK, SB_HEADS, SB_HEAD_DIM).transpose(1, 0, 2, 3, 4)
    qpos = jnp.arange(nb * Q_BLOCK).reshape(nb, Q_BLOCK)
    kf = k.astype(jnp.float32)
    vf = v.astype(jnp.float32)
    kpos = jnp.arange(n)
    out = lax.map(lambda blk: stick_breaking_block(blk[0], blk[1], kf, vf, kpos), (qb, qpos))
    out = out.transpose(1, 0, 2, 3, 4).reshape(b, nb * Q_BLOCK, SB_HEADS, SB_HEAD_DIM)
    return out[:, :n].astype(q.dtype)

def stick_breaking_step(q, k, v, k_past, v_past):
    s = q.shape[1]
    past = k_past.shape[1]
    k_all = jnp.concatenate([k_past.astype(jnp.float32), k.astype(jnp.float32)], axis=1)
    v_all = jnp.concatenate([v_past.astype(jnp.float32), v.astype(jnp.float32)], axis=1)
    qpos = past + jnp.arange(s)
    kpos = jnp.arange(past + s)
    out = stick_breaking_block(q.astype(jnp.float32), qpos, k_all, v_all, kpos)
    return out.astype(q.dtype)

def hier_route(hf, w_rg, b_rg, w_re, b_re):
    n = hf.shape[0]
    x32 = hf.astype(jnp.float32)
    rows = jnp.arange(n)
    cg = x32 @ w_rg.astype(jnp.float32) + b_rg.astype(jnp.float32)
    g_idx = jnp.argmax(cg, axis=-1)
    p_g = jax.nn.softmax(cg, axis=-1)[rows, g_idx]
    fe = (x32 @ w_re.astype(jnp.float32) + b_re.astype(jnp.float32)).reshape(n, N_GROUPS, EXPERTS_PER_GROUP)
    p_e = jax.nn.softmax(fe[rows, g_idx], axis=-1)
    top_p, top_i = lax.top_k(p_e, TOP_K)
    top_p = top_p / jnp.sum(top_p, axis=-1, keepdims=True)
    experts = g_idx[:, None].astype(jnp.int32) * EXPERTS_PER_GROUP + top_i.astype(jnp.int32)
    return experts, top_p * p_g[:, None]

def hier_moe(h, w_rg, b_rg, w_re, b_re, w_gate, w_up, w_down):
    b, n, d = h.shape
    ntok = b * n
    hf = h.reshape(ntok, d)
    experts, weights = hier_route(hf, w_rg, b_rg, w_re, b_re)
    n_assign = ntok * TOP_K
    e_flat = experts.reshape(n_assign)
    order = jnp.argsort(e_flat)
    e_sorted = e_flat[order]
    counts = jnp.bincount(e_flat, length=N_EXPERTS)
    padded = (counts + MOE_BLOCK - 1) // MOE_BLOCK * MOE_BLOCK
    starts = jnp.cumsum(counts) - counts
    pends = jnp.cumsum(padded)
    pstarts = pends - padded
    dest_sorted = pstarts[e_sorted] + jnp.arange(n_assign) - starts[e_sorted]
    cap = -(-(n_assign + N_EXPERTS * (MOE_BLOCK - 1)) // MOE_BLOCK) * MOE_BLOCK
    nblk = cap // MOE_BLOCK
    buf = jnp.zeros((cap, d), h.dtype).at[dest_sorted].set(hf[order // TOP_K])
    blk_e = jnp.minimum(jnp.searchsorted(pends, jnp.arange(nblk) * MOE_BLOCK, side='right'), N_EXPERTS - 1)

    def expert_block(args):
        xb, e = args
        gate = xb @ w_gate[e]
        up = xb @ w_up[e]
        return (jax.nn.silu(gate) * up) @ w_down[e]

    yb = lax.map(expert_block, (buf.reshape(nblk, MOE_BLOCK, d), blk_e)).reshape(cap, d)
    dest = jnp.zeros((n_assign,), jnp.int32).at[order].set(dest_sorted.astype(jnp.int32))
    y = yb[dest].reshape(ntok, TOP_K, d).astype(jnp.float32)
    out = jnp.einsum('nkd,nk->nd', y, weights)
    return out.astype(h.dtype).reshape(b, n, d)

def trunk_layer(h, pool_prefix, pool_offset, k_past, v_past,
                norm_mix, w_in, q_norm, k_norm, pool_mix, pool_scale,
                w_pool_out, w_sb_out, w_o, norm_ffn,
                w_router_group, b_router_group, w_router_expert, b_router_expert,
                w_gate, w_up, w_down):
    b, n, _ = h.shape
    hn = rms_norm(h, norm_mix)
    z = hn @ w_in
    u, q, k, v, g_pool, g_sb = jnp.split(z, IN_SPLITS, axis=-1)
    q = rms_norm(q.reshape(b, n, SB_HEADS, SB_HEAD_DIM), q_norm)
    k = rms_norm(k.reshape(b, n, SB_HEADS, SB_HEAD_DIM), k_norm)
    v = v.reshape(b, n, SB_HEADS, SB_HEAD_DIM)
    pool_out = multiscale_pool(u, pool_prefix, pool_offset, pool_mix, pool_scale)
    if k_past is None:
        sb_out = stick_breaking_prompt(q, k, v)
    else:
        sb_out = stick_breaking_step(q, k, v, k_past, v_past)
    merged = (jax.nn.sigmoid(g_pool) * (pool_out @ w_pool_out)
              + jax.nn.sigmoid(g_sb) * (sb_out.reshape(b, n, SB_WIDTH) @ w_sb_out))
    h = h + merged @ w_o
    h = h + hier_moe(rms_norm(h, norm_ffn), w_router_group, b_router_group,
                     w_router_expert, b_router_expert, w_gate, w_up, w_down)
    new_pool = jnp.concatenate([pool_prefix.astype(u.dtype), u], axis=1)[:, -POOL_STATE:]
    return h, k, v, new_pool

def setup_inputs(seed: int = 0) -> dict:
    key = jax.random.key(seed)
    ks = jax.random.split(key, 24)

    def nrm(k, shape, scale):
        return jax.random.normal(k, shape, jnp.float32) * scale

    return {
        'x_prompt': nrm(ks[0], (BATCH, SEQ, D_MODEL), 1.0),
        'x_sample': nrm(ks[1], (DEC_BATCH, DEC_SEQ, D_MODEL), 1.0),
        'cache_sb_k': nrm(ks[2], (DEPTH, DEC_BATCH, PAST_LEN, SB_HEADS, SB_HEAD_DIM), 1.0),
        'cache_sb_v': nrm(ks[3], (DEPTH, DEC_BATCH, PAST_LEN, SB_HEADS, SB_HEAD_DIM), 1.0),
        'state_pool': nrm(ks[4], (DEPTH, DEC_BATCH, POOL_STATE, POOL_WIDTH), 1.0),
        'meta_tokens': nrm(ks[5], (N_META, D_MODEL), 1.0),
        'norm_mix': 1.0 + nrm(ks[6], (DEPTH, D_MODEL), 0.02),
        'w_in': nrm(ks[7], (DEPTH, D_MODEL, IN_WIDTH), D_MODEL ** -0.5),
        'q_norm': 1.0 + nrm(ks[8], (DEPTH, SB_HEAD_DIM), 0.02),
        'k_norm': 1.0 + nrm(ks[9], (DEPTH, SB_HEAD_DIM), 0.02),
        'pool_mix': nrm(ks[10], (DEPTH, N_POOL_GROUPS, POOL_GROUP, POOL_GROUP), POOL_GROUP ** -0.5),
        'pool_scale': 1.0 + nrm(ks[11], (DEPTH, POOL_WIDTH), 0.1),
        'w_pool_out': nrm(ks[12], (DEPTH, POOL_WIDTH, D_MODEL), POOL_WIDTH ** -0.5),
        'w_sb_out': nrm(ks[13], (DEPTH, SB_WIDTH, D_MODEL), SB_WIDTH ** -0.5),
        'w_o': nrm(ks[14], (DEPTH, D_MODEL, D_MODEL), D_MODEL ** -0.5),
        'norm_ffn': 1.0 + nrm(ks[15], (DEPTH, D_MODEL), 0.02),
        'w_router_group': nrm(ks[16], (DEPTH, D_MODEL, N_GROUPS), D_MODEL ** -0.5),
        'b_router_group': nrm(ks[17], (DEPTH, N_GROUPS), 0.01),
        'w_router_expert': nrm(ks[18], (DEPTH, D_MODEL, N_EXPERTS), D_MODEL ** -0.5),
        'b_router_expert': nrm(ks[19], (DEPTH, N_EXPERTS), 0.01),
        'w_gate': nrm(ks[20], (DEPTH, N_EXPERTS, D_MODEL, D_EXPERT), D_MODEL ** -0.5),
        'w_up': nrm(ks[21], (DEPTH, N_EXPERTS, D_MODEL, D_EXPERT), D_MODEL ** -0.5),
        'w_down': nrm(ks[22], (DEPTH, N_EXPERTS, D_EXPERT, D_MODEL), D_EXPERT ** -0.5),
    }

def reference(x_prompt, x_sample, cache_sb_k, cache_sb_v, state_pool, meta_tokens,
              norm_mix, w_in, q_norm, k_norm, pool_mix, pool_scale, w_pool_out, w_sb_out, w_o,
              norm_ffn, w_router_group, b_router_group, w_router_expert, b_router_expert,
              w_gate, w_up, w_down):
    b = x_prompt.shape[0]
    meta = jnp.broadcast_to(meta_tokens.astype(x_prompt.dtype)[None], (b, N_META, D_MODEL))
    hp = jnp.concatenate([meta, x_prompt], axis=1)
    hs = x_sample
    zero_prefix = jnp.zeros((b, POOL_STATE, POOL_WIDTH), x_prompt.dtype)
    kp_l, vp_l, pp_l, ks_l, vs_l, ps_l = [], [], [], [], [], []
    for l in range(DEPTH):
        lw = (norm_mix[l], w_in[l], q_norm[l], k_norm[l], pool_mix[l], pool_scale[l],
              w_pool_out[l], w_sb_out[l], w_o[l], norm_ffn[l],
              w_router_group[l], b_router_group[l], w_router_expert[l], b_router_expert[l],
              w_gate[l], w_up[l], w_down[l])
        hp, kp, vp, pp = trunk_layer(hp, zero_prefix, 0, None, None, *lw)
        hs, ks, vs, ps = trunk_layer(hs, state_pool[l], POOL_STATE, cache_sb_k[l], cache_sb_v[l], *lw)
        kp_l.append(kp)
        vp_l.append(vp)
        pp_l.append(pp)
        ks_l.append(ks)
        vs_l.append(vs)
        ps_l.append(ps)
    return (hp[:, N_META:], hs, jnp.stack(kp_l), jnp.stack(vp_l), jnp.stack(pp_l),
            jnp.stack(ks_l), jnp.stack(vs_l), jnp.stack(ps_l))


_drawn_inputs = setup_inputs


def setup_inputs(seed=0):
    import zlib

    import numpy as np

    out = dict(_drawn_inputs(seed))
    spreads = {}
    factors = {'q_norm': 11.848, 'b_router_group': 11.201, 'b_router_expert': 3.095}
    for name, (base, spread) in spreads.items():
        noise = np.random.default_rng([zlib.crc32(name.encode()), seed]).standard_normal(out[name].shape)
        drawn = base * np.exp(spread * noise) if base else spread * noise
        out[name] = jnp.asarray(drawn.astype(out[name].dtype))
    for name, factor in factors.items():
        out[name] = (out[name] * factor).astype(out[name].dtype)
    return out
```

```python
from contextlib import ExitStack

import concourse.bass as bass
from concourse import mybir

F32 = mybir.dt.float32
BF16 = mybir.dt.bfloat16
I32 = mybir.dt.int32
U32 = mybir.dt.uint32
ALU = mybir.AluOpType
ACT = mybir.ActivationFunctionType
AX = mybir.AxisListType

P = 128
BANK = 512
D = 1024
KD = D // P
SEQ, META, SAMP, PAST = 512, 16, 64, 512
HEADS, HD = 8, 64
PAIRS = HEADS // 2
W = HEADS * HD
KW = W // P
POOL_STATE = 15
EPS = 1e-6
FRAME_TILES = SEQ // P
TILES = FRAME_TILES + 1
SM = SAMP + META
TOK = SEQ + SAMP
ALL = TOK + META
UW = META + SEQ + POOL_STATE + SAMP
GROUPS, PER_GROUP, EXPERTS = 4, 8, 32
TOP = 2
F = 512
KF = F // P
SLOTS = 128
J = -(-TOK // SLOTS)
EXTRA = TOK * TOP // SLOTS
NBLK = EXPERTS + EXTRA
RING = 6
SLOT = KD * BANK
NEG = -1.0e30
EMPTY = 1.0e6

TILE_ROWS = [P] * FRAME_TILES + [SM]
TOK_ROWS = [P] * FRAME_TILES + [SAMP]
TILE_COL = [SM + P * t for t in range(FRAME_TILES)] + [0]
TOK_COL = [SAMP + P * t for t in range(FRAME_TILES)] + [0]


def stream_index():
    order = ["k", "q", "u", "v", ("gate", 0, 0), ("gate", 0, 1), ("out", 0), ("gate", 1, 0), ("gate", 1, 1),
             ("out", 1), ("wo", 0), ("wo", 1)]
    return {name: n for n, name in enumerate(order)}


STREAM = stream_index()
FRONT = len(STREAM)


def expert_stream(kind, e):
    if kind == "down":
        return FRONT + 3 * e + 4 if (not isinstance(e, int) or e < EXPERTS - 1) else FRONT + 3 * EXPERTS - 1
    first = FRONT + 3 * e - 1 if (not isinstance(e, int) or e > 0) else FRONT
    return first + (kind == "up")


def attention_units():
    units = []
    for pair in range(PAIRS):
        for block in range(FRAME_TILES):
            units += [(pair, block, 0), (pair, block, 1)]
        units.append((pair, FRAME_TILES, 0))
    return units


UNITS = attention_units()
GROUP_OF = []
for _n, (_pair, _block, _hh) in enumerate(UNITS):
    GROUP_OF.append(GROUP_OF[-1] + (_hh == 0) if _n else 0)
KEYS = [META + P * (b + 1) for b in range(FRAME_TILES)] + [PAST + SAMP]
CW = PAST + SAMP + META
FIRST = [CW - k for k in KEYS]


def build(nc, x_prompt, x_sample, cache_k, cache_v, state_pool, meta, norm_mix, w_in, q_norm, k_norm, pool_mix,
          pool_scale, w_pool_out, w_sb_out, w_o, norm_ffn, w_rg, b_rg, w_re, b_re, w_gate, w_up, w_down,
          y_out, nk_prompt, nv_prompt, np_prompt, nk_sample, nv_sample, np_sample, hn_dram, part_dram):
    with ExitStack() as ctx:
        def sem(name):
            return ctx.enter_context(nc.semaphore(name))

        arena = ctx.enter_context(nc.sbuf_tensor("arena", [P, 53200], F32))
        del arena
        base = 16512
        place = [base]

        def sb(name, shape, dt=F32):
            n = 4 if dt != BF16 else 2
            for s in shape[1:]:
                n *= s
            off = place[0]
            place[0] += (n + 31) // 32 * 32
            return nc.alloc_sbuf_tensor_at(name, shape, dt, offset=off)

        ring = sb("ring", [P, RING, SLOT])
        ident = sb("ident", [P, P])
        ident_b = sb("ident_b", [P, P], BF16)
        mask_p = sb("mask_p", [P, P], BF16)
        mask_s = sb("mask_s", [P, SAMP], BF16)
        tri = sb("tri", [P, P], BF16)
        ones = sb("ones", [P, P], BF16)
        zeros = sb("zeros", [P, CW])
        gain_mix = sb("gain_mix", [P, KD])
        gain_q = sb("gain_q", [P, HD])
        gain_k = sb("gain_k", [P, HD])
        scale_pool = sb("scale_pool", [P, KW])
        mix = sb("mix", [P, KW, P])
        router = sb("router", [P, KD, GROUPS + EXPERTS])
        router_bias = sb("router_bias", [P, GROUPS + EXPERTS])
        iota_e = sb("iota_e", [P, NBLK])
        iota_r = sb("iota_r", [P, SLOTS])
        token = sb("token", [P, TILES])
        stat = sb("stat", [P, 4, 8])
        stat_h = sb("stat_h", [P, 3, TILES * HEADS])
        idx = sb("idx", [P, 2, NBLK], I32)
        wgt = sb("wgt", [P, NBLK])
        in_rows = sb("in_rows", [P, 2, 1], I32)
        out_rows = sb("out_rows", [P, 2, 1], I32)
        out_wgt = sb("out_wgt", [P, 2, 1])
        ctl = sb("ctl", [1, 1 + EXTRA], I32)
        hnT = sb("hnT", [P, KD, ALL])
        u_off = place[0]
        sbT = sb("sbT", [P, KW, TOK])
        place[0] = u_off
        U = sb("U", [P, KW, UW])
        mixedT = sb("mixedT", [P, KW, TOK])
        region = place[0]
        kT = sb("kT", [P, PAIRS, ALL])
        qT = sb("qT", [P, PAIRS, ALL])
        pastkT = sb("pastkT", [P, PAIRS, PAST])
        V = sb("V", [P, TILES, W])
        work = place[0]
        pastV = sb("pastV", [P, PAST // P, W])
        after_pv = place[0]
        place[0] = work
        ptmp = sb("ptmp", [P, 2, UW])
        place[0] = region
        xn = sb("xn", [P, 2, D])
        pastk = sb("pastk", [P, PAST // P, W])
        state_rows = sb("state_rows", [POOL_STATE, W])
        place[0] = work - 4 * TILES * W
        square = sb("square", [P, D])
        place[0] = after_pv
        xr = sb("xr", [P, TILES, D])
        top_early = place[0]
        place[0] = after_pv
        krow = sb("krow", [P, TILES, W])
        qrow = sb("qrow", [P, TILES, W])
        place[0] = after_pv
        beta = sb("beta", [P, 3, CW])
        keep = sb("keep", [P, 2, CW + 8])
        AT = sb("AT", [P, 2, TILES, P])
        pool_rows = sb("pool_rows", [32 + POOL_STATE, W])
        top = max(place[0], top_early)
        place[0] = region
        mergedT = sb("mergedT", [P, KD, TOK])
        h = sb("h", [P, TILES, D])
        hn2 = sb("hn2", [P, 2, D])
        turned = place[0]
        hn2T = sb("hn2T", [P, 2, KD, P])
        gain_ffn = sb("gain_ffn", [P, D])
        behind_gates = place[0]
        square2 = sb("square2", [P, D])
        place[0] = behind_gates
        sg = sb("sg", [P, 2, TOK])
        top = max(top, place[0])
        place[0] = region
        logits = sb("logits", [P, TILES, GROUPS + EXPERTS])
        lg8 = sb("lg8", [P, TILES, 8])
        fm = sb("fm", [P, TILES, EXPERTS])
        best_g = sb("best_g", [P, TILES, 8])
        best_e = sb("best_e", [P, TILES, 8])
        at_g = sb("at_g", [P, TILES, 8], U32)
        at_e = sb("at_e", [P, TILES, 8], U32)
        eg = sb("eg", [P, TILES, GROUPS])
        small = sb("small", [P, 12, TILES])
        pick = sb("pick", [P, TOP, TILES])
        hot = sb("hot", [P, TOP, TILES, EXPERTS])
        hot_b = sb("hot_b", [P, TILES, EXPERTS], BF16)
        cnt = sb("cnt", [P, EXPERTS])
        nb = sb("nb", [P, EXPERTS])
        ebase = sb("ebase", [P, 2, EXPERTS])
        prod = sb("prod", [P, TOP, TILES, EXPERTS])
        rank = sb("rank", [P, TOP, TILES])
        past_first = sb("past_first", [P, TOP, TILES])
        base_of = sb("base_of", [P, TOP, TILES])
        blk = sb("blk", [P, TOP, TILES])
        tmp10 = sb("tmp10", [P, TOP, TILES])
        val = sb("val", [P, TOP, TILES, 3])
        etab = sb("etab", [1, EXTRA, EXPERTS])
        efin = sb("efin", [1, 1 + EXTRA])
        tabf = sb("tabf", [P, 2, NBLK])
        assert place[0] <= region + 4 * KD * TOK
        place[0] = turned
        slot_hot = sb("slot_hot", [P, TOP, TILES, SLOTS])
        blk_hot = sb("blk_hot", [P, TOP, TILES, NBLK])
        blk_val = sb("blk_val", [P, TOP, TILES, 3, NBLK])
        place[0] = u_off - 4 * KD * ALL
        xg = sb("xg", [P, 2, D])
        xT = sb("xT", [P, 2, KD, P])
        silu = sb("silu", [P, F])
        hid = sb("hid", [P, F])
        hidT = sb("hidT", [P, KF, P])
        yb = sb("yb", [P, 2, D])
        assert place[0] <= region, (place[0], region)
        assert top <= 229344, top
        ps = ctx.enter_context(nc.psum_tensor("ps", [P, 8, BANK], F32))
        psf = ps[:, :, :].rearrange("p b n -> p (b n)")

        def banks(b, lo, hi, rows=P, first=0):
            return psf[first:first + rows, b * BANK + lo:b * BANK + hi]

        slot_loaded = [sem(f"slot_loaded{i}") for i in range(RING)]
        x_loaded = [sem(f"x_loaded{t}") for t in range(TILES)]
        consts_loaded = sem("consts_loaded")
        pastk_loaded = sem("pastk_loaded")
        pastv_loaded = sem("pastv_loaded")
        h_loaded = sem("h_loaded")
        consts_made = sem("consts_made")
        step = sem("vector_step")
        stat_ready = sem("sums_initialised")
        attn_init = sem("attention_initialised")
        k_stored = sem("k_stored")
        v_stored = sem("v_stored")
        state_stored = sem("state_stored")
        pstep = sem("pool_step")
        pool_passed = sem("pool_passed")
        sq_done = sem("x_squares")
        ms_done = sem("x_mean_squares")
        root_done = sem("x_roots")
        xn_ready = sem("xn_ready")
        early_T = sem("early_transposes")
        early_out = sem("early_transposes_read")
        xT_made = sem("x_transposed")
        hnT_ready = sem("hnT_ready")
        rows_made = sem("rows_projected")
        rows_sq = sem("rows_squared")
        rows_out = sem("rows_read")
        qk_ms = sem("qk_mean_squares")
        qk_root = sem("qk_roots")
        qk_ready = sem("qk_rows_ready")
        u_made = sem("u_projected")
        u_out = sem("u_read")
        v_out = sem("v_read")
        qkT_made = sem("qk_transposed")
        qkT_out = sem("qkT_ready")
        poolT_made = sem("pool_state_transposed")
        poolT_out = sem("pool_state_read")
        pooled = sem("pooled")
        sums_done = sem("pool_sums")
        mix_made = sem("pool_mixed")
        mix_out = sem("mixedT_ready")
        z_made = sem("scores_ready")
        gates_done = sem("beta_keep_ready")
        a_ready = sem("weights_ready")
        AT_made = sem("weights_transposed")
        AT_out = sem("AT_ready")
        pv_made = sem("attention_output")
        pv_out = sem("sbT_ready")
        g_made = sem("gates_projected")
        g_out = sem("gates_sigmoid")
        p_made = sem("branch_projected")
        merged = sem("merged")
        o_made = sem("mixer_output")
        h_ready = sem("h_ready")
        hsq = sem("h_squares")
        hms = sem("h_mean_squares")
        hroot = sem("h_roots")
        hn2_ready = sem("hn2_ready")
        hn2T_made = sem("hn2_transposed")
        hn2T_out = sem("hn2T_ready")
        logits_made = sem("router_logits")
        route_a = sem("router_differences")
        route_e = sem("router_exponentials")
        hot_ready = sem("choices_ready")
        ranks_made = sem("ranks_counted")
        table_in = sem("table_inputs")
        table_made = sem("table_made")
        table_out = sem("table_ready")
        stored = sem("stored")
        hn_stored = [sem(f"hn_stored{i}") for i in range(2)]
        ins_ready = sem("block_gather_rows_copied")
        outs_ready = sem("block_scatter_rows_copied")
        gathered = [sem(f"gathered{i}") for i in range(2)]
        xg_init = sem("gather_buffers_initialised")
        eT_made = sem("block_transposed")
        eT_out = sem("block_xT_ready")
        gate_made = sem("block_gate")
        silu_done = sem("block_silu")
        up_made = sem("block_up")
        hid_done = sem("block_hidden")
        hidT_made = sem("block_hidden_transposed")
        hidT_out = sem("block_hidT_ready")
        down_made = sem("block_down")
        y_ready = sem("block_output")
        scattered = [sem(f"scattered{i}") for i in range(2)]
        extra_loaded = sem("extra_weights_loaded")
        extra_gathered = sem("extra_gathered")
        extra_scattered = sem("extra_scattered")
        all_scattered = sem("all_blocks_scattered")
        part_loaded = [sem(f"part_loaded{t}") for t in range(TILES)]
        y_done = sem("y_ready")

        def loaded(eng, i):
            eng.wait_ge(slot_loaded[i % RING], 16 * (i // RING + 1))

        def w_slot(i, cols=BANK):
            return ring[:, i % RING, :].rearrange("p (k n) -> p k n", n=cols)

        block = ctx.enter_context(nc.Block())

        @block.sync
        def _(sp):
            win = w_in[0].rearrange("(k p) n -> p k n", p=P)
            src = {"u": win[:, :, 0:W], "q": win[:, :, W:2 * W], "k": win[:, :, 2 * W:3 * W], "v": win[:, :, 3 * W:4 * W]}
            wo = w_o[0].rearrange("(k p) n -> p k n", p=P)
            for br in range(2):
                for j in range(2):
                    c = 4 * W + br * D + j * BANK
                    src["gate", br, j] = win[:, :, c:c + BANK]
                    src["wo", j] = wo[:, :, j * BANK:(j + 1) * BANK]
            src["out", 0] = w_pool_out[0].rearrange("(k p) n -> p k n", p=P)
            src["out", 1] = w_sb_out[0].rearrange("(k p) n -> p k n", p=P)

            used = {"k": (rows_made, TILES), "q": (rows_made, 2 * TILES), "u": (u_made, KW), "v": (rows_made, 3 * TILES)}
            for br in range(2):
                for j in range(2):
                    used["gate", br, j] = (g_made, KD * br + 4 * (j + 1))
                    used["wo", j] = (o_made, TILES)
                used["out", br] = (p_made, KD * (br + 1))
            used[FRONT] = (gate_made, 1)
            used[FRONT + 1] = (up_made, 1)
            for name, i in STREAM.items():
                used[i] = used[name]

            def free_slot(i):
                sp.wait_ge(*used[i - RING])

            for name, i in STREAM.items():
                if i >= RING:
                    free_slot(i)
                cols = D if name[0] == "out" else BANK
                sp.dma_start(w_slot(i, cols), src[name]).then_inc(slot_loaded[i % RING], 16)

            made = {"gate": gate_made, "up": up_made, "down": down_made}

            def expert_matrix(kind, e, slot, done):
                source = {"gate": w_gate, "up": w_up, "down": w_down}[kind][0, e].rearrange("(k p) n -> p k n", p=P)
                dst = ring[:, slot, :].rearrange("p (k n) -> p k n", n=D if kind == "down" else F)
                sp.dma_start(dst, source).then_inc(done, 16)

            def early(kind, e):
                i = expert_stream(kind, e)
                free_slot(i)
                expert_matrix(kind, e, i % RING, slot_loaded[i % RING])

            def steady(kind, e, like):
                slot = expert_stream(kind, like) % RING
                sp.wait_ge(made[kind], e - 1)
                expert_matrix(kind, e, slot, slot_loaded[slot])

            early("gate", 0)
            early("up", 0)
            for e in (1, 2):
                early("gate", e)
                early("up", e)
                early("down", e - 1)
            with sp.Fori(0, EXPERTS // 2 - 2) as it:
                for k in range(2):
                    steady("gate", it * 2 + (3 + k), 3 + k)
                    steady("up", it * 2 + (3 + k), 3 + k)
                    steady("down", it * 2 + (2 + k), 2 + k)
            steady("gate", EXPERTS - 1, EXPERTS - 1)
            steady("up", EXPERTS - 1, EXPERTS - 1)
            steady("down", EXPERTS - 2, EXPERTS - 2)
            i = expert_stream("down", EXPERTS - 1)
            sp.wait_ge(gate_made, EXPERTS - 1)
            expert_matrix("down", EXPERTS - 1, i % RING, slot_loaded[i % RING])

            sp.wait_ge(table_out, 1)
            n_extra = sp.value_load(ctl[0:1, 0:1], min_val=0, max_val=EXTRA)
            with sp.If(n_extra > 0):
                with sp.Fori(0, EXTRA) as i:
                    with sp.If(i < n_extra):
                        e = sp.value_load(ctl[0:1, bass.ds(i + 1, 1)], min_val=0, max_val=EXPERTS - 1)
                        sp.wait_ge(down_made, i + EXPERTS)
                        for slot, kind in enumerate(("gate", "up", "down")):
                            expert_matrix(kind, e, slot, extra_loaded)

            sp.wait_ge(all_scattered, 1)
            sp.wait_ge(down_made, EXPERTS)
            for t in range(TILES):
                n = TOK_ROWS[t]
                for k in range(TOP):
                    sp.dma_start(ring[0:n, t, k * D:(k + 1) * D],
                                 part_dram[k * TOK + t * P:k * TOK + t * P + n, :]).then_inc(part_loaded[t], 16)
            for t in range(TILES):
                n = TOK_ROWS[t]
                sp.wait_ge(y_done, t + 1)
                sp.dma_start(y_out[t * P:t * P + n, :], h[0:n, t, :]).then_inc(stored, 16)
            sp.wait_ge(k_stored, 16 * 6)
            sp.wait_ge(v_stored, 16 * 6)
            sp.wait_ge(state_stored, 32)
            sp.wait_ge(stored, 16 * TILES)

        @block.gpsimd
        def _(pool):
            count = [0]

            def link(ins):
                count[0] += 1
                ins.then_inc(pstep, 1)
                pool.wait_ge(pstep, count[0])

            pool.memset(ident[:, :], 0.0)
            pool.memset(ones[:, :], 1.0)
            pool.memset(mask_p[:, :], 0.0)
            pool.memset(mask_s[:, :], 0.0)
            link(pool.memset(ident_b[:, :], 0.0))
            pool.affine_select(out=ident[:, :], in_=ident[:, :], compare_op=ALU.not_equal, fill=1.0, base=0,
                               pattern=[[-1, P]], channel_multiplier=1)
            pool.affine_select(out=ident_b[:, :], in_=ident_b[:, :], compare_op=ALU.not_equal, fill=1.0, base=0,
                               pattern=[[-1, P]], channel_multiplier=1)
            link(pool.affine_select(out=mask_p[:, :], in_=mask_p[:, :], compare_op=ALU.is_gt, fill=NEG, base=0,
                                    pattern=[[-1, P]], channel_multiplier=1))
            for hh in range(2):
                m = mask_s[hh * SAMP:(hh + 1) * SAMP, :]
                link(pool.affine_select(out=m, in_=m, compare_op=ALU.is_gt, fill=NEG, base=0,
                                        pattern=[[-1, SAMP]], channel_multiplier=1))
            pool.affine_select(out=tri[:, :], in_=ones[:, :], compare_op=ALU.is_gt, fill=0.0, base=0,
                               pattern=[[1, P]], channel_multiplier=-1)
            pool.iota(iota_e[:, :], [[1, NBLK]], base=0, channel_multiplier=0,
                      allow_small_or_imprecise_dtypes=True)
            pool.iota(iota_r[:, :], [[1, SLOTS]], base=0, channel_multiplier=0,
                      allow_small_or_imprecise_dtypes=True)
            pool.iota(token[:, :], [[P, TILES]], base=1, channel_multiplier=1, allow_small_or_imprecise_dtypes=True)
            pool.memset(zeros[:, :], 0.0).then_inc(consts_made, 1)

            for g in range(KW):
                pool.wait_ge(u_out, 3 * (g + 1))
                if g == 0:
                    pool.wait_ge(poolT_out, 1)
                source = U[:, g, :]
                for s in range(g + 1):
                    d = 2 ** s
                    lo = 2 * d - 1
                    dst = ptmp[:, s % 2, :]
                    if s == 0 and g >= 1:
                        pool.wait_ge(pooled, g)
                    ins = pool.tensor_tensor(dst[:, lo:UW], source[:, lo:UW], source[:, lo - d:UW - d], ALU.add)
                    if s < g:
                        link(ins)
                    source = dst
                ins.then_inc(sums_done, 1)

            for rows, made, need, prompt, sample, done in ((krow, qk_ready, 1, nk_prompt, nk_sample, k_stored),
                                                           (V, v_out, TILES, nv_prompt, nv_sample, v_stored)):
                pool.wait_ge(made, need)
                for t in range(FRAME_TILES):
                    pool.dma_start(prompt[META + t * P:META + (t + 1) * P, :], rows[:, t, :]).then_inc(done, 16)
                pool.dma_start(prompt[0:META, :], rows[SAMP:SM, FRAME_TILES, :]).then_inc(done, 16)
                pool.dma_start(sample, rows[0:SAMP, FRAME_TILES, :]).then_inc(done, 16)
            pool.wait_ge(pooled, KW)
            pool.dma_start(pastV[:, :, :], cache_v.rearrange("(c p) n -> p c n", p=P)).then_inc(pastv_loaded, 16)
            pool.wait_ge(poolT_out, 3)
            pool.dma_start(np_prompt, pool_rows[0:POOL_STATE, :]).then_inc(state_stored, 16)
            pool.dma_start(np_sample, pool_rows[32:32 + POOL_STATE, :]).then_inc(state_stored, 16)

            pool.wait_ge(pv_out, GROUP_OF[-1] + 1)
            pool.wait_ge(v_stored, 16 * 6)
            pool.wait_ge(state_stored, 32)
            for t in range(FRAME_TILES):
                pool.dma_start(h[:, t, :], x_prompt[0, t * P:(t + 1) * P, :]).then_inc(h_loaded, 16)
            pool.dma_start(h[0:SAMP, FRAME_TILES, :], x_sample[0]).then_inc(h_loaded, 16)
            pool.dma_start(gain_ffn[:, :], norm_ffn.to_broadcast([P, D])).then_inc(h_loaded, 16)

            for t in range(TILES):
                n = TOK_ROWS[t]
                pool.wait_ge(hn2_ready, t + 1)
                pool.dma_start(hn_dram[t * P:t * P + n, :], hn2[0:n, t % 2, :]).then_inc(hn_stored[t % 2], 16)

            pool.wait_ge(o_made, TILES)
            pool.memset(xg[:, :, :], 0.0).then_inc(xg_init, 1)
            pool.wait_ge(table_out, 1)
            for i in range(2):
                pool.wait_ge(hn_stored[i], 16 * (-(-(TILES - i) // 2)))
            pool.wait_ge(xg_init, 1)

            last_in, last_out = pool.to_reg(TOK - 1), pool.to_reg(TOP * TOK - 1)

            def reached(semaphore, value):
                pool.wait_ge(semaphore, value)
                pool.sem_inc(pool_passed, 1)

            def gather(e, odd, done):
                pool.tensor_copy(in_rows[:, odd, :], idx[:, 0, bass.ds(e, 1)]).then_inc(ins_ready, 1)
                reached(ins_ready, e + 1)
                pool.indirect_dma_start(out=xg[:, odd, :], out_offset=None, in_=hn_dram,
                                        in_offset=bass.IndirectOffsetOnAxis(ap=in_rows[:, odd, :].bitcast(U32), axis=0),
                                        bounds_check=last_in, oob_is_err=False).then_inc(done, 16)

            def out_columns(e, odd):
                pool.tensor_copy(out_rows[:, odd, :], idx[:, 1, bass.ds(e, 1)])
                pool.tensor_copy(out_wgt[:, odd, :], wgt[:, bass.ds(e, 1)]).then_inc(outs_ready, 1)

            def scatter(e, odd, done):
                reached(outs_ready, e + 1)
                reached(y_ready, e + 1)
                pool.indirect_dma_start(out=part_dram, in_=yb[:, odd, :], in_offset=None,
                                        out_offset=bass.IndirectOffsetOnAxis(ap=out_rows[:, odd, :].bitcast(U32), axis=0),
                                        bounds_check=last_out, oob_is_err=False).then_inc(done, 16)

            gather(0, 0, gathered[0])
            gather(1, 1, gathered[1])

            def around(e, odd, fetch=True, first=False):
                if fetch:
                    reached(eT_made, e + 1)
                    gather(e + 2, odd, gathered[odd])
                if not first:
                    reached(scattered[odd], (e - odd) * 8)
                out_columns(e, odd)
                if not (isinstance(e, int) and e == 0):
                    scatter(e - 1, 1 - odd, scattered[1 - odd])

            around(0, 0, first=True)
            around(1, 1, first=True)
            with pool.Fori(0, EXPERTS // 2 - 2) as it:
                for odd in range(2):
                    around(it * 2 + (2 + odd), odd)
            around(EXPERTS - 2, 0, fetch=False)
            around(EXPERTS - 1, 1, fetch=False)
            scatter(EXPERTS - 1, 1, scattered[1])
            for odd in range(2):
                pool.wait_ge(scattered[odd], 16 * (EXPERTS // 2))

            n_extra = pool.value_load(ctl[0:1, 0:1], min_val=0, max_val=EXTRA)
            with pool.If(n_extra > 0):
                with pool.Fori(0, EXTRA) as i:
                    with pool.If(i < n_extra):
                        gather(i + EXPERTS, 0, extra_gathered)
                        out_columns(i + EXPERTS, 0)
                        scatter(i + EXPERTS, 0, extra_scattered)
                        reached(extra_scattered, i * 16 + 16)
            pool.sem_inc(all_scattered, 1)

        @block.scalar
        def _(act):
            for t in range(FRAME_TILES):
                act.dma_start(xr[:, t, :], x_prompt[0, t * P:(t + 1) * P, :]).then_inc(x_loaded[t], 16)
            act.dma_start(xr[0:SAMP, FRAME_TILES, :], x_sample[0]).then_inc(x_loaded[FRAME_TILES], 16)
            act.dma_start(xr[SAMP:SM, FRAME_TILES, :], meta).then_inc(x_loaded[FRAME_TILES], 16)
            act.dma_start(pastk[:, :, :], cache_k.rearrange("(c p) n -> p c n", p=P)).then_inc(pastk_loaded, 16)
            act.dma_start(state_rows[:, :], state_pool).then_inc(pastk_loaded, 16)
            with nc.allow_non_contiguous_dma(reason="gains by channel, a few KB"):
                act.dma_start(gain_mix[:, :], norm_mix.rearrange("a (k p) -> p (a k)", p=P)).then_inc(consts_loaded, 16)
                act.dma_start(scale_pool[:, :], pool_scale.rearrange("a (k p) -> p (a k)", p=P)).then_inc(consts_loaded, 16)
            act.dma_start(gain_q[:, :], q_norm.to_broadcast([P, HD])).then_inc(consts_loaded, 16)
            act.dma_start(gain_k[:, :], k_norm.to_broadcast([P, HD])).then_inc(consts_loaded, 16)
            act.dma_start(mix[:, :, :], pool_mix[0].rearrange("g c d -> c g d")).then_inc(consts_loaded, 16)
            act.dma_start(router[:, :, 0:GROUPS], w_rg[0].rearrange("(k p) n -> p k n", p=P)).then_inc(consts_loaded, 16)
            act.dma_start(router[:, :, GROUPS:], w_re[0].rearrange("(k p) n -> p k n", p=P)).then_inc(consts_loaded, 16)
            act.dma_start(router_bias[:, 0:GROUPS], b_rg.to_broadcast([P, GROUPS])).then_inc(consts_loaded, 16)
            act.dma_start(router_bias[:, GROUPS:], b_re.to_broadcast([P, EXPERTS])).then_inc(consts_loaded, 16)

            act.wait_ge(stat_ready, 2)
            for t in range(TILES):
                act.wait_ge(x_loaded[t], 32 if t == FRAME_TILES else 16)
                if t:
                    act.wait_ge(sq_done, t)
                n = TILE_ROWS[t]
                act.activation(square[0:n, :], xr[0:n, t, :], ACT.Square,
                               accum_out=stat[0:n, 0, t:t + 1]).then_inc(sq_done, 1)
            act.wait_ge(ms_done, 1)
            act.activation(stat[:, 2, 0:TILES], stat[:, 1, 0:TILES], ACT.Sqrt).then_inc(root_done, 1)
            for c in range(PAST // P):
                act.wait_ge(early_T, c + 2)
                act.activation(pastkT[:, :, c * P:(c + 1) * P],
                               ps[:, 4 + c, :].rearrange("p (j n) -> p j n", j=PAIRS), ACT.Copy).then_inc(early_out, 1)
            for n in range(2 * TILES):
                r = TILE_ROWS[n % TILES]
                act.wait_ge(rows_made, n + 1)
                if n >= 2:
                    act.wait_ge(rows_out, n - 1)
                act.activation(square[0:r, (n % 2) * W:(n % 2 + 1) * W], ps[0:r, n % 8, :],
                               ACT.Square).then_inc(rows_sq, 1)
                if n % TILES == TILES - 1:
                    i = n // TILES
                    act.wait_ge(qk_ms, i + 1)
                    act.activation(stat_h[:, 2, :], stat_h[:, 1, :], ACT.Sqrt).then_inc(qk_root, 1)
            for mt in range(KW):
                b = (2 + 2 * mt) % 8
                act.wait_ge(u_made, mt + 1)
                act.activation(U[:, mt, META:META + SEQ], banks(b, 0, SEQ), ACT.Copy).then_inc(u_out, 1)
                act.activation(U[:, mt, 0:META], banks(b + 1, SAMP, SM), ACT.Copy).then_inc(u_out, 1)
                act.activation(U[:, mt, UW - SAMP:UW], banks(b + 1, 0, SAMP), ACT.Copy).then_inc(u_out, 1)
            for t in range(TILES):
                n = TILE_ROWS[t]
                act.wait_ge(rows_made, 2 * TILES + t + 1)
                act.activation(V[0:n, t, :], ps[0:n, 2 + t, :], ACT.Copy).then_inc(v_out, 1)
            act.wait_ge(consts_loaded, 16 * 9)
            for g in range(KW):
                act.wait_ge(mix_made, g + 1)
                act.activation(mixedT[:, g, :], banks(2 * g, BANK - SAMP, 2 * BANK), ACT.Copy,
                               scale=scale_pool[:, g:g + 1]).then_inc(mix_out, 1)

            def sigmoids(n):
                pair, b, _ = UNITS[n]
                lo = BANK - META if b < FRAME_TILES else 0
                z = banks(2 * (n % 2), lo, lo + KEYS[b])
                act.wait_ge(z_made, n + 1)
                if n == 0:
                    act.wait_ge(qkT_out, 2 * TILES)
                    act.wait_ge(attn_init, 2)
                if n >= 3:
                    act.wait_ge(AT_made, n - 2)
                act.activation(beta[:, n % 3, FIRST[b]:CW], z, ACT.Sigmoid, scale=HD ** -0.5)
                if n >= 2:
                    act.wait_ge(a_ready, n - 1)
                act.activation(keep[:, n % 2, FIRST[b]:CW], z, ACT.Sigmoid, scale=-HD ** -0.5).then_inc(gates_done, 1)

            def transposed(n):
                pair, b, _ = UNITS[n]
                act.wait_ge(AT_made, n + 1)
                if n >= 2:
                    act.wait_ge(pv_made, n - 1)
                at = 4 + n % 2
                if b < FRAME_TILES:
                    act.activation(AT[:, n % 2, 0:b + 1, :], banks(at, 0, P * (b + 1)).rearrange("p (c n) -> p c n", n=P),
                                   ACT.Copy)
                    act.activation(AT[SAMP:SM, n % 2, FRAME_TILES, :], banks(6, 0, P, META, SAMP),
                                   ACT.Copy).then_inc(AT_out, 1)
                else:
                    act.activation(AT[:, n % 2, 0:FRAME_TILES, :], banks(at, 0, BANK).rearrange("p (c n) -> p c n", n=P),
                                   ACT.Copy)
                    act.activation(AT[0:SAMP, n % 2, FRAME_TILES, :], banks(6, 0, P, SAMP),
                                   ACT.Copy).then_inc(AT_out, 1)

            for n in range(len(UNITS) + 2):
                if n < len(UNITS):
                    sigmoids(n)
                if n >= 2:
                    transposed(n - 2)

            act.wait_ge(state_stored, 32)
            for m in range(2 * KD):
                act.wait_ge(g_made, m + 1)
                if m >= 2:
                    act.wait_ge(merged, m - 1)
                act.activation(sg[:, m % 2, :], banks(4 * (m % 2), BANK - SAMP, 2 * BANK),
                               ACT.Sigmoid).then_inc(g_out, 1)
            for t in range(TILES):
                n = TOK_ROWS[t]
                act.wait_ge(h_ready, t + 1)
                act.activation(square2[0:n, :], h[0:n, t, :], ACT.Square,
                               accum_out=stat[0:n, 0, t:t + 1]).then_inc(hsq, 1)
                act.wait_ge(hms, t + 1)
                act.activation(stat[0:n, 2, t:t + 1], stat[0:n, 1, t:t + 1], ACT.Sqrt).then_inc(hroot, 1)
            act.wait_ge(route_a, 1)
            act.activation(eg[:, :, :], eg[:, :, :], ACT.Exp)
            act.activation(small[:, 1, :], small[:, 0, :], ACT.Exp).then_inc(route_e, 1)

            def take_x(e, odd):
                act.wait_ge(eT_made, e + 1)
                act.activation(xT[:, odd, :, :], psf[:, 0:2 * BANK].rearrange("p (k n) -> p k n", n=P),
                               ACT.Copy).then_inc(eT_out, 1)

            def take_gate(e):
                act.wait_ge(gate_made, e + 1)
                act.activation(silu[:, :], ps[:, 2, :], ACT.Silu).then_inc(silu_done, 1)

            def take_down(e, odd):
                act.wait_ge(down_made, e + 1)
                act.wait_ge(outs_ready, e + 1)
                act.activation(yb[:, odd, :], psf[:, 5 * BANK:7 * BANK], ACT.Copy,
                               scale=out_wgt[:, odd, :]).then_inc(y_ready, 1)

            take_x(0, 0)
            take_gate(0)
            take_x(1, 1)

            def around(e, odd, last=False):
                act.wait_ge(hid_done, e)
                take_gate(e)
                if not last:
                    take_x(e + 1, 1 - odd)
                take_down(e - 1, 1 - odd)

            around(1, 1)
            around(2, 0)
            with act.Fori(0, EXPERTS // 2 - 2) as it:
                for k in range(2):
                    around(it * 2 + (3 + k), 1 - k)
            around(EXPERTS - 1, 1, last=True)
            take_down(EXPERTS - 1, 1)

            act.wait_ge(table_out, 1)
            n_extra = act.value_load(ctl[0:1, 0:1], min_val=0, max_val=EXTRA)
            with act.If(n_extra > 0):
                with act.Fori(0, EXTRA) as i:
                    with act.If(i < n_extra):
                        take_x(i + EXPERTS, 0)
                        act.wait_ge(hid_done, i + EXPERTS)
                        take_gate(i + EXPERTS)
                        take_down(i + EXPERTS, 0)

        @block.tensor
        def _(pe):
            pe.wait_ge(consts_made, 1)
            pe.wait_ge(pastk_loaded, 32)
            for g in range(KW):
                last = pe.transpose(banks(3, g * POOL_STATE, (g + 1) * POOL_STATE), state_rows[:, g * P:(g + 1) * P],
                                    ident[0:POOL_STATE, 0:POOL_STATE])
            last.then_inc(early_T, 1)
            for c in range(PAST // P):
                for j in range(PAIRS):
                    last = pe.transpose(banks(4 + c, j * P, (j + 1) * P), pastk[:, c, j * P:(j + 1) * P], ident[:, :])
                last.then_inc(early_T, 1)
            for t in range(TILES):
                n = TILE_ROWS[t]
                pe.wait_ge(xn_ready, t + 1)
                if t == 1:
                    pe.wait_ge(poolT_out, 1)
                if t >= 2:
                    pe.wait_ge(hnT_ready, t - 1)
                for k in range(KD):
                    last = pe.transpose(banks(2 * (t % 2), k * P, k * P + n), xn[0:n, t % 2, k * P:(k + 1) * P],
                                        ident[0:n, 0:n])
                last.then_inc(xT_made, 1)
            pe.wait_ge(hnT_ready, TILES)
            pe.wait_ge(early_out, PAST // P)

            def project_rows(name, unit, bank):
                i = STREAM[name]
                loaded(pe, i)
                for t in range(TILES):
                    n, c = TILE_ROWS[t], TILE_COL[t]
                    if unit + t >= 8 and name == "q":
                        pe.wait_ge(rows_out, unit + t - 7)
                    if name == "v":
                        pe.wait_ge(u_out, 3 * ((bank(t) - 2) // 2 + 1))
                    for k in range(KD):
                        last = pe.matmul(ps[0:n, bank(t), :], hnT[:, k, c:c + n], w_slot(i)[:, k, :],
                                         start=(k == 0), stop=(k == KD - 1))
                    last.then_inc(rows_made, 1)

            def columns(out_bank, i, cols, m, rhs, kchunks):
                for k in range(kchunks):
                    lhsT = w_slot(i, cols)[:, k, m * P:(m + 1) * P]
                    pe.matmul(banks(out_bank, BANK - SAMP, BANK), lhsT, rhs(k)[0], start=(k == 0), stop=(k == kchunks - 1))
                for k in range(kchunks):
                    lhsT = w_slot(i, cols)[:, k, m * P:(m + 1) * P]
                    last = pe.matmul(banks(out_bank + 1, 0, BANK), lhsT, rhs(k)[1], start=(k == 0), stop=(k == kchunks - 1))
                return last

            project_rows("k", 0, lambda t: t % 8)
            project_rows("q", TILES, lambda t: (TILES + t) % 8)
            i = STREAM["u"]
            loaded(pe, i)
            for mt in range(KW):
                b = (2 + 2 * mt) % 8
                pe.wait_ge(rows_out, min(2 * TILES, b + 2 if b >= 2 else 2 * TILES))
                for k in range(KD):
                    pe.matmul(banks(b, 0, SEQ), w_slot(i)[:, k, mt * P:(mt + 1) * P], hnT[:, k, SM:ALL],
                              start=(k == 0), stop=(k == KD - 1))
                for k in range(KD):
                    last = pe.matmul(banks(b + 1, 0, SM), w_slot(i)[:, k, mt * P:(mt + 1) * P], hnT[:, k, 0:SM],
                                     start=(k == 0), stop=(k == KD - 1))
                last.then_inc(u_made, 1)
            project_rows("v", 2 * TILES, lambda t: 2 + t)

            for i in range(2 * TILES):
                rows, t = (krow, qrow)[i // TILES], i % TILES
                n, b = TILE_ROWS[t], (7 + i) % 8
                if t == 0:
                    pe.wait_ge(qk_ready, i // TILES + 1)
                if i == 0:
                    pe.wait_ge(u_out, 3 * KW)
                if 3 <= i < 8:
                    pe.wait_ge(v_out, b - 1)
                if i >= 8:
                    pe.wait_ge(qkT_out, i - 7)
                for j in range(PAIRS):
                    last = pe.transpose(banks(b, j * P, j * P + n), rows[0:n, t, j * P:(j + 1) * P], ident[0:n, 0:n])
                last.then_inc(qkT_made, 1)
            pe.wait_ge(qkT_out, 2 * TILES)
            for grp, lo in ((0, META + SEQ - POOL_STATE), (1, UW - POOL_STATE)):
                for g in range(KW):
                    last = pe.transpose(banks(6 + grp, g * P, (g + 1) * P, POOL_STATE), U[:, g, lo:lo + POOL_STATE],
                                        ident[:, :])
            last.then_inc(poolT_made, 1)
            for g in range(KW):
                pe.wait_ge(pooled, g + 1)
                if g == 0:
                    pe.wait_ge(consts_loaded, 16 * 9)
                if g == 3:
                    pe.wait_ge(poolT_out, 3)
                pe.matmul(banks(2 * g, BANK - SAMP, BANK), mix[:, g, :], mixedT[:, g, 0:SAMP], start=True, stop=True)
                pe.matmul(banks(2 * g + 1, 0, BANK), mix[:, g, :], mixedT[:, g, SAMP:TOK], start=True,
                          stop=True).then_inc(mix_made, 1)
            pe.wait_ge(mix_out, KW)

            def scores(n):
                pair, b, hh = UNITS[n]
                z = 2 * (n % 2)
                if n >= 2:
                    pe.wait_ge(gates_done, n - 1)
                if b < FRAME_TILES:
                    rows = slice(hh * HD, (hh + 1) * HD)
                    q = qT[rows, pair, SM + b * P:SM + (b + 1) * P]
                    pe.matmul(banks(z, BANK - META, BANK), q, kT[rows, pair, SAMP:SM], start=True, stop=True)
                    pe.matmul(banks(z + 1, 0, P * (b + 1)), q, kT[rows, pair, SM:SM + P * (b + 1)], start=True,
                              stop=True)
                    pe.matmul(banks(z + 1, P * b, P * (b + 1)), ident_b[:, :], mask_p[:, :], start=False,
                              stop=True, skip_group_check=True).then_inc(z_made, 1)
                else:
                    for s in range(2):
                        rows = slice(s * HD, (s + 1) * HD)
                        q = qT[rows, pair, 0:SAMP]
                        pe.matmul(banks(z, 0, PAST, SAMP, s * SAMP), q, pastkT[rows, pair, :], start=True, stop=True,
                                  skip_group_check=True)
                        pe.matmul(banks(z + 1, 0, SAMP, SAMP, s * SAMP), q, kT[rows, pair, 0:SAMP], start=True, stop=False,
                                  skip_group_check=True)
                    pe.matmul(banks(z + 1, 0, SAMP), ident_b[:, :], mask_s[:, :], start=False, stop=True,
                              skip_group_check=True).then_inc(z_made, 1)

            def turn(n):
                pair, b, hh = UNITS[n]
                at = 4 + n % 2
                pe.wait_ge(a_ready, n + 1)
                if n >= 2:
                    pe.wait_ge(AT_out, n - 1)
                if n < 2:
                    pe.wait_ge(mix_out, KW)
                w = beta[:, n % 3, :]
                if b < FRAME_TILES:
                    lo = FIRST[b]
                    for c in range(b + 1):
                        pe.transpose(banks(at, c * P, (c + 1) * P), w[:, lo + META + c * P:lo + META + (c + 1) * P],
                                     ident[:, :])
                    if n >= 1:
                        pe.wait_ge(AT_out, n)
                    pe.transpose(banks(6, 0, P, SM), w[:, lo - SAMP:lo + META], ident[:, :]).then_inc(AT_made, 1)
                else:
                    lo = FIRST[b]
                    for c in range(PAST // P):
                        pe.transpose(banks(at, c * P, (c + 1) * P), w[:, lo + c * P:lo + (c + 1) * P], ident[:, :])
                    pe.wait_ge(AT_out, n)
                    pe.transpose(banks(6, 0, P, SAMP), w[:, lo + PAST:CW], ident[:, :]).then_inc(AT_made, 1)

            def values(n):
                pair, b, hh = UNITS[n]
                group = GROUP_OF[n]
                pe.wait_ge(AT_out, n + 1)
                if group >= 1 and hh == 0:
                    pe.wait_ge(pv_out, group)
                if b < FRAME_TILES:
                    out = banks(7, BANK - P, BANK, HD, hh * HD)
                    cols = slice((2 * pair + hh) * HD, (2 * pair + hh + 1) * HD)
                    for c in range(b + 1):
                        pe.matmul(out, V[:, c, cols], AT[:, n % 2, c, :], start=(c == 0), stop=False,
                                  skip_group_check=True)
                    pe.matmul(out, V[SAMP:SM, FRAME_TILES, cols], AT[SAMP:SM, n % 2, FRAME_TILES, :], start=False,
                              stop=True, skip_group_check=True).then_inc(pv_made, 1)
                else:
                    if pair == 0:
                        pe.wait_ge(pastv_loaded, 16)
                    for s in range(2):
                        out = banks(7, BANK - P, BANK - P + SAMP, HD, s * HD)
                        cols = slice((2 * pair + s) * HD, (2 * pair + s + 1) * HD)
                        q = slice(s * SAMP, (s + 1) * SAMP)
                        for c in range(PAST // P):
                            pe.matmul(out, pastV[:, c, cols], AT[:, n % 2, c, q], start=(c == 0), stop=False,
                                      skip_group_check=True)
                        last = pe.matmul(out, V[0:SAMP, FRAME_TILES, cols], AT[0:SAMP, n % 2, FRAME_TILES, q],
                                         start=False, stop=True, skip_group_check=True)
                    last.then_inc(pv_made, 1)

            for n in range(len(UNITS) + 3):
                if n < len(UNITS):
                    scores(n)
                if 2 <= n < len(UNITS) + 2:
                    turn(n - 2)
                if n >= 3:
                    values(n - 3)

            pe.wait_ge(pv_out, GROUP_OF[-1] + 1)
            for m in range(2 * KD):
                br, mt = m // KD, m % KD
                bank = 4 * (m % 2)
                if m >= 2:
                    pe.wait_ge(merged, m - 1)
                gi, wi = STREAM["gate", br, mt // 4], STREAM["out", br]
                if mt % 4 == 0:
                    loaded(pe, gi)
                if mt == 0:
                    loaded(pe, wi)
                columns(bank, gi, BANK, mt % 4, lambda k: (hnT[:, k, 0:SAMP], hnT[:, k, SM:ALL]), KD).then_inc(g_made, 1)
                src = (mixedT, sbT)[br]
                columns(bank + 2, wi, D, mt, lambda k: (src[:, k, 0:SAMP], src[:, k, SAMP:TOK]), KW).then_inc(p_made, 1)

            def turn_tile(t):
                n = TOK_ROWS[t]
                pe.wait_ge(hn2_ready, t + 1)
                if t >= 1:
                    pe.wait_ge(hn2T_out, t)
                for k in range(KD):
                    last = pe.transpose(banks(4, k * P, k * P + n), hn2[0:n, t % 2, k * P:(k + 1) * P], ident[0:n, 0:n])
                last.then_inc(hn2T_made, 1)

            def route_tile(t):
                n = TOK_ROWS[t]
                pe.wait_ge(hn2T_out, t + 1)
                width = GROUPS + EXPERTS
                for k in range(KD):
                    last = pe.matmul(banks(6, t * width, (t + 1) * width, n), hn2T[:, t % 2, k, 0:n], router[:, k, :],
                                     start=(k == 0), stop=(k == KD - 1), skip_group_check=True)
                last.then_inc(logits_made, 1)

            pe.wait_ge(merged, 2 * KD)
            for j in range(2):
                loaded(pe, STREAM["wo", j])
            for t in range(TILES):
                n, c = TOK_ROWS[t], TOK_COL[t]
                if t >= 2:
                    pe.wait_ge(h_ready, t - 1)
                for j in range(2):
                    for k in range(KD):
                        last = pe.matmul(banks(2 * (t % 2) + j, 0, BANK, n), mergedT[:, k, c:c + n],
                                         w_slot(STREAM["wo", j])[:, k, :], start=(k == 0), stop=(k == KD - 1))
                    if j == 0 and t >= 1:
                        turn_tile(t - 1)
                last.then_inc(o_made, 1)
                if t >= 1:
                    route_tile(t - 1)
            turn_tile(TILES - 1)
            route_tile(TILES - 1)

            pe.wait_ge(hot_ready, 1)
            for t in range(TILES):
                n = TOK_ROWS[t]
                out = banks(0, t * EXPERTS, (t + 1) * EXPERTS, n)
                for s in range(t):
                    pe.matmul(out, ones[:, 0:n], hot_b[:, s, :], start=(s == 0), stop=False, skip_group_check=True)
                pe.matmul(out, tri[0:n, 0:n], hot_b[0:n, t, :], start=(t == 0), stop=True, skip_group_check=True)
            for t in range(TILES):
                n = TOK_ROWS[t]
                last = pe.matmul(banks(1, 0, EXPERTS), ones[0:n, :], hot_b[0:n, t, :], start=(t == 0), stop=(t == TILES - 1))
            last.then_inc(ranks_made, 1)
            pe.wait_ge(table_in, 1)
            for k in range(TOP):
                for t in range(TILES):
                    n = TOK_ROWS[t]
                    last = pe.matmul(banks(2, 0, 3 * NBLK), slot_hot[0:n, k, t, :],
                                     blk_val[0:n, k, t, :, :].rearrange("p v b -> p (v b)"),
                                     start=(k + t == 0), stop=(k == TOP - 1 and t == TILES - 1))
            last.then_inc(table_made, 1)

            def turn_x(e, odd, want=None):
                if want is None:
                    pe.wait_ge(gathered[odd], (e - odd) * 8 + 16)
                    if not (isinstance(e, int) and e == 0):
                        pe.wait_ge(eT_out, e)
                for k in range(KD):
                    last = pe.transpose(banks(0, k * P, (k + 1) * P), xg[:, odd, k * P:(k + 1) * P], ident[:, :])
                last.then_inc(eT_made, 1)

            def wide(e, odd, kind, bank, slot, index, done):
                if index is not None:
                    pe.wait_ge(slot_loaded[slot], index)
                w = ring[:, slot, :].rearrange("p (k n) -> p k n", n=F)
                for k in range(KD):
                    last = pe.matmul(ps[:, bank, :], xT[:, odd, k, :], w[:, k, :], start=(k == 0), stop=(k == KD - 1))
                last.then_inc(done, 1)

            def turn_hidden(e):
                pe.wait_ge(hid_done, e + 1)
                for k in range(KF):
                    last = pe.transpose(banks(4, k * P, (k + 1) * P), hid[:, k * P:(k + 1) * P], ident[:, :])
                last.then_inc(hidT_made, 1)

            def down(e, slot, index, first=False):
                if index is not None:
                    pe.wait_ge(slot_loaded[slot], index)
                pe.wait_ge(hidT_out, e + 1)
                if not first:
                    pe.wait_ge(y_ready, e)
                w = ring[:, slot, :].rearrange("p (k n) -> p k n", n=D)
                for j in range(2):
                    for k in range(KF):
                        last = pe.matmul(ps[:, 5 + j, :], hidT[:, k, :], w[:, k, j * BANK:(j + 1) * BANK],
                                         start=(k == 0), stop=(k == KF - 1))
                last.then_inc(down_made, 1)

            def turns_of(kind, e, like):
                i = expert_stream(kind, like)
                base = (i // RING + 1) * 16
                return i % RING, (e - like) * 8 + base

            def around(e, odd, like, first=False, last=False):
                slot, need = turns_of("gate", e, like)
                pe.wait_ge(eT_out, e + 1)
                pe.wait_ge(silu_done, e)
                wide(e, odd, "gate", 2, slot, need, gate_made)
                turn_hidden(e - 1)
                slot, need = turns_of("up", e, like)
                wide(e, odd, "up", 3, slot, need, up_made)
                if not last:
                    turn_x(e + 1, 1 - odd)
                slot, need = turns_of("down", e - 1, like - 1)
                down(e - 1, slot, need, first)

            pe.wait_ge(table_out, 1)
            turn_x(0, 0)
            pe.wait_ge(eT_out, 1)
            slot, need = turns_of("gate", 0, 0)
            wide(0, 0, "gate", 2, slot, need, gate_made)
            slot, need = turns_of("up", 0, 0)
            wide(0, 0, "up", 3, slot, need, up_made)
            turn_x(1, 1)
            around(1, 1, 1, first=True)
            around(2, 0, 2)
            with pe.Fori(0, EXPERTS // 2 - 2) as it:
                for k in range(2):
                    around(it * 2 + (3 + k), 1 - k, 3 + k)
            around(EXPERTS - 1, 1, EXPERTS - 1, last=True)
            turn_hidden(EXPERTS - 1)
            slot, need = turns_of("down", EXPERTS - 1, EXPERTS - 1)
            down(EXPERTS - 1, slot, need)

            pe.wait_ge(table_out, 1)
            n_extra = pe.value_load(ctl[0:1, 0:1], min_val=0, max_val=EXTRA)
            with pe.If(n_extra > 0):
                with pe.Fori(0, EXTRA) as i:
                    with pe.If(i < n_extra):
                        pe.wait_ge(extra_gathered, i * 16 + 16)
                        pe.wait_ge(eT_out, i + EXPERTS)
                        turn_x(i + EXPERTS, 0, want=False)
                        pe.wait_ge(extra_loaded, i * 48 + 48)
                        pe.wait_ge(eT_out, i + EXPERTS + 1)
                        wide(i, 0, "gate", 2, 0, None, gate_made)
                        wide(i, 0, "up", 3, 1, None, up_made)
                        turn_hidden(i + EXPERTS)
                        down(i + EXPERTS, 2, None)

        @block.vector
        def _(dve):
            count = [0]

            def link(ins):
                count[0] += 1
                ins.then_inc(step, 1)
                dve.wait_ge(step, count[0])

            dve.memset(stat[:, :, :], 1.0).then_inc(stat_ready, 1)
            dve.memset(stat_h[:, :, :], 1.0).then_inc(stat_ready, 1)
            dve.wait_ge(sq_done, TILES)
            dve.tensor_scalar(stat[:, 1, 0:TILES], stat[:, 0, 0:TILES], 1.0 / D, EPS, ALU.mult, ALU.add).then_inc(ms_done, 1)
            dve.wait_ge(root_done, 1)
            link(dve.reciprocal(stat[:, 3, 0:TILES], stat[:, 2, 0:TILES]))
            dve.wait_ge(early_T, 1)
            dve.tensor_copy(U[:, :, META + SEQ:META + SEQ + POOL_STATE],
                            banks(3, 0, KW * POOL_STATE).rearrange("p (g n) -> p g n", g=KW)).then_inc(poolT_out, 1)

            def norm_x(t):
                n = TILE_ROWS[t]
                if t >= 2:
                    dve.wait_ge(xT_made, t - 1)
                dve.tensor_scalar(xn[0:n, t % 2, :], xr[0:n, t, :], stat[0:n, 3, t:t + 1], None, ALU.mult).then_inc(xn_ready, 1)

            def take_hn(t):
                n, c = TILE_ROWS[t], TILE_COL[t]
                dve.wait_ge(xT_made, t + 1)
                src = banks(2 * (t % 2), 0, 2 * BANK).rearrange("p (k n) -> p k n", k=KD)[:, :, 0:n]
                dve.tensor_tensor(hnT[:, :, c:c + n], src,
                                  gain_mix[:, :].unsqueeze(2).to_broadcast([P, KD, n]), ALU.mult).then_inc(hnT_ready, 1)

            dve.wait_ge(consts_loaded, 16 * 9)
            norm_x(0)
            for t in range(TILES):
                if t + 1 < TILES:
                    norm_x(t + 1)
                take_hn(t)

            dve.wait_ge(stat_ready, 2)
            for i, (rows, gain) in enumerate(((krow, gain_k), (qrow, gain_q))):
                for t in range(TILES):
                    u = i * TILES + t
                    n = TILE_ROWS[t]
                    dve.wait_ge(rows_made, u + 1)
                    if u == 0:
                        dve.wait_ge(xT_made, TILES)
                    dve.wait_ge(rows_sq, u + 1)
                    dve.tensor_tensor(rows[0:n, t, :].rearrange("p (h d) -> p h d", h=HEADS),
                                      ps[0:n, u % 8, :].rearrange("p (h d) -> p h d", h=HEADS),
                                      gain[0:n, :].unsqueeze(1).to_broadcast([n, HEADS, HD]), ALU.mult)
                    dve.tensor_reduce(stat_h[0:n, 0, t * HEADS:(t + 1) * HEADS],
                                      square[0:n, (u % 2) * W:(u % 2 + 1) * W].rearrange("p (h d) -> p h d", h=HEADS),
                                      AX.X, ALU.add).then_inc(rows_out, 1)
                dve.wait_ge(rows_out, (i + 1) * TILES)
                dve.tensor_scalar(stat_h[:, 1, :], stat_h[:, 0, :], 1.0 / HD, EPS, ALU.mult, ALU.add).then_inc(qk_ms, 1)
                dve.wait_ge(qk_root, i + 1)
                link(dve.reciprocal(stat_h[:, 0, :], stat_h[:, 2, :]))
                for t in range(TILES):
                    n = TILE_ROWS[t]
                    r = rows[0:n, t, :].rearrange("p (h d) -> p h d", h=HEADS)
                    inv = stat_h[0:n, 0, t * HEADS:(t + 1) * HEADS].unsqueeze(2).to_broadcast([n, HEADS, HD])
                    last = dve.tensor_tensor(r, r, inv, ALU.mult)
                last.then_inc(qk_ready, 1)
                dve.wait_ge(qk_ready, i + 1)

            for g in range(KW):
                dve.wait_ge(sums_done, g + 1)
                sums = ptmp[:, g % 2, :]
                for dst, lo, n in ((SAMP, META, SEQ), (0, UW - SAMP, SAMP)):
                    last = dve.scalar_tensor_tensor(out=mixedT[:, g, dst:dst + n], in0=sums[:, lo:lo + n],
                                                    scalar=1.0 / 2 ** (g + 1), in1=U[:, g, lo:lo + n],
                                                    op0=ALU.mult, op1=ALU.subtract)
                last.then_inc(pooled, 1)
            for i in range(2 * TILES):
                dst, t = (kT, qT)[i // TILES], i % TILES
                n, c = TILE_ROWS[t], TILE_COL[t]
                dve.wait_ge(qkT_made, i + 1)
                dve.tensor_copy(dst[:, :, c:c + n],
                                ps[:, (7 + i) % 8, :].rearrange("p (j n) -> p j n", j=PAIRS)[:, :, 0:n]).then_inc(qkT_out, 1)
            dve.wait_ge(poolT_made, 1)
            for i in range(2):
                dve.tensor_copy(pool_rows[32 * i:32 * i + POOL_STATE, :], ps[0:POOL_STATE, 6 + i, :]).then_inc(poolT_out, 1)

            dve.wait_ge(qkT_out, 2 * TILES)
            dve.wait_ge(qkT_made, 2 * TILES)
            dve.wait_ge(k_stored, 16 * 6)
            dve.memset(beta[:, :, :], 0.0).then_inc(attn_init, 1)
            dve.memset(keep[:, :, CW:CW + 1], 1.0).then_inc(attn_init, 1)
            dve.wait_ge(attn_init, 2)
            dve.wait_ge(consts_made, 1)

            def weigh(n):
                pair, b, hh = UNITS[n]
                lo = FIRST[b]
                kp = keep[:, n % 2, :]
                dve.wait_ge(gates_done, n + 1)
                count[0] += 1
                dve.tensor_tensor_scan(kp[:, lo:CW][:, ::-1], kp[:, lo:CW][:, ::-1], zeros[:, lo:CW], 1.0, ALU.mult,
                                       ALU.add).then_inc(step, 1)
                dve.wait_ge(step, count[0])
                dve.tensor_tensor(beta[:, n % 3, lo:CW], beta[:, n % 3, lo:CW], kp[:, lo + 1:CW + 1],
                                  ALU.mult).then_inc(a_ready, 1)

            def take_output(n):
                pair, b, hh = UNITS[n]
                if b < FRAME_TILES and hh == 0:
                    return
                group = GROUP_OF[n]
                dve.wait_ge(pv_made, n + 1)
                if group == 0:
                    dve.wait_ge(poolT_made, 1)
                if b < FRAME_TILES:
                    dve.tensor_copy(sbT[:, pair, SAMP + b * P:SAMP + (b + 1) * P],
                                    banks(7, BANK - P, BANK)).then_inc(pv_out, 1)
                else:
                    dve.tensor_copy(sbT[:, pair, 0:SAMP], banks(7, BANK - P, BANK - P + SAMP)).then_inc(pv_out, 1)

            for n in range(len(UNITS) + 4):
                if n >= 4:
                    take_output(n - 4)
                if n < len(UNITS):
                    weigh(n)

            for m in range(2 * KD):
                br, mt = m // KD, m % KD
                proj = banks(4 * (m % 2) + 2, BANK - SAMP, 2 * BANK)
                dve.wait_ge(g_out, m + 1)
                dve.wait_ge(p_made, m + 1)
                if br == 0:
                    dve.tensor_tensor(mergedT[:, mt, :], sg[:, m % 2, :], proj, ALU.mult).then_inc(merged, 1)
                else:
                    link(dve.tensor_tensor(sg[:, m % 2, :], sg[:, m % 2, :], proj, ALU.mult))
                    dve.tensor_tensor(mergedT[:, mt, :], mergedT[:, mt, :], sg[:, m % 2, :], ALU.add).then_inc(merged, 1)

            dve.wait_ge(h_loaded, 16 * (TILES + 1))
            for t in range(TILES):
                n = TOK_ROWS[t]
                dve.wait_ge(o_made, t + 1)
                dve.tensor_tensor(h[0:n, t, :], h[0:n, t, :], banks(2 * (t % 2), 0, 2 * BANK, n), ALU.add).then_inc(h_ready, 1)
                dve.wait_ge(hsq, t + 1)
                dve.tensor_scalar(stat[0:n, 1, t:t + 1], stat[0:n, 0, t:t + 1], 1.0 / D, EPS, ALU.mult,
                                  ALU.add).then_inc(hms, 1)
                dve.wait_ge(hroot, t + 1)
                link(dve.reciprocal(stat[0:n, 3, t:t + 1], stat[0:n, 2, t:t + 1]))
                if t >= 2:
                    dve.wait_ge(hn_stored[t % 2], 16 * (t // 2))
                dve.scalar_tensor_tensor(out=hn2[0:n, t % 2, :], in0=h[0:n, t, :], scalar=stat[0:n, 3, t:t + 1],
                                         in1=gain_ffn[0:n, :], op0=ALU.mult, op1=ALU.mult).then_inc(hn2_ready, 1)
                dve.wait_ge(hn2T_made, t + 1)
                if t >= 2:
                    dve.wait_ge(logits_made, t - 1)
                dve.tensor_copy(hn2T[:, t % 2, :, 0:n],
                                banks(4, 0, 2 * BANK).rearrange("p (k n) -> p k n", k=KD)[:, :, 0:n]).then_inc(hn2T_out, 1)

            width = GROUPS + EXPERTS
            dve.wait_ge(logits_made, TILES)
            dve.memset(logits[:, :, :], 0.0)
            link(dve.memset(lg8[:, :, :], NEG))
            for t in range(TILES):
                n = TOK_ROWS[t]
                last = dve.tensor_tensor(logits[0:n, t, :], banks(6, t * width, (t + 1) * width, n), router_bias[0:n, :],
                                         ALU.add)
            link(last)
            link(dve.tensor_copy(lg8[:, :, 0:GROUPS], logits[:, :, 0:GROUPS]))
            for t in range(TILES):
                last = dve.max(best_g[:, t, :], lg8[:, t, :])
            link(last)
            for t in range(TILES):
                last = dve.max_index(at_g[:, t, :], best_g[:, t, :], lg8[:, t, :])
            link(last)
            wide3 = [P, TILES, EXPERTS]

            def over_e(ap):
                return ap.unsqueeze(2).to_broadcast(wide3)

            group_of = small[:, 2, :]
            link(dve.tensor_copy(group_of, at_g[:, :, 0:1].rearrange("p t a -> p (t a)")))
            link(dve.tensor_scalar(small[:, 3, :], group_of, float(PER_GROUP), None, ALU.mult))
            link(dve.tensor_tensor(fm[:, :, :], iota_e[:, 0:EXPERTS].unsqueeze(1).to_broadcast(wide3), over_e(small[:, 3, :]),
                                   ALU.subtract))
            link(dve.tensor_scalar(prod[:, 0, :, :], fm[:, :, :], 0.0, None, ALU.is_ge))
            link(dve.tensor_scalar(prod[:, 1, :, :], fm[:, :, :], float(PER_GROUP), None, ALU.is_lt))
            link(dve.tensor_tensor(prod[:, 0, :, :], prod[:, 0, :, :], prod[:, 1, :, :], ALU.mult))
            link(dve.tensor_tensor(fm[:, :, :], logits[:, :, GROUPS:], prod[:, 0, :, :], ALU.mult))
            link(dve.tensor_scalar(prod[:, 1, :, :], prod[:, 0, :, :], -NEG, NEG, ALU.mult, ALU.add))
            link(dve.tensor_tensor(fm[:, :, :], fm[:, :, :], prod[:, 1, :, :], ALU.add))
            for t in range(TILES):
                last = dve.max(best_e[:, t, :], fm[:, t, :])
            link(last)
            for t in range(TILES):
                last = dve.max_index(at_e[:, t, :], best_e[:, t, :], fm[:, t, :])
            link(last)
            dve.tensor_tensor(eg[:, :, :], logits[:, :, 0:GROUPS],
                              best_g[:, :, 0:1].to_broadcast([P, TILES, GROUPS]), ALU.subtract)
            dve.tensor_tensor(small[:, 0, :], best_e[:, :, 1:2].rearrange("p t a -> p (t a)"),
                              best_e[:, :, 0:1].rearrange("p t a -> p (t a)"), ALU.subtract).then_inc(route_a, 1)
            for k in range(TOP):
                last = dve.tensor_copy(pick[:, k, :], at_e[:, :, k:k + 1].rearrange("p t a -> p (t a)"))
            link(last)
            for k in range(TOP):
                last = dve.tensor_tensor(hot[:, k, :, :], iota_e[:, 0:EXPERTS].unsqueeze(1).to_broadcast(wide3),
                                         over_e(pick[:, k, :]), ALU.is_equal)
            link(last)
            dve.tensor_tensor(hot_b[:, :, :], hot[:, 0, :, :], hot[:, 1, :, :], ALU.add).then_inc(hot_ready, 1)
            dve.wait_ge(route_e, 1)
            link(dve.tensor_reduce(small[:, 4, :], eg[:, :, :], AX.X, ALU.add))
            link(dve.tensor_scalar(small[:, 5, :], small[:, 1, :], 1.0, None, ALU.add))
            link(dve.tensor_tensor(small[:, 6, :], small[:, 4, :], small[:, 5, :], ALU.mult))
            link(dve.reciprocal(small[:, 7, :], small[:, 6, :]))
            link(dve.tensor_copy(val[:, 0, :, 2], small[:, 7, :]))
            link(dve.tensor_tensor(val[:, 1, :, 2], small[:, 7, :], small[:, 1, :], ALU.mult))
            link(dve.tensor_copy(val[:, 0, :, 0], token[:, :]))
            dve.tensor_copy(val[:, 1, :, 0], token[:, :])
            dve.tensor_copy(val[:, 0, :, 1], token[:, :])
            link(dve.tensor_scalar(val[:, 1, :, 1], token[:, :], float(TOK), None, ALU.add))

            dve.wait_ge(ranks_made, 1)
            link(dve.tensor_copy(cnt[:, :], banks(1, 0, EXPERTS)))
            link(dve.tensor_scalar(nb[:, :], cnt[:, :], float(SLOTS), None, ALU.is_gt))
            for j in range(2, J):
                link(dve.tensor_scalar(ebase[:, 0, :], cnt[:, :], float(SLOTS * j), None, ALU.is_gt))
                link(dve.tensor_tensor(nb[:, :], nb[:, :], ebase[:, 0, :], ALU.add))
            link(dve.tensor_tensor_scan(ebase[:, 1, :], zeros[:, 0:EXPERTS], nb[:, :], 0.0, ALU.add, ALU.add))
            link(dve.tensor_tensor(ebase[:, 0, :], ebase[:, 1, :], nb[:, :], ALU.subtract))
            for k in range(TOP):
                for t in range(TILES):
                    n = TOK_ROWS[t]
                    dve.tensor_tensor(prod[0:n, k, t, :], hot[0:n, k, t, :], banks(0, t * EXPERTS, (t + 1) * EXPERTS, n),
                                      ALU.mult)
            dve.memset(prod[SAMP:P, :, FRAME_TILES, :], 0.0).then_inc(step, 1)
            count[0] += 1
            dve.wait_ge(step, count[0])
            link(dve.tensor_reduce(rank[:, :, :], prod[:, :, :, :], AX.X, ALU.add))
            link(dve.tensor_tensor(prod[:, :, :, :].rearrange("p k t e -> p (k t) e"),
                                   hot[:, :, :, :].rearrange("p k t e -> p (k t) e"),
                                   ebase[:, 0, :].unsqueeze(1).to_broadcast([P, TOP * TILES, EXPERTS]), ALU.mult))
            link(dve.tensor_reduce(base_of[:, :, :], prod[:, :, :, :], AX.X, ALU.add))
            link(dve.tensor_scalar(past_first[:, :, :], rank[:, :, :], float(SLOTS), None, ALU.is_ge))
            link(dve.tensor_copy(blk[:, :, :], past_first[:, :, :]))
            for j in range(2, J):
                link(dve.tensor_scalar(tmp10[:, :, :], rank[:, :, :], float(SLOTS * j), None, ALU.is_ge))
                link(dve.tensor_tensor(blk[:, :, :], blk[:, :, :], tmp10[:, :, :], ALU.add))
            link(dve.scalar_tensor_tensor(out=rank[:, :, :], in0=blk[:, :, :], scalar=-float(SLOTS), in1=rank[:, :, :],
                                          op0=ALU.mult, op1=ALU.add))
            link(dve.tensor_tensor(blk[:, :, :], blk[:, :, :], base_of[:, :, :], ALU.add))
            link(dve.tensor_scalar(blk[:, :, :], blk[:, :, :], float(EXPERTS - 1), None, ALU.add))
            link(dve.tensor_tensor(blk[:, :, :], blk[:, :, :], pick[:, :, :], ALU.subtract))
            link(dve.tensor_tensor(blk[:, :, :], blk[:, :, :], past_first[:, :, :], ALU.mult))
            link(dve.tensor_tensor(blk[:, :, :], blk[:, :, :], pick[:, :, :], ALU.add))
            kt = TOP * TILES
            dve.tensor_tensor(slot_hot[:, :, :, :].rearrange("p k t s -> p (k t) s"),
                              iota_r[:, :].unsqueeze(1).to_broadcast([P, kt, SLOTS]),
                              rank[:, :, :].rearrange("p k t -> p (k t)").unsqueeze(2).to_broadcast([P, kt, SLOTS]),
                              ALU.is_equal)
            link(dve.tensor_tensor(blk_hot[:, :, :, :].rearrange("p k t s -> p (k t) s"),
                                   iota_e[:, :].unsqueeze(1).to_broadcast([P, kt, NBLK]),
                                   blk[:, :, :].rearrange("p k t -> p (k t)").unsqueeze(2).to_broadcast([P, kt, NBLK]),
                                   ALU.is_equal))
            for v in range(3):
                last = dve.tensor_tensor(blk_val[:, :, :, v, :].rearrange("p k t s -> p (k t) s"),
                                         blk_hot[:, :, :, :].rearrange("p k t s -> p (k t) s"),
                                         val[:, :, :, v].rearrange("p k t -> p (k t)").unsqueeze(2).to_broadcast([P, kt, NBLK]),
                                         ALU.mult)
            last.then_inc(table_in, 1)
            for i in range(EXTRA):
                last = dve.tensor_scalar(etab[:, i, :], ebase[0:1, 1, :], float(i), None, ALU.is_le)
            link(last)
            link(dve.tensor_reduce(efin[:, 1:1 + EXTRA], etab[:, :, :], AX.X, ALU.add))
            link(dve.tensor_scalar(efin[:, 1:1 + EXTRA], efin[:, 1:1 + EXTRA], float(EXPERTS - 1), None, ALU.min))
            link(dve.tensor_copy(efin[:, 0:1], ebase[0:1, 1, EXPERTS - 1:EXPERTS]))
            link(dve.tensor_copy(ctl[:, :], efin[:, :]))
            dve.wait_ge(table_made, 1)
            table = banks(2, 0, 3 * NBLK).rearrange("p (v b) -> p v b", v=3)
            link(dve.tensor_scalar(tabf[:, :, :], table[:, 0:2, :], 0.0, EMPTY, ALU.is_equal, ALU.mult))
            link(dve.tensor_tensor(tabf[:, :, :], tabf[:, :, :], table[:, 0:2, :], ALU.add))
            link(dve.tensor_scalar(tabf[:, :, :], tabf[:, :, :], -1.0, None, ALU.add))
            link(dve.tensor_copy(wgt[:, :], table[:, 2, :]))
            dve.tensor_copy(idx[:, :, :], tabf[:, :, :]).then_inc(table_out, 1)

            def take_up(e):
                dve.wait_ge(silu_done, e + 1)
                dve.wait_ge(up_made, e + 1)
                dve.tensor_tensor(hid[:, :], silu[:, :], ps[:, 3, :], ALU.mult).then_inc(hid_done, 1)

            def take_hidden(e):
                dve.wait_ge(hidT_made, e + 1)
                dve.tensor_copy(hidT[:, :, :], ps[:, 4, :].rearrange("p (k n) -> p k n", k=KF)).then_inc(hidT_out, 1)

            take_up(0)
            with dve.Fori(1, EXPERTS) as e:
                take_hidden(e - 1)
                take_up(e)
            take_hidden(EXPERTS - 1)

            n_extra = dve.value_load(ctl[0:1, 0:1], min_val=0, max_val=EXTRA)
            with dve.If(n_extra > 0):
                with dve.Fori(0, EXTRA) as i:
                    with dve.If(i < n_extra):
                        take_up(i + EXPERTS)
                        take_hidden(i + EXPERTS)

            for t in range(TILES):
                n = TOK_ROWS[t]
                dve.wait_ge(part_loaded[t], 32)
                link(dve.tensor_tensor(h[0:n, t, :], h[0:n, t, :], ring[0:n, t, 0:D], ALU.add))
                dve.tensor_tensor(h[0:n, t, :], h[0:n, t, :], ring[0:n, t, D:2 * D], ALU.add).then_inc(y_done, 1)


_INS = ["x_prompt", "x_sample", "cache_sb_k", "cache_sb_v", "state_pool", "meta_tokens", "norm_mix", "w_in", "q_norm",
        "k_norm", "pool_mix", "pool_scale", "w_pool_out", "w_sb_out", "w_o", "norm_ffn", "w_router_group",
        "b_router_group", "w_router_expert", "b_router_expert", "w_gate", "w_up", "w_down"]


def kernel(**inputs):
    import numpy as _np
    import concourse.bacc as _bacc
    from concourse import mybir as _mybir
    from concourse.bass_utils import run_bass_kernel_spmd as _run

    nc = _bacc.Bacc("TRN2", target_bir_lowering=False, num_devices=1)
    arrays, args = {}, []
    for name in _INS:
        a = _np.ascontiguousarray(inputs[name])
        if name in ("cache_sb_k", "cache_sb_v"):
            a = a.reshape(PAST, W)
        if name == "state_pool":
            a = a.reshape(POOL_STATE, W)
        arrays[f"in_{name}_dram"] = a
        args.append(nc.dram_tensor(f"in_{name}_dram", a.shape, _mybir.dt.from_np(a.dtype), kind="ExternalInput").ap())
    outs = {"y": (TOK, D), "nk_prompt": (META + SEQ, W), "nv_prompt": (META + SEQ, W), "np_prompt": (POOL_STATE, W),
            "nk_sample": (SAMP, W), "nv_sample": (SAMP, W), "np_sample": (POOL_STATE, W)}
    for name, shape in outs.items():
        args.append(nc.dram_tensor(f"out_{name}_dram", shape, F32, kind="ExternalOutput").ap())
    args.append(nc.dram_tensor("hn_dram", (TOK, D), F32, kind="Internal").ap())
    args.append(nc.dram_tensor("part_dram", (TOP * TOK, D), F32, kind="Internal").ap())
    build(nc, *args)
    r = _run(nc, [arrays], core_ids=[0])
    got = {name: r.results[0][f"out_{name}_dram"] for name in outs}
    heads = (HEADS, HD)
    return (got["y"][:SEQ].reshape(1, SEQ, D), got["y"][SEQ:].reshape(1, SAMP, D),
            got["nk_prompt"].reshape(1, 1, META + SEQ, *heads), got["nv_prompt"].reshape(1, 1, META + SEQ, *heads),
            got["np_prompt"].reshape(1, 1, POOL_STATE, W),
            got["nk_sample"].reshape(1, 1, SAMP, *heads), got["nv_sample"].reshape(1, 1, SAMP, *heads),
            got["np_sample"].reshape(1, 1, POOL_STATE, W))
```

```python
from contextlib import ExitStack

import concourse.bass as bass
from concourse import mybir

F32 = mybir.dt.float32
BF16 = mybir.dt.bfloat16
I32 = mybir.dt.int32
U32 = mybir.dt.uint32
ALU = mybir.AluOpType
ACT = mybir.ActivationFunctionType
AX = mybir.AxisListType

P = 128
BANK = 512
D = 1024
KD = D // P
SEQ, META, SAMP, PAST = 512, 16, 64, 512
HEADS, HD = 8, 64
PAIRS = HEADS // 2
W = HEADS * HD
KW = W // P
POOL_STATE = 15
EPS = 1e-6
FRAME_TILES = SEQ // P
TILES = FRAME_TILES + 1
SM = SAMP + META
TOK = SEQ + SAMP
ALL = TOK + META
HALF_D = D // 2
UW = META + SEQ + POOL_STATE + SAMP
GROUPS, PER_GROUP, EXPERTS = 4, 8, 32
TOP = 2
F = 512
KF = F // P
SLOTS = 64
J = -(-TOK // SLOTS)
EXTRA = TOK * TOP // SLOTS
NBLK = EXPERTS + EXTRA
RING = 6
SLOT = KD * BANK
NEG = -1.0e30
EMPTY = 1.0e6

TILE_ROWS = [P] * FRAME_TILES + [SM]
TOK_ROWS = [P] * FRAME_TILES + [SAMP]


def stream_index():
    order = ["k", "q", "u", "v", ("gate", 0, 0), ("gate", 0, 1), ("out", 0), ("gate", 1, 0), ("gate", 1, 1),
             ("out", 1), ("wo", 0), ("wo", 1)]
    return {name: n for n, name in enumerate(order)}


STREAM = stream_index()
FRONT = len(STREAM)


KINDS = ("gate", "up", "down")


def expert_slot(kind, odd):
    return 3 * odd + KINDS.index(kind)


def expert_count(e, odd):
    return (e - odd) * 8 + 16 * (FRONT // RING + 1)


def attention_units():
    units = []
    for pair in range(PAIRS):
        for block in range(FRAME_TILES):
            units += [(pair, block, 0), (pair, block, 1)]
        units.append((pair, FRAME_TILES, 0))
    return units


UNITS = attention_units()
GROUP_OF = []
for _n, (_pair, _block, _hh) in enumerate(UNITS):
    GROUP_OF.append(GROUP_OF[-1] + (_hh == 0) if _n else 0)
KEYS = [META + P * (b + 1) for b in range(FRAME_TILES)] + [PAST + SAMP]
CW = PAST + SAMP + META
FIRST = [CW - k for k in KEYS]


def build(nc, x_prompt, x_sample, cache_k, cache_v, state_pool, meta, norm_mix, w_in, q_norm, k_norm, pool_mix,
          pool_scale, w_pool_out, w_sb_out, w_o, norm_ffn, w_rg, b_rg, w_re, b_re, w_gate, w_up, w_down,
          y_out, nk_prompt, nv_prompt, np_prompt, nk_sample, nv_sample, np_sample, hn_dram, part_dram):
    with ExitStack() as ctx:
        def sem(name):
            return ctx.enter_context(nc.semaphore(name))

        arena = ctx.enter_context(nc.sbuf_tensor("arena", [P, 53200], F32))
        del arena
        base = 16512
        place = [base]

        def sb(name, shape, dt=F32):
            n = 4 if dt != BF16 else 2
            for s in shape[1:]:
                n *= s
            off = place[0]
            place[0] += (n + 31) // 32 * 32
            return nc.alloc_sbuf_tensor_at(name, shape, dt, offset=off)

        ring = sb("ring", [P, RING, SLOT])
        ident = sb("ident", [P, P])
        ident_b = sb("ident_b", [P, P], BF16)
        mask_p = sb("mask_p", [P, P], BF16)
        mask_s = sb("mask_s", [P, SAMP], BF16)
        tri = sb("tri", [P, P], BF16)
        ones = sb("ones", [P, P], BF16)
        zeros = sb("zeros", [P, CW])
        gain_mix = sb("gain_mix", [P, KD])
        gain_q = sb("gain_q", [P, HD])
        gain_k = sb("gain_k", [P, HD])
        scale_pool = sb("scale_pool", [P, KW])
        mix = sb("mix", [P, KW, P])
        router = sb("router", [P, KD, GROUPS + EXPERTS])
        router_bias = sb("router_bias", [P, GROUPS + EXPERTS])
        iota_e = sb("iota_e", [P, NBLK])
        iota_r = sb("iota_r", [P, 2 * SLOTS])
        token = sb("token", [P, TILES])
        half = sb("half", [P, 1])
        stat = sb("stat", [P, 4, 8])
        stat_h = sb("stat_h", [P, 3, TILES * HEADS])
        idx = sb("idx", [P, 2, NBLK], I32)
        wgt = sb("wgt", [P, NBLK])
        in_rows = sb("in_rows", [P, 2, 1], I32)
        out_rows = sb("out_rows", [P, 2, 1], I32)
        out_wgt = sb("out_wgt", [P, 2, 1])
        ctl = sb("ctl", [1, 1 + EXTRA], I32)
        hnT = sb("hnT", [P, KD, ALL])
        u_off = place[0]
        sbT = sb("sbT", [P, KW, TOK])
        place[0] = u_off
        U = sb("U", [P, KW, UW])
        mixedT = sb("mixedT", [P, KW, TOK])
        region = place[0]
        kT = sb("kT", [P, PAIRS, ALL])
        qT = sb("qT", [P, PAIRS, ALL])
        pastkT = sb("pastkT", [P, PAIRS, PAST])
        V = sb("V", [P, TILES, W])
        work = place[0]
        pastV = sb("pastV", [P, PAST // P, W])
        after_pv = place[0]
        place[0] = work
        ptmp = sb("ptmp", [P, 2, UW])
        place[0] = region
        xn = sb("xn", [P, 2, D])
        pastk = sb("pastk", [P, PAST // P, W])
        state_rows = sb("state_rows", [POOL_STATE, W])
        place[0] = work - 4 * TILES * W
        square = sb("square", [P, D])
        place[0] = after_pv
        xr = sb("xr", [P, TILES, D])
        top_early = place[0]
        place[0] = after_pv
        krow = sb("krow", [P, TILES, W])
        qrow = sb("qrow", [P, TILES, W])
        place[0] = after_pv
        beta = sb("beta", [P, 3, CW])
        keep = sb("keep", [P, 2, CW + 8])
        AT = sb("AT", [P, 2, TILES, P])
        pool_rows = sb("pool_rows", [32 + POOL_STATE, W])
        top = max(place[0], top_early)
        place[0] = region
        mergedT = sb("mergedT", [P, KD, TOK])
        h = sb("h", [P, TILES, D])
        hn2 = sb("hn2", [P, 2, D])
        turned = place[0]
        hn2T = sb("hn2T", [P, 2, KD, P])
        gain_ffn = sb("gain_ffn", [P, D])
        behind_gates = place[0]
        square2 = sb("square2", [P, D])
        place[0] = behind_gates
        sg = sb("sg", [P, 2, TOK])
        top = max(top, place[0])
        place[0] = region
        logits = sb("logits", [P, TILES, GROUPS + EXPERTS])
        lg8 = sb("lg8", [P, TILES, 8])
        fm = sb("fm", [P, TILES, EXPERTS])
        best_g = sb("best_g", [P, TILES, 8])
        best_e = sb("best_e", [P, TILES, 8])
        at_g = sb("at_g", [P, TILES, 8], U32)
        at_e = sb("at_e", [P, TILES, 8], U32)
        eg = sb("eg", [P, TILES, GROUPS])
        small = sb("small", [P, 12, TILES])
        pick = sb("pick", [P, TOP, TILES])
        hot = sb("hot", [P, TOP, TILES, EXPERTS])
        hot_b = sb("hot_b", [P, TILES, EXPERTS], BF16)
        cnt = sb("cnt", [P, EXPERTS])
        nb = sb("nb", [P, EXPERTS])
        ebase = sb("ebase", [P, 2, EXPERTS])
        prod = sb("prod", [P, TOP, TILES, EXPERTS])
        rank = sb("rank", [P, TOP, TILES])
        past_first = sb("past_first", [P, TOP, TILES])
        base_of = sb("base_of", [P, TOP, TILES])
        blk = sb("blk", [P, TOP, TILES])
        tmp10 = sb("tmp10", [P, TOP, TILES])
        val = sb("val", [P, TOP, TILES, 3])
        etab = sb("etab", [1, EXTRA, EXPERTS])
        efin = sb("efin", [1, 1 + EXTRA])
        tabf = sb("tabf", [P, 2, NBLK])
        assert place[0] <= region + 4 * KD * TOK
        place[0] = turned
        slot_hot = sb("slot_hot", [P, TOP, TILES, 2 * SLOTS])
        blk_hot = sb("blk_hot", [P, TOP, TILES, NBLK])
        blk_val = sb("blk_val", [P, TOP, TILES, 3, NBLK])
        place[0] = u_off - 4 * KD * ALL
        xg = sb("xg", [P, 2, HALF_D])
        xT = sb("xT", [P, 2, KD // 2, 2, SLOTS])
        silu = sb("silu", [P, F // 2])
        hid = sb("hid", [P, F // 2])
        hidT = sb("hidT", [P, KF // 2, 2, SLOTS])
        yb = sb("yb", [P, 2, HALF_D])
        assert place[0] <= region, (place[0], region)
        assert top <= 229344, top
        ps = ctx.enter_context(nc.psum_tensor("ps", [P, 8, BANK], F32))
        psf = ps[:, :, :].rearrange("p b n -> p (b n)")

        def banks(b, lo, hi, rows=P, first=0):
            return psf[first:first + rows, b * BANK + lo:b * BANK + hi]

        slot_loaded = [sem(f"slot_loaded{i}") for i in range(RING)]
        x_loaded = [sem(f"x_loaded{t}") for t in range(TILES)]
        consts_loaded = sem("consts_loaded")
        pastk_loaded = sem("pastk_loaded")
        pastv_loaded = sem("pastv_loaded")
        h_loaded = sem("h_loaded")
        consts_made = sem("consts_made")
        step = sem("vector_step")
        stat_ready = sem("sums_initialised")
        attn_init = sem("attention_initialised")
        k_stored = sem("k_stored")
        v_stored = sem("v_stored")
        state_stored = sem("state_stored")
        pstep = sem("pool_step")
        pool_passed = sem("pool_passed")
        sq_done = sem("x_squares")
        ms_done = sem("x_mean_squares")
        root_done = sem("x_roots")
        xn_ready = sem("xn_ready")
        early_T = sem("early_transposes")
        early_out = sem("early_transposes_read")
        xT_made = sem("x_transposed")
        hnT_ready = sem("hnT_ready")
        rows_made = sem("rows_projected")
        rows_sq = sem("rows_squared")
        rows_out = sem("rows_read")
        qk_ms = sem("qk_mean_squares")
        qk_root = sem("qk_roots")
        qk_ready = sem("qk_rows_ready")
        u_made = sem("u_projected")
        u_out = sem("u_read")
        v_out = sem("v_read")
        qkT_made = sem("qk_transposed")
        qkT_out = sem("qkT_ready")
        poolT_made = sem("pool_state_transposed")
        poolT_out = sem("pool_state_read")
        pooled = sem("pooled")
        sums_done = sem("pool_sums")
        mix_made = sem("pool_mixed")
        mix_out = sem("mixedT_ready")
        z_made = sem("scores_ready")
        gates_done = sem("beta_keep_ready")
        a_ready = sem("weights_ready")
        AT_made = sem("weights_transposed")
        AT_out = sem("AT_ready")
        pv_made = sem("attention_output")
        pv_out = sem("sbT_ready")
        g_made = sem("gates_projected")
        g_out = sem("gates_sigmoid")
        p_made = sem("branch_projected")
        merged = sem("merged")
        o_made = sem("mixer_output")
        h_ready = sem("h_ready")
        hsq = sem("h_squares")
        hms = sem("h_mean_squares")
        hroot = sem("h_roots")
        hn2_ready = sem("hn2_ready")
        hn2T_made = sem("hn2_transposed")
        hn2T_out = sem("hn2T_ready")
        logits_made = sem("router_logits")
        route_a = sem("router_differences")
        route_e = sem("router_exponentials")
        hot_ready = sem("choices_ready")
        ranks_made = sem("ranks_counted")
        table_in = sem("table_inputs")
        table_made = sem("table_made")
        table_out = sem("table_ready")
        stored = sem("stored")
        hn_stored = [sem(f"hn_stored{i}") for i in range(2)]
        ins_ready = sem("block_gather_rows_copied")
        outs_ready = sem("block_scatter_rows_copied")
        gathered = [sem(f"gathered{i}") for i in range(2)]
        xg_init = sem("gather_buffers_initialised")
        eT_made = sem("block_transposed")
        eT_out = sem("block_xT_ready")
        wide_made = sem("block_gate_up")
        silu_done = sem("block_silu")
        hid_done = sem("block_hidden")
        hidT_made = sem("block_hidden_transposed")
        hidT_out = sem("block_hidT_ready")
        down_made = sem("block_down")
        y_ready = sem("block_output")
        scattered = [sem(f"scattered{i}") for i in range(2)]
        extra_loaded = sem("extra_weights_loaded")
        extra_gathered = sem("extra_gathered")
        extra_scattered = sem("extra_scattered")
        all_scattered = sem("all_blocks_scattered")
        part_loaded = [sem(f"part_loaded{t}") for t in range(TILES)]
        y_done = sem("y_ready")

        def loaded(eng, i):
            eng.wait_ge(slot_loaded[i % RING], 16 * (i // RING + 1))

        def w_slot(i, cols=BANK):
            return ring[:, i % RING, :].rearrange("p (k n) -> p k n", n=cols)

        block = ctx.enter_context(nc.Block())

        @block.sync
        def _(sp):
            win = w_in[0].rearrange("(k p) n -> p k n", p=P)
            src = {"u": win[:, :, 0:W], "q": win[:, :, W:2 * W], "k": win[:, :, 2 * W:3 * W], "v": win[:, :, 3 * W:4 * W]}
            wo = w_o[0].rearrange("(k p) n -> p k n", p=P)
            for br in range(2):
                for j in range(2):
                    c = 4 * W + br * D + j * BANK
                    src["gate", br, j] = win[:, :, c:c + BANK]
                    src["wo", j] = wo[:, :, j * BANK:(j + 1) * BANK]
            src["out", 0] = w_pool_out[0].rearrange("(k p) n -> p k n", p=P)
            src["out", 1] = w_sb_out[0].rearrange("(k p) n -> p k n", p=P)

            used = {"k": (rows_made, TILES), "q": (rows_made, 2 * TILES), "u": (u_made, KW), "v": (rows_made, 3 * TILES)}
            for br in range(2):
                for j in range(2):
                    used["gate", br, j] = (g_made, KD * br + 4 * (j + 1))
                    used["wo", j] = (o_made, TILES)
                used["out", br] = (p_made, KD * (br + 1))
            for name, i in STREAM.items():
                used[i] = used[name]

            def free_slot(i):
                sp.wait_ge(*used[i - RING])

            for name, i in STREAM.items():
                if i >= RING:
                    free_slot(i)
                cols = D if name[0] == "out" else BANK
                sp.dma_start(w_slot(i, cols), src[name]).then_inc(slot_loaded[i % RING], 16)

            def expert_matrix(kind, e, slot, done):
                source = {"gate": w_gate, "up": w_up, "down": w_down}[kind][0, e].rearrange("(k p) n -> p k n", p=P)
                dst = ring[:, slot, :].rearrange("p (k n) -> p k n", n=D if kind == "down" else F)
                sp.dma_start(dst, source).then_inc(done, 16)

            for e in range(2):
                for kind in KINDS:
                    slot = expert_slot(kind, e)
                    free_slot(FRONT + slot)
                    expert_matrix(kind, e, slot, slot_loaded[slot])
            with sp.Fori(1, EXPERTS // 2) as it:
                for odd in range(2):
                    e = it * 2 + odd
                    for kind in KINDS:
                        slot = expert_slot(kind, odd)
                        sp.wait_ge(down_made if kind == "down" else wide_made, e - 1)
                        expert_matrix(kind, e, slot, slot_loaded[slot])

            sp.wait_ge(table_out, 1)
            n_extra = sp.value_load(ctl[0:1, 0:1], min_val=0, max_val=EXTRA)
            with sp.If(n_extra > 0):
                with sp.Fori(0, EXTRA) as i:
                    with sp.If(i < n_extra):
                        e = sp.value_load(ctl[0:1, bass.ds(i + 1, 1)], min_val=0, max_val=EXPERTS - 1)
                        sp.wait_ge(down_made, i + EXPERTS)
                        for slot, kind in enumerate(KINDS):
                            expert_matrix(kind, e, slot, extra_loaded)

            parts = part_dram.rearrange("(k t h) n -> k t (h n)", k=TOP, h=2)
            sp.wait_ge(all_scattered, 1)
            sp.wait_ge(down_made, EXPERTS)
            for t in range(TILES):
                n = TOK_ROWS[t]
                for k in range(TOP):
                    sp.dma_start(ring[0:n, t, k * D:(k + 1) * D],
                                 parts[k, t * P:t * P + n, :]).then_inc(part_loaded[t], 16)
            for t in range(TILES):
                n = TOK_ROWS[t]
                sp.wait_ge(y_done, t + 1)
                sp.dma_start(y_out[t * P:t * P + n, :], h[0:n, t, :]).then_inc(stored, 16)
            sp.wait_ge(k_stored, 16 * 6)
            sp.wait_ge(v_stored, 16 * 6)
            sp.wait_ge(state_stored, 32)
            sp.wait_ge(stored, 16 * TILES)

        @block.gpsimd
        def _(pool):
            count = [0]

            def link(ins):
                count[0] += 1
                ins.then_inc(pstep, 1)
                pool.wait_ge(pstep, count[0])

            pool.memset(ident[:, :], 0.0)
            pool.memset(ones[:, :], 1.0)
            pool.memset(mask_p[:, :], 0.0)
            pool.memset(mask_s[:, :], 0.0)
            link(pool.memset(ident_b[:, :], 0.0))
            pool.affine_select(out=ident[:, :], in_=ident[:, :], compare_op=ALU.not_equal, fill=1.0, base=0,
                               pattern=[[-1, P]], channel_multiplier=1)
            pool.affine_select(out=ident_b[:, :], in_=ident_b[:, :], compare_op=ALU.not_equal, fill=1.0, base=0,
                               pattern=[[-1, P]], channel_multiplier=1)
            link(pool.affine_select(out=mask_p[:, :], in_=mask_p[:, :], compare_op=ALU.is_gt, fill=NEG, base=0,
                                    pattern=[[-1, P]], channel_multiplier=1))
            for hh in range(2):
                m = mask_s[hh * SAMP:(hh + 1) * SAMP, :]
                link(pool.affine_select(out=m, in_=m, compare_op=ALU.is_gt, fill=NEG, base=0,
                                        pattern=[[-1, SAMP]], channel_multiplier=1))
            pool.affine_select(out=tri[:, :], in_=ones[:, :], compare_op=ALU.is_gt, fill=0.0, base=0,
                               pattern=[[1, P]], channel_multiplier=-1)
            pool.iota(iota_e[:, :], [[1, NBLK]], base=0, channel_multiplier=0,
                      allow_small_or_imprecise_dtypes=True)
            pool.iota(iota_r[:, :], [[0, 2], [1, SLOTS]], base=0, channel_multiplier=0,
                      allow_small_or_imprecise_dtypes=True)
            pool.iota(token[:, :], [[P, TILES]], base=1, channel_multiplier=1, allow_small_or_imprecise_dtypes=True)
            link(pool.memset(half[0:SLOTS, :], -2.0))
            link(pool.memset(half[SLOTS:P, :], -1.0))
            pool.memset(zeros[:, :], 0.0).then_inc(consts_made, 1)

            for g in range(KW):
                pool.wait_ge(u_out, 3 * (g + 1))
                if g == 0:
                    pool.wait_ge(poolT_out, 1)
                source = U[:, g, :]
                for s in range(g + 1):
                    d = 2 ** s
                    lo = 2 * d - 1
                    dst = ptmp[:, s % 2, :]
                    if s == 0 and g >= 1:
                        pool.wait_ge(pooled, g)
                    ins = pool.tensor_tensor(dst[:, lo:UW], source[:, lo:UW], source[:, lo - d:UW - d], ALU.add)
                    if s < g:
                        link(ins)
                    source = dst
                ins.then_inc(sums_done, 1)

            for rows, made, need, prompt, sample, done in ((krow, qk_ready, 1, nk_prompt, nk_sample, k_stored),
                                                           (V, v_out, TILES, nv_prompt, nv_sample, v_stored)):
                pool.wait_ge(made, need)
                for t in range(FRAME_TILES):
                    pool.dma_start(prompt[META + t * P:META + (t + 1) * P, :], rows[:, t, :]).then_inc(done, 16)
                pool.dma_start(prompt[0:META, :], rows[SAMP:SM, FRAME_TILES, :]).then_inc(done, 16)
                pool.dma_start(sample, rows[0:SAMP, FRAME_TILES, :]).then_inc(done, 16)
            pool.wait_ge(pooled, KW)
            pool.dma_start(pastV[:, :, :], cache_v.rearrange("(c p) n -> p c n", p=P)).then_inc(pastv_loaded, 16)
            pool.wait_ge(poolT_out, 3)
            pool.dma_start(np_prompt, pool_rows[0:POOL_STATE, :]).then_inc(state_stored, 16)
            pool.dma_start(np_sample, pool_rows[32:32 + POOL_STATE, :]).then_inc(state_stored, 16)

            pool.wait_ge(pv_out, GROUP_OF[-1] + 1)
            pool.wait_ge(v_stored, 16 * 6)
            pool.wait_ge(state_stored, 32)
            for t in range(FRAME_TILES):
                pool.dma_start(h[:, t, :], x_prompt[0, t * P:(t + 1) * P, :]).then_inc(h_loaded, 16)
            pool.dma_start(h[0:SAMP, FRAME_TILES, :], x_sample[0]).then_inc(h_loaded, 16)
            pool.dma_start(gain_ffn[:, :], norm_ffn.to_broadcast([P, D])).then_inc(h_loaded, 16)

            hn_rows = hn_dram.rearrange("(t h) n -> t (h n)", h=2)
            for t in range(TILES):
                n = TOK_ROWS[t]
                pool.wait_ge(hn2_ready, t + 1)
                pool.dma_start(hn_rows[t * P:t * P + n, :], hn2[0:n, t % 2, :]).then_inc(hn_stored[t % 2], 16)

            pool.wait_ge(o_made, TILES)
            pool.memset(xg[:, :, :], 0.0).then_inc(xg_init, 1)
            pool.wait_ge(table_out, 1)
            for i in range(2):
                pool.wait_ge(hn_stored[i], 16 * (-(-(TILES - i) // 2)))
            pool.wait_ge(xg_init, 1)

            last_in, last_out = pool.to_reg(2 * TOK - 1), pool.to_reg(2 * TOP * TOK - 1)

            def reached(semaphore, value):
                pool.wait_ge(semaphore, value)
                pool.sem_inc(pool_passed, 1)

            def gather(e, odd, done):
                pool.tensor_copy(in_rows[:, odd, :], idx[:, 0, bass.ds(e, 1)]).then_inc(ins_ready, 1)
                reached(ins_ready, e + 1)
                pool.indirect_dma_start(out=xg[:, odd, :], out_offset=None, in_=hn_dram,
                                        in_offset=bass.IndirectOffsetOnAxis(ap=in_rows[:, odd, :].bitcast(U32), axis=0),
                                        bounds_check=last_in, oob_is_err=False).then_inc(done, 16)

            def out_columns(e, odd):
                pool.tensor_copy(out_rows[:, odd, :], idx[:, 1, bass.ds(e, 1)])
                pool.tensor_copy(out_wgt[:, odd, :], wgt[:, bass.ds(e, 1)]).then_inc(outs_ready, 1)

            def scatter(e, odd, done):
                reached(outs_ready, e + 1)
                reached(y_ready, e + 1)
                pool.indirect_dma_start(out=part_dram, in_=yb[:, odd, :], in_offset=None,
                                        out_offset=bass.IndirectOffsetOnAxis(ap=out_rows[:, odd, :].bitcast(U32), axis=0),
                                        bounds_check=last_out, oob_is_err=False).then_inc(done, 16)

            gather(0, 0, gathered[0])
            gather(1, 1, gathered[1])

            def around(e, odd, fetch=True, first=False):
                if fetch:
                    reached(eT_made, e + 1)
                    gather(e + 2, odd, gathered[odd])
                if not first:
                    reached(scattered[odd], (e - odd) * 8)
                out_columns(e, odd)
                if not (isinstance(e, int) and e == 0):
                    scatter(e - 1, 1 - odd, scattered[1 - odd])

            around(0, 0, first=True)
            around(1, 1, first=True)
            with pool.Fori(0, EXPERTS // 2 - 2) as it:
                for odd in range(2):
                    around(it * 2 + (2 + odd), odd)
            around(EXPERTS - 2, 0, fetch=False)
            around(EXPERTS - 1, 1, fetch=False)
            scatter(EXPERTS - 1, 1, scattered[1])
            for odd in range(2):
                pool.wait_ge(scattered[odd], 16 * (EXPERTS // 2))

            n_extra = pool.value_load(ctl[0:1, 0:1], min_val=0, max_val=EXTRA)
            with pool.If(n_extra > 0):
                with pool.Fori(0, EXTRA) as i:
                    with pool.If(i < n_extra):
                        gather(i + EXPERTS, 0, extra_gathered)
                        out_columns(i + EXPERTS, 0)
                        scatter(i + EXPERTS, 0, extra_scattered)
                        reached(extra_scattered, i * 16 + 16)
            pool.sem_inc(all_scattered, 1)

        @block.scalar
        def _(act):
            for t in range(FRAME_TILES):
                act.dma_start(xr[:, t, :], x_prompt[0, t * P:(t + 1) * P, :]).then_inc(x_loaded[t], 16)
            act.dma_start(xr[0:SAMP, FRAME_TILES, :], x_sample[0]).then_inc(x_loaded[FRAME_TILES], 16)
            act.dma_start(xr[SAMP:SM, FRAME_TILES, :], meta).then_inc(x_loaded[FRAME_TILES], 16)
            act.dma_start(pastk[:, :, :], cache_k.rearrange("(c p) n -> p c n", p=P)).then_inc(pastk_loaded, 16)
            act.dma_start(state_rows[:, :], state_pool).then_inc(pastk_loaded, 16)
            with nc.allow_non_contiguous_dma(reason="gains by channel, a few KB"):
                act.dma_start(gain_mix[:, :], norm_mix.rearrange("a (k p) -> p (a k)", p=P)).then_inc(consts_loaded, 16)
                act.dma_start(scale_pool[:, :], pool_scale.rearrange("a (k p) -> p (a k)", p=P)).then_inc(consts_loaded, 16)
            act.dma_start(gain_q[:, :], q_norm.to_broadcast([P, HD])).then_inc(consts_loaded, 16)
            act.dma_start(gain_k[:, :], k_norm.to_broadcast([P, HD])).then_inc(consts_loaded, 16)
            act.dma_start(mix[:, :, :], pool_mix[0].rearrange("g c d -> c g d")).then_inc(consts_loaded, 16)
            act.dma_start(router[:, :, 0:GROUPS], w_rg[0].rearrange("(k p) n -> p k n", p=P)).then_inc(consts_loaded, 16)
            act.dma_start(router[:, :, GROUPS:], w_re[0].rearrange("(k p) n -> p k n", p=P)).then_inc(consts_loaded, 16)
            act.dma_start(router_bias[:, 0:GROUPS], b_rg.to_broadcast([P, GROUPS])).then_inc(consts_loaded, 16)
            act.dma_start(router_bias[:, GROUPS:], b_re.to_broadcast([P, EXPERTS])).then_inc(consts_loaded, 16)

            act.wait_ge(stat_ready, 2)
            for t in range(TILES):
                act.wait_ge(x_loaded[t], 32 if t == FRAME_TILES else 16)
                if t:
                    act.wait_ge(sq_done, t)
                n = TILE_ROWS[t]
                act.activation(square[0:n, :], xr[0:n, t, :], ACT.Square,
                               accum_out=stat[0:n, 0, t:t + 1]).then_inc(sq_done, 1)
            act.wait_ge(ms_done, 1)
            act.activation(stat[:, 2, 0:TILES], stat[:, 1, 0:TILES], ACT.Sqrt).then_inc(root_done, 1)
            for c in range(PAST // P):
                act.wait_ge(early_T, c + 2)
                act.activation(pastkT[:, :, c * P:(c + 1) * P],
                               ps[:, 4 + c, :].rearrange("p (j n) -> p j n", j=PAIRS), ACT.Copy).then_inc(early_out, 1)
            for n in range(2 * TILES):
                r = TILE_ROWS[n % TILES]
                act.wait_ge(rows_made, n + 1)
                if n >= 2:
                    act.wait_ge(rows_out, n - 1)
                act.activation(square[0:r, (n % 2) * W:(n % 2 + 1) * W], ps[0:r, n % 8, :],
                               ACT.Square).then_inc(rows_sq, 1)
                if n % TILES == TILES - 1:
                    i = n // TILES
                    act.wait_ge(qk_ms, i + 1)
                    act.activation(stat_h[:, 2, :], stat_h[:, 1, :], ACT.Sqrt).then_inc(qk_root, 1)
            for mt in range(KW):
                b = (2 + 2 * mt) % 8
                act.wait_ge(u_made, mt + 1)
                first = BANK - ALL // 2
                act.activation(U[:, mt, META:META + SEQ], banks(b, first, first + SEQ), ACT.Copy).then_inc(u_out, 1)
                act.activation(U[:, mt, 0:META], banks(b, first + TOK, first + ALL), ACT.Copy).then_inc(u_out, 1)
                act.activation(U[:, mt, UW - SAMP:UW], banks(b, first + SEQ, first + TOK), ACT.Copy).then_inc(u_out, 1)
            for t in range(TILES):
                n = TILE_ROWS[t]
                act.wait_ge(rows_made, 2 * TILES + t + 1)
                act.activation(V[0:n, t, :], ps[0:n, 2 + t, :], ACT.Copy).then_inc(v_out, 1)
            act.wait_ge(consts_loaded, 16 * 9)
            for g in range(KW):
                act.wait_ge(mix_made, g + 1)
                act.activation(mixedT[:, g, :], banks(2 * g, BANK - TOK // 2, BANK + TOK // 2), ACT.Copy,
                               scale=scale_pool[:, g:g + 1]).then_inc(mix_out, 1)

            def sigmoids(n):
                pair, b, _ = UNITS[n]
                lo = BANK - META if b < FRAME_TILES else 0
                z = banks(2 * (n % 2), lo, lo + KEYS[b])
                act.wait_ge(z_made, n + 1)
                if n == 0:
                    act.wait_ge(qkT_out, 2 * TILES)
                    act.wait_ge(attn_init, 2)
                if n >= 3:
                    act.wait_ge(AT_made, n - 2)
                act.activation(beta[:, n % 3, FIRST[b]:CW], z, ACT.Sigmoid, scale=HD ** -0.5)
                if n >= 2:
                    act.wait_ge(a_ready, n - 1)
                act.activation(keep[:, n % 2, FIRST[b]:CW], z, ACT.Sigmoid, scale=-HD ** -0.5).then_inc(gates_done, 1)

            def transposed(n):
                pair, b, _ = UNITS[n]
                act.wait_ge(AT_made, n + 1)
                if n >= 2:
                    act.wait_ge(pv_made, n - 1)
                at = 4 + n % 2
                if b < FRAME_TILES:
                    act.activation(AT[:, n % 2, 0:b + 1, :], banks(at, 0, P * (b + 1)).rearrange("p (c n) -> p c n", n=P),
                                   ACT.Copy)
                    act.activation(AT[SAMP:SM, n % 2, FRAME_TILES, :], banks(6, 0, P, META, SAMP),
                                   ACT.Copy).then_inc(AT_out, 1)
                else:
                    act.activation(AT[:, n % 2, 0:FRAME_TILES, :], banks(at, 0, BANK).rearrange("p (c n) -> p c n", n=P),
                                   ACT.Copy)
                    act.activation(AT[0:SAMP, n % 2, FRAME_TILES, :], banks(6, 0, P, SAMP),
                                   ACT.Copy).then_inc(AT_out, 1)

            for n in range(len(UNITS) + 2):
                if n < len(UNITS):
                    sigmoids(n)
                if n >= 2:
                    transposed(n - 2)

            act.wait_ge(state_stored, 32)
            for m in range(2 * KD):
                act.wait_ge(g_made, m + 1)
                if m >= 2:
                    act.wait_ge(merged, m - 1)
                act.activation(sg[:, m % 2, :], banks(4 * (m % 2), BANK - TOK // 2, BANK + TOK // 2),
                               ACT.Sigmoid).then_inc(g_out, 1)
            for t in range(TILES):
                n = TOK_ROWS[t]
                act.wait_ge(h_ready, t + 1)
                act.activation(square2[0:n, :], h[0:n, t, :], ACT.Square,
                               accum_out=stat[0:n, 0, t:t + 1]).then_inc(hsq, 1)
                act.wait_ge(hms, t + 1)
                act.activation(stat[0:n, 2, t:t + 1], stat[0:n, 1, t:t + 1], ACT.Sqrt).then_inc(hroot, 1)
            act.wait_ge(route_a, 1)
            act.activation(eg[:, :, :], eg[:, :, :], ACT.Exp)
            act.activation(small[:, 1, :], small[:, 0, :], ACT.Exp).then_inc(route_e, 1)

            def take_x(e, odd):
                act.wait_ge(eT_made, e + 1)
                act.activation(xT[:, odd, :, :, :], ps[:, odd, :].rearrange("p (c h n) -> p c h n", c=KD // 2, h=2),
                               ACT.Copy).then_inc(eT_out, 1)

            def take_gate(e, odd):
                act.wait_ge(wide_made, e + 1)
                act.activation(silu[:, :], ps[:, 2 + odd, 0:F // 2], ACT.Silu).then_inc(silu_done, 1)

            def take_down(e, odd):
                act.wait_ge(down_made, e + 1)
                act.wait_ge(outs_ready, e + 1)
                act.activation(yb[:, odd, :], ps[:, 6 + odd, :], ACT.Copy, scale=out_wgt[:, odd, :]).then_inc(y_ready, 1)

            take_x(0, 0)
            with act.Fori(0, EXPERTS // 2 - 1) as it:
                for odd in range(2):
                    take_gate(it * 2 + odd, odd)
                    take_x(it * 2 + (1 + odd), 1 - odd)
                    take_down(it * 2 + odd, odd)
            take_gate(EXPERTS - 2, 0)
            take_x(EXPERTS - 1, 1)
            take_down(EXPERTS - 2, 0)
            take_gate(EXPERTS - 1, 1)
            take_down(EXPERTS - 1, 1)

            act.wait_ge(table_out, 1)
            n_extra = act.value_load(ctl[0:1, 0:1], min_val=0, max_val=EXTRA)
            with act.If(n_extra > 0):
                with act.Fori(0, EXTRA) as i:
                    with act.If(i < n_extra):
                        take_x(i + EXPERTS, 0)
                        take_gate(i + EXPERTS, 0)
                        take_down(i + EXPERTS, 0)

        @block.tensor
        def _(pe):
            pe.wait_ge(consts_made, 1)
            pe.wait_ge(pastk_loaded, 32)
            for g in range(KW):
                last = pe.transpose(banks(3, g * POOL_STATE, (g + 1) * POOL_STATE), state_rows[:, g * P:(g + 1) * P],
                                    ident[0:POOL_STATE, 0:POOL_STATE])
            last.then_inc(early_T, 1)
            for c in range(PAST // P):
                for j in range(PAIRS):
                    last = pe.transpose(banks(4 + c, j * P, (j + 1) * P), pastk[:, c, j * P:(j + 1) * P], ident[:, :])
                last.then_inc(early_T, 1)
            for t in range(TILES):
                n = TILE_ROWS[t]
                pe.wait_ge(xn_ready, t + 1)
                if t == 1:
                    pe.wait_ge(poolT_out, 1)
                if t >= 2:
                    pe.wait_ge(hnT_ready, t - 1)
                for k in range(KD):
                    last = pe.transpose(banks(2 * (t % 2), k * P, k * P + n), xn[0:n, t % 2, k * P:(k + 1) * P],
                                        ident[0:n, 0:n])
                last.then_inc(xT_made, 1)
            pe.wait_ge(hnT_ready, TILES)
            pe.wait_ge(early_out, PAST // P)

            def project_rows(name, unit, bank):
                i = STREAM[name]
                loaded(pe, i)
                for t in range(TILES):
                    n, c = TILE_ROWS[t], P * t
                    if unit + t >= 8 and name == "q":
                        pe.wait_ge(rows_out, unit + t - 7)
                    if name == "v":
                        pe.wait_ge(u_out, 3 * ((bank(t) - 2) // 2 + 1))
                    for k in range(KD):
                        last = pe.matmul(ps[0:n, bank(t), :], hnT[:, k, c:c + n], w_slot(i)[:, k, :],
                                         start=(k == 0), stop=(k == KD - 1))
                    last.then_inc(rows_made, 1)

            def columns(bank, i, width, m, src, chunks, cols):
                for k in range(chunks):
                    lhsT = w_slot(i, width)[:, k, m * P:(m + 1) * P]
                    for j in range(2):
                        out = banks(bank, BANK - cols // 2, BANK) if j == 0 else banks(bank + 1, 0, cols // 2)
                        last = pe.matmul(out, lhsT, src[:, k, j * cols // 2:(j + 1) * cols // 2], start=(k == 0),
                                         stop=(k == chunks - 1))
                return last

            project_rows("k", 0, lambda t: t % 8)
            project_rows("q", TILES, lambda t: (TILES + t) % 8)
            i = STREAM["u"]
            loaded(pe, i)
            for mt in range(KW):
                b = (2 + 2 * mt) % 8
                pe.wait_ge(rows_out, min(2 * TILES, b + 2 if b >= 2 else 2 * TILES))
                columns(b, i, W, mt, hnT, KD, ALL).then_inc(u_made, 1)
            project_rows("v", 2 * TILES, lambda t: 2 + t)

            for i in range(2 * TILES):
                rows, t = (krow, qrow)[i // TILES], i % TILES
                n, b = TILE_ROWS[t], (7 + i) % 8
                if t == 0:
                    pe.wait_ge(qk_ready, i // TILES + 1)
                if i == 0:
                    pe.wait_ge(u_out, 3 * KW)
                if 3 <= i < 8:
                    pe.wait_ge(v_out, b - 1)
                if i >= 8:
                    pe.wait_ge(qkT_out, i - 7)
                for j in range(PAIRS):
                    last = pe.transpose(banks(b, j * P, j * P + n), rows[0:n, t, j * P:(j + 1) * P], ident[0:n, 0:n])
                last.then_inc(qkT_made, 1)
            pe.wait_ge(qkT_out, 2 * TILES)
            for grp, lo in ((0, META + SEQ - POOL_STATE), (1, UW - POOL_STATE)):
                for g in range(KW):
                    last = pe.transpose(banks(6 + grp, g * P, (g + 1) * P, POOL_STATE), U[:, g, lo:lo + POOL_STATE],
                                        ident[:, :])
            last.then_inc(poolT_made, 1)
            for g in range(KW):
                pe.wait_ge(pooled, g + 1)
                if g == 0:
                    pe.wait_ge(consts_loaded, 16 * 9)
                if g == 3:
                    pe.wait_ge(poolT_out, 3)
                pe.matmul(banks(2 * g, BANK - TOK // 2, BANK), mix[:, g, :], mixedT[:, g, 0:TOK // 2], start=True, stop=True)
                pe.matmul(banks(2 * g + 1, 0, TOK // 2), mix[:, g, :], mixedT[:, g, TOK // 2:TOK], start=True,
                          stop=True).then_inc(mix_made, 1)
            pe.wait_ge(mix_out, KW)

            def scores(n):
                pair, b, hh = UNITS[n]
                z = 2 * (n % 2)
                if n >= 2:
                    pe.wait_ge(gates_done, n - 1)
                if b < FRAME_TILES:
                    rows = slice(hh * HD, (hh + 1) * HD)
                    q = qT[rows, pair, b * P:(b + 1) * P]
                    pe.matmul(banks(z, BANK - META, BANK), q, kT[rows, pair, TOK:ALL], start=True, stop=True)
                    pe.matmul(banks(z + 1, 0, P * (b + 1)), q, kT[rows, pair, 0:P * (b + 1)], start=True,
                              stop=True)
                    pe.matmul(banks(z + 1, P * b, P * (b + 1)), ident_b[:, :], mask_p[:, :], start=False,
                              stop=True, skip_group_check=True).then_inc(z_made, 1)
                else:
                    for s in range(2):
                        rows = slice(s * HD, (s + 1) * HD)
                        q = qT[rows, pair, SEQ:TOK]
                        pe.matmul(banks(z, 0, PAST, SAMP, s * SAMP), q, pastkT[rows, pair, :], start=True, stop=True,
                                  skip_group_check=True)
                        pe.matmul(banks(z + 1, 0, SAMP, SAMP, s * SAMP), q, kT[rows, pair, SEQ:TOK], start=True, stop=False,
                                  skip_group_check=True)
                    pe.matmul(banks(z + 1, 0, SAMP), ident_b[:, :], mask_s[:, :], start=False, stop=True,
                              skip_group_check=True).then_inc(z_made, 1)

            def turn(n):
                pair, b, hh = UNITS[n]
                at = 4 + n % 2
                pe.wait_ge(a_ready, n + 1)
                if n >= 2:
                    pe.wait_ge(AT_out, n - 1)
                if n < 2:
                    pe.wait_ge(mix_out, KW)
                w = beta[:, n % 3, :]
                if b < FRAME_TILES:
                    lo = FIRST[b]
                    for c in range(b + 1):
                        pe.transpose(banks(at, c * P, (c + 1) * P), w[:, lo + META + c * P:lo + META + (c + 1) * P],
                                     ident[:, :])
                    if n >= 1:
                        pe.wait_ge(AT_out, n)
                    pe.transpose(banks(6, 0, P, SM), w[:, lo - SAMP:lo + META], ident[:, :]).then_inc(AT_made, 1)
                else:
                    lo = FIRST[b]
                    for c in range(PAST // P):
                        pe.transpose(banks(at, c * P, (c + 1) * P), w[:, lo + c * P:lo + (c + 1) * P], ident[:, :])
                    pe.wait_ge(AT_out, n)
                    pe.transpose(banks(6, 0, P, SAMP), w[:, lo + PAST:CW], ident[:, :]).then_inc(AT_made, 1)

            def values(n):
                pair, b, hh = UNITS[n]
                group = GROUP_OF[n]
                pe.wait_ge(AT_out, n + 1)
                if group >= 1 and hh == 0:
                    pe.wait_ge(pv_out, group)
                if b < FRAME_TILES:
                    out = banks(7, BANK - P, BANK, HD, hh * HD)
                    cols = slice((2 * pair + hh) * HD, (2 * pair + hh + 1) * HD)
                    for c in range(b + 1):
                        pe.matmul(out, V[:, c, cols], AT[:, n % 2, c, :], start=(c == 0), stop=False,
                                  skip_group_check=True)
                    pe.matmul(out, V[SAMP:SM, FRAME_TILES, cols], AT[SAMP:SM, n % 2, FRAME_TILES, :], start=False,
                              stop=True, skip_group_check=True).then_inc(pv_made, 1)
                else:
                    if pair == 0:
                        pe.wait_ge(pastv_loaded, 16)
                    for s in range(2):
                        out = banks(7, BANK - P, BANK - P + SAMP, HD, s * HD)
                        cols = slice((2 * pair + s) * HD, (2 * pair + s + 1) * HD)
                        q = slice(s * SAMP, (s + 1) * SAMP)
                        for c in range(PAST // P):
                            pe.matmul(out, pastV[:, c, cols], AT[:, n % 2, c, q], start=(c == 0), stop=False,
                                      skip_group_check=True)
                        last = pe.matmul(out, V[0:SAMP, FRAME_TILES, cols], AT[0:SAMP, n % 2, FRAME_TILES, q],
                                         start=False, stop=True, skip_group_check=True)
                    last.then_inc(pv_made, 1)

            for n in range(len(UNITS) + 3):
                if n < len(UNITS):
                    scores(n)
                if 2 <= n < len(UNITS) + 2:
                    turn(n - 2)
                if n >= 3:
                    values(n - 3)

            pe.wait_ge(pv_out, GROUP_OF[-1] + 1)
            for m in range(2 * KD):
                br, mt = m // KD, m % KD
                bank = 4 * (m % 2)
                if m >= 2:
                    pe.wait_ge(merged, m - 1)
                gi, wi = STREAM["gate", br, mt // 4], STREAM["out", br]
                if mt % 4 == 0:
                    loaded(pe, gi)
                if mt == 0:
                    loaded(pe, wi)
                columns(bank, gi, BANK, mt % 4, hnT, KD, TOK).then_inc(g_made, 1)
                src = (mixedT, sbT)[br]
                columns(bank + 2, wi, D, mt, src, KW, TOK).then_inc(p_made, 1)

            def turn_tile(t):
                n = TOK_ROWS[t]
                pe.wait_ge(hn2_ready, t + 1)
                if t >= 1:
                    pe.wait_ge(hn2T_out, t)
                for k in range(KD):
                    last = pe.transpose(banks(4, k * P, k * P + n), hn2[0:n, t % 2, k * P:(k + 1) * P], ident[0:n, 0:n])
                last.then_inc(hn2T_made, 1)

            def route_tile(t):
                n = TOK_ROWS[t]
                pe.wait_ge(hn2T_out, t + 1)
                width = GROUPS + EXPERTS
                for k in range(KD):
                    last = pe.matmul(banks(6, t * width, (t + 1) * width, n), hn2T[:, t % 2, k, 0:n], router[:, k, :],
                                     start=(k == 0), stop=(k == KD - 1), skip_group_check=True)
                last.then_inc(logits_made, 1)

            pe.wait_ge(merged, 2 * KD)
            for j in range(2):
                loaded(pe, STREAM["wo", j])
            for t in range(TILES):
                n, c = TOK_ROWS[t], P * t
                if t >= 2:
                    pe.wait_ge(h_ready, t - 1)
                for j in range(2):
                    for k in range(KD):
                        last = pe.matmul(banks(2 * (t % 2) + j, 0, BANK, n), mergedT[:, k, c:c + n],
                                         w_slot(STREAM["wo", j])[:, k, :], start=(k == 0), stop=(k == KD - 1))
                    if j == 0 and t >= 1:
                        turn_tile(t - 1)
                last.then_inc(o_made, 1)
                if t >= 1:
                    route_tile(t - 1)
            turn_tile(TILES - 1)
            route_tile(TILES - 1)

            pe.wait_ge(hot_ready, 1)
            for t in range(TILES):
                n = TOK_ROWS[t]
                out = banks(0, t * EXPERTS, (t + 1) * EXPERTS, n)
                for s in range(t):
                    pe.matmul(out, ones[:, 0:n], hot_b[:, s, :], start=(s == 0), stop=False, skip_group_check=True)
                pe.matmul(out, tri[0:n, 0:n], hot_b[0:n, t, :], start=(t == 0), stop=True, skip_group_check=True)
            for t in range(TILES):
                n = TOK_ROWS[t]
                last = pe.matmul(banks(1, 0, EXPERTS), ones[0:n, :], hot_b[0:n, t, :], start=(t == 0), stop=(t == TILES - 1))
            last.then_inc(ranks_made, 1)
            pe.wait_ge(table_in, 1)
            for k in range(TOP):
                for t in range(TILES):
                    n = TOK_ROWS[t]
                    last = pe.matmul(banks(2, 0, 3 * NBLK), slot_hot[0:n, k, t, :],
                                     blk_val[0:n, k, t, :, :].rearrange("p v b -> p (v b)"),
                                     start=(k + t == 0), stop=(k == TOP - 1 and t == TILES - 1))
            last.then_inc(table_made, 1)

            def turn_x(odd):
                for c in range(KD // 2):
                    last = pe.transpose(banks(odd, c * P, (c + 1) * P), xg[:, odd, c * P:(c + 1) * P], ident[:, :])
                last.then_inc(eT_made, 1)

            def wide(e, odd, slot):
                pe.wait_ge(eT_out, e + 1)
                w = ring[:, slot:slot + 2, :].rearrange("p m (k n) -> p k m n", n=F)
                for k in range(KD):
                    for s in range(2):
                        out = banks(2 + odd, 0, BANK, SLOTS, s * SLOTS).rearrange("p (m n) -> p m n", m=2)
                        last = pe.matmul(out, xT[:, odd, k % (KD // 2), k // (KD // 2), :],
                                         w[:, k, :, s * F // 2:(s + 1) * F // 2], start=(k == 0), stop=(k == KD - 1),
                                         skip_group_check=True)
                last.then_inc(wide_made, 1)

            def turn_hidden(e, odd):
                pe.wait_ge(hid_done, e + 1)
                for c in range(KF // 2):
                    last = pe.transpose(banks(4 + odd, c * P, (c + 1) * P), hid[:, c * P:(c + 1) * P], ident[:, :])
                last.then_inc(hidT_made, 1)

            def down(e, odd, slot, first=False):
                pe.wait_ge(hidT_out, e + 1)
                if not first:
                    pe.wait_ge(y_ready, e)
                w = ring[:, slot, :].rearrange("p (k n) -> p k n", n=D)
                for k in range(KF):
                    for s in range(2):
                        last = pe.matmul(banks(6 + odd, 0, BANK, SLOTS, s * SLOTS),
                                         hidT[:, k % (KF // 2), k // (KF // 2), :],
                                         w[:, k, s * HALF_D:(s + 1) * HALF_D], start=(k == 0), stop=(k == KF - 1),
                                         skip_group_check=True)
                last.then_inc(down_made, 1)

            def around(e, odd, first=False, last=False):
                for kind in ("gate", "up"):
                    pe.wait_ge(slot_loaded[expert_slot(kind, odd)], expert_count(e, odd))
                wide(e, odd, expert_slot("gate", odd))
                if not last:
                    pe.wait_ge(gathered[1 - odd], (e + (odd - 1) + 1) * 8 + 16)
                    turn_x(1 - odd)
                turn_hidden(e, odd)
                pe.wait_ge(slot_loaded[expert_slot("down", odd)], expert_count(e, odd))
                down(e, odd, expert_slot("down", odd), first)

            pe.wait_ge(table_out, 1)
            pe.wait_ge(gathered[0], 16)
            turn_x(0)
            around(0, 0, first=True)
            around(1, 1)
            with pe.Fori(1, EXPERTS // 2 - 1) as it:
                for odd in range(2):
                    around(it * 2 + odd, odd)
            around(EXPERTS - 2, 0)
            around(EXPERTS - 1, 1, last=True)

            pe.wait_ge(table_out, 1)
            n_extra = pe.value_load(ctl[0:1, 0:1], min_val=0, max_val=EXTRA)
            with pe.If(n_extra > 0):
                with pe.Fori(0, EXTRA) as i:
                    with pe.If(i < n_extra):
                        pe.wait_ge(extra_gathered, i * 16 + 16)
                        turn_x(0)
                        pe.wait_ge(extra_loaded, i * 48 + 48)
                        wide(i + EXPERTS, 0, 0)
                        turn_hidden(i + EXPERTS, 0)
                        down(i + EXPERTS, 0, 2)

        @block.vector
        def _(dve):
            count = [0]

            def link(ins):
                count[0] += 1
                ins.then_inc(step, 1)
                dve.wait_ge(step, count[0])

            dve.memset(stat[:, :, :], 1.0).then_inc(stat_ready, 1)
            dve.memset(stat_h[:, :, :], 1.0).then_inc(stat_ready, 1)
            dve.wait_ge(sq_done, TILES)
            dve.tensor_scalar(stat[:, 1, 0:TILES], stat[:, 0, 0:TILES], 1.0 / D, EPS, ALU.mult, ALU.add).then_inc(ms_done, 1)
            dve.wait_ge(root_done, 1)
            link(dve.reciprocal(stat[:, 3, 0:TILES], stat[:, 2, 0:TILES]))
            dve.wait_ge(early_T, 1)
            dve.tensor_copy(U[:, :, META + SEQ:META + SEQ + POOL_STATE],
                            banks(3, 0, KW * POOL_STATE).rearrange("p (g n) -> p g n", g=KW)).then_inc(poolT_out, 1)

            def norm_x(t):
                n = TILE_ROWS[t]
                if t >= 2:
                    dve.wait_ge(xT_made, t - 1)
                dve.tensor_scalar(xn[0:n, t % 2, :], xr[0:n, t, :], stat[0:n, 3, t:t + 1], None, ALU.mult).then_inc(xn_ready, 1)

            def take_hn(t):
                n, c = TILE_ROWS[t], P * t
                dve.wait_ge(xT_made, t + 1)
                src = banks(2 * (t % 2), 0, 2 * BANK).rearrange("p (k n) -> p k n", k=KD)[:, :, 0:n]
                dve.tensor_tensor(hnT[:, :, c:c + n], src,
                                  gain_mix[:, :].unsqueeze(2).to_broadcast([P, KD, n]), ALU.mult).then_inc(hnT_ready, 1)

            dve.wait_ge(consts_loaded, 16 * 9)
            norm_x(0)
            for t in range(TILES):
                if t + 1 < TILES:
                    norm_x(t + 1)
                take_hn(t)

            dve.wait_ge(stat_ready, 2)
            for i, (rows, gain) in enumerate(((krow, gain_k), (qrow, gain_q))):
                for t in range(TILES):
                    u = i * TILES + t
                    n = TILE_ROWS[t]
                    dve.wait_ge(rows_made, u + 1)
                    if u == 0:
                        dve.wait_ge(xT_made, TILES)
                    dve.wait_ge(rows_sq, u + 1)
                    dve.tensor_tensor(rows[0:n, t, :].rearrange("p (h d) -> p h d", h=HEADS),
                                      ps[0:n, u % 8, :].rearrange("p (h d) -> p h d", h=HEADS),
                                      gain[0:n, :].unsqueeze(1).to_broadcast([n, HEADS, HD]), ALU.mult)
                    dve.tensor_reduce(stat_h[0:n, 0, t * HEADS:(t + 1) * HEADS],
                                      square[0:n, (u % 2) * W:(u % 2 + 1) * W].rearrange("p (h d) -> p h d", h=HEADS),
                                      AX.X, ALU.add).then_inc(rows_out, 1)
                dve.wait_ge(rows_out, (i + 1) * TILES)
                dve.tensor_scalar(stat_h[:, 1, :], stat_h[:, 0, :], 1.0 / HD, EPS, ALU.mult, ALU.add).then_inc(qk_ms, 1)
                dve.wait_ge(qk_root, i + 1)
                link(dve.reciprocal(stat_h[:, 0, :], stat_h[:, 2, :]))
                for t in range(TILES):
                    n = TILE_ROWS[t]
                    r = rows[0:n, t, :].rearrange("p (h d) -> p h d", h=HEADS)
                    inv = stat_h[0:n, 0, t * HEADS:(t + 1) * HEADS].unsqueeze(2).to_broadcast([n, HEADS, HD])
                    last = dve.tensor_tensor(r, r, inv, ALU.mult)
                last.then_inc(qk_ready, 1)
                dve.wait_ge(qk_ready, i + 1)

            for g in range(KW):
                dve.wait_ge(sums_done, g + 1)
                sums = ptmp[:, g % 2, :]
                for dst, lo, n in ((0, META, SEQ), (SEQ, UW - SAMP, SAMP)):
                    last = dve.scalar_tensor_tensor(out=mixedT[:, g, dst:dst + n], in0=sums[:, lo:lo + n],
                                                    scalar=1.0 / 2 ** (g + 1), in1=U[:, g, lo:lo + n],
                                                    op0=ALU.mult, op1=ALU.subtract)
                last.then_inc(pooled, 1)
            for i in range(2 * TILES):
                dst, t = (kT, qT)[i // TILES], i % TILES
                n, c = TILE_ROWS[t], P * t
                dve.wait_ge(qkT_made, i + 1)
                dve.tensor_copy(dst[:, :, c:c + n],
                                ps[:, (7 + i) % 8, :].rearrange("p (j n) -> p j n", j=PAIRS)[:, :, 0:n]).then_inc(qkT_out, 1)
            dve.wait_ge(poolT_made, 1)
            for i in range(2):
                dve.tensor_copy(pool_rows[32 * i:32 * i + POOL_STATE, :], ps[0:POOL_STATE, 6 + i, :]).then_inc(poolT_out, 1)

            dve.wait_ge(qkT_out, 2 * TILES)
            dve.wait_ge(qkT_made, 2 * TILES)
            dve.wait_ge(k_stored, 16 * 6)
            dve.memset(beta[:, :, :], 0.0).then_inc(attn_init, 1)
            dve.memset(keep[:, :, CW:CW + 1], 1.0).then_inc(attn_init, 1)
            dve.wait_ge(attn_init, 2)
            dve.wait_ge(consts_made, 1)

            def weigh(n):
                pair, b, hh = UNITS[n]
                lo = FIRST[b]
                kp = keep[:, n % 2, :]
                dve.wait_ge(gates_done, n + 1)
                count[0] += 1
                dve.tensor_tensor_scan(kp[:, lo:CW][:, ::-1], kp[:, lo:CW][:, ::-1], zeros[:, lo:CW], 1.0, ALU.mult,
                                       ALU.add).then_inc(step, 1)
                dve.wait_ge(step, count[0])
                dve.tensor_tensor(beta[:, n % 3, lo:CW], beta[:, n % 3, lo:CW], kp[:, lo + 1:CW + 1],
                                  ALU.mult).then_inc(a_ready, 1)

            def take_output(n):
                pair, b, hh = UNITS[n]
                if b < FRAME_TILES and hh == 0:
                    return
                group = GROUP_OF[n]
                dve.wait_ge(pv_made, n + 1)
                if group == 0:
                    dve.wait_ge(poolT_made, 1)
                if b < FRAME_TILES:
                    dve.tensor_copy(sbT[:, pair, b * P:(b + 1) * P],
                                    banks(7, BANK - P, BANK)).then_inc(pv_out, 1)
                else:
                    dve.tensor_copy(sbT[:, pair, SEQ:TOK], banks(7, BANK - P, BANK - P + SAMP)).then_inc(pv_out, 1)

            for n in range(len(UNITS) + 4):
                if n >= 4:
                    take_output(n - 4)
                if n < len(UNITS):
                    weigh(n)

            for m in range(2 * KD):
                br, mt = m // KD, m % KD
                proj = banks(4 * (m % 2) + 2, BANK - TOK // 2, BANK + TOK // 2)
                dve.wait_ge(g_out, m + 1)
                dve.wait_ge(p_made, m + 1)
                if br == 0:
                    dve.tensor_tensor(mergedT[:, mt, :], sg[:, m % 2, :], proj, ALU.mult).then_inc(merged, 1)
                else:
                    link(dve.tensor_tensor(sg[:, m % 2, :], sg[:, m % 2, :], proj, ALU.mult))
                    dve.tensor_tensor(mergedT[:, mt, :], mergedT[:, mt, :], sg[:, m % 2, :], ALU.add).then_inc(merged, 1)

            dve.wait_ge(h_loaded, 16 * (TILES + 1))
            for t in range(TILES):
                n = TOK_ROWS[t]
                dve.wait_ge(o_made, t + 1)
                dve.tensor_tensor(h[0:n, t, :], h[0:n, t, :], banks(2 * (t % 2), 0, 2 * BANK, n), ALU.add).then_inc(h_ready, 1)
                dve.wait_ge(hsq, t + 1)
                dve.tensor_scalar(stat[0:n, 1, t:t + 1], stat[0:n, 0, t:t + 1], 1.0 / D, EPS, ALU.mult,
                                  ALU.add).then_inc(hms, 1)
                dve.wait_ge(hroot, t + 1)
                link(dve.reciprocal(stat[0:n, 3, t:t + 1], stat[0:n, 2, t:t + 1]))
                if t >= 2:
                    dve.wait_ge(hn_stored[t % 2], 16 * (t // 2))
                dve.scalar_tensor_tensor(out=hn2[0:n, t % 2, :], in0=h[0:n, t, :], scalar=stat[0:n, 3, t:t + 1],
                                         in1=gain_ffn[0:n, :], op0=ALU.mult, op1=ALU.mult).then_inc(hn2_ready, 1)
                dve.wait_ge(hn2T_made, t + 1)
                if t >= 2:
                    dve.wait_ge(logits_made, t - 1)
                dve.tensor_copy(hn2T[:, t % 2, :, 0:n],
                                banks(4, 0, 2 * BANK).rearrange("p (k n) -> p k n", k=KD)[:, :, 0:n]).then_inc(hn2T_out, 1)

            width = GROUPS + EXPERTS
            dve.wait_ge(logits_made, TILES)
            dve.memset(logits[:, :, :], 0.0)
            link(dve.memset(lg8[:, :, :], NEG))
            for t in range(TILES):
                n = TOK_ROWS[t]
                last = dve.tensor_tensor(logits[0:n, t, :], banks(6, t * width, (t + 1) * width, n), router_bias[0:n, :],
                                         ALU.add)
            link(last)
            link(dve.tensor_copy(lg8[:, :, 0:GROUPS], logits[:, :, 0:GROUPS]))
            for t in range(TILES):
                last = dve.max(best_g[:, t, :], lg8[:, t, :])
            link(last)
            for t in range(TILES):
                last = dve.max_index(at_g[:, t, :], best_g[:, t, :], lg8[:, t, :])
            link(last)
            wide3 = [P, TILES, EXPERTS]

            def over_e(ap):
                return ap.unsqueeze(2).to_broadcast(wide3)

            group_of = small[:, 2, :]
            link(dve.tensor_copy(group_of, at_g[:, :, 0:1].rearrange("p t a -> p (t a)")))
            link(dve.tensor_scalar(small[:, 3, :], group_of, float(PER_GROUP), None, ALU.mult))
            link(dve.tensor_tensor(fm[:, :, :], iota_e[:, 0:EXPERTS].unsqueeze(1).to_broadcast(wide3), over_e(small[:, 3, :]),
                                   ALU.subtract))
            link(dve.tensor_scalar(prod[:, 0, :, :], fm[:, :, :], 0.0, None, ALU.is_ge))
            link(dve.tensor_scalar(prod[:, 1, :, :], fm[:, :, :], float(PER_GROUP), None, ALU.is_lt))
            link(dve.tensor_tensor(prod[:, 0, :, :], prod[:, 0, :, :], prod[:, 1, :, :], ALU.mult))
            link(dve.tensor_tensor(fm[:, :, :], logits[:, :, GROUPS:], prod[:, 0, :, :], ALU.mult))
            link(dve.tensor_scalar(prod[:, 1, :, :], prod[:, 0, :, :], -NEG, NEG, ALU.mult, ALU.add))
            link(dve.tensor_tensor(fm[:, :, :], fm[:, :, :], prod[:, 1, :, :], ALU.add))
            for t in range(TILES):
                last = dve.max(best_e[:, t, :], fm[:, t, :])
            link(last)
            for t in range(TILES):
                last = dve.max_index(at_e[:, t, :], best_e[:, t, :], fm[:, t, :])
            link(last)
            dve.tensor_tensor(eg[:, :, :], logits[:, :, 0:GROUPS],
                              best_g[:, :, 0:1].to_broadcast([P, TILES, GROUPS]), ALU.subtract)
            dve.tensor_tensor(small[:, 0, :], best_e[:, :, 1:2].rearrange("p t a -> p (t a)"),
                              best_e[:, :, 0:1].rearrange("p t a -> p (t a)"), ALU.subtract).then_inc(route_a, 1)
            for k in range(TOP):
                last = dve.tensor_copy(pick[:, k, :], at_e[:, :, k:k + 1].rearrange("p t a -> p (t a)"))
            link(last)
            for k in range(TOP):
                last = dve.tensor_tensor(hot[:, k, :, :], iota_e[:, 0:EXPERTS].unsqueeze(1).to_broadcast(wide3),
                                         over_e(pick[:, k, :]), ALU.is_equal)
            link(last)
            dve.tensor_tensor(hot_b[:, :, :], hot[:, 0, :, :], hot[:, 1, :, :], ALU.add).then_inc(hot_ready, 1)
            dve.wait_ge(route_e, 1)
            link(dve.tensor_reduce(small[:, 4, :], eg[:, :, :], AX.X, ALU.add))
            link(dve.tensor_scalar(small[:, 5, :], small[:, 1, :], 1.0, None, ALU.add))
            link(dve.tensor_tensor(small[:, 6, :], small[:, 4, :], small[:, 5, :], ALU.mult))
            link(dve.reciprocal(small[:, 7, :], small[:, 6, :]))
            link(dve.tensor_copy(val[:, 0, :, 2], small[:, 7, :]))
            link(dve.tensor_tensor(val[:, 1, :, 2], small[:, 7, :], small[:, 1, :], ALU.mult))
            link(dve.tensor_copy(val[:, 0, :, 0], token[:, :]))
            dve.tensor_copy(val[:, 1, :, 0], token[:, :])
            dve.tensor_copy(val[:, 0, :, 1], token[:, :])
            link(dve.tensor_scalar(val[:, 1, :, 1], token[:, :], float(TOK), None, ALU.add))

            dve.wait_ge(ranks_made, 1)
            link(dve.tensor_copy(cnt[:, :], banks(1, 0, EXPERTS)))
            link(dve.tensor_scalar(nb[:, :], cnt[:, :], float(SLOTS), None, ALU.is_gt))
            for j in range(2, J):
                link(dve.tensor_scalar(ebase[:, 0, :], cnt[:, :], float(SLOTS * j), None, ALU.is_gt))
                link(dve.tensor_tensor(nb[:, :], nb[:, :], ebase[:, 0, :], ALU.add))
            link(dve.tensor_tensor_scan(ebase[:, 1, :], zeros[:, 0:EXPERTS], nb[:, :], 0.0, ALU.add, ALU.add))
            link(dve.tensor_tensor(ebase[:, 0, :], ebase[:, 1, :], nb[:, :], ALU.subtract))
            for k in range(TOP):
                for t in range(TILES):
                    n = TOK_ROWS[t]
                    dve.tensor_tensor(prod[0:n, k, t, :], hot[0:n, k, t, :], banks(0, t * EXPERTS, (t + 1) * EXPERTS, n),
                                      ALU.mult)
            dve.memset(prod[SAMP:P, :, FRAME_TILES, :], 0.0).then_inc(step, 1)
            count[0] += 1
            dve.wait_ge(step, count[0])
            link(dve.tensor_reduce(rank[:, :, :], prod[:, :, :, :], AX.X, ALU.add))
            link(dve.tensor_tensor(prod[:, :, :, :].rearrange("p k t e -> p (k t) e"),
                                   hot[:, :, :, :].rearrange("p k t e -> p (k t) e"),
                                   ebase[:, 0, :].unsqueeze(1).to_broadcast([P, TOP * TILES, EXPERTS]), ALU.mult))
            link(dve.tensor_reduce(base_of[:, :, :], prod[:, :, :, :], AX.X, ALU.add))
            link(dve.tensor_scalar(past_first[:, :, :], rank[:, :, :], float(SLOTS), None, ALU.is_ge))
            link(dve.tensor_copy(blk[:, :, :], past_first[:, :, :]))
            for j in range(2, J):
                link(dve.tensor_scalar(tmp10[:, :, :], rank[:, :, :], float(SLOTS * j), None, ALU.is_ge))
                link(dve.tensor_tensor(blk[:, :, :], blk[:, :, :], tmp10[:, :, :], ALU.add))
            link(dve.scalar_tensor_tensor(out=rank[:, :, :], in0=blk[:, :, :], scalar=-float(SLOTS), in1=rank[:, :, :],
                                          op0=ALU.mult, op1=ALU.add))
            link(dve.tensor_tensor(blk[:, :, :], blk[:, :, :], base_of[:, :, :], ALU.add))
            link(dve.tensor_scalar(blk[:, :, :], blk[:, :, :], float(EXPERTS - 1), None, ALU.add))
            link(dve.tensor_tensor(blk[:, :, :], blk[:, :, :], pick[:, :, :], ALU.subtract))
            link(dve.tensor_tensor(blk[:, :, :], blk[:, :, :], past_first[:, :, :], ALU.mult))
            link(dve.tensor_tensor(blk[:, :, :], blk[:, :, :], pick[:, :, :], ALU.add))
            kt = TOP * TILES
            dve.tensor_tensor(slot_hot[:, :, :, :].rearrange("p k t s -> p (k t) s"),
                              iota_r[:, :].unsqueeze(1).to_broadcast([P, kt, 2 * SLOTS]),
                              rank[:, :, :].rearrange("p k t -> p (k t)").unsqueeze(2).to_broadcast([P, kt, 2 * SLOTS]),
                              ALU.is_equal)
            link(dve.tensor_tensor(blk_hot[:, :, :, :].rearrange("p k t s -> p (k t) s"),
                                   iota_e[:, :].unsqueeze(1).to_broadcast([P, kt, NBLK]),
                                   blk[:, :, :].rearrange("p k t -> p (k t)").unsqueeze(2).to_broadcast([P, kt, NBLK]),
                                   ALU.is_equal))
            for v in range(3):
                last = dve.tensor_tensor(blk_val[:, :, :, v, :].rearrange("p k t s -> p (k t) s"),
                                         blk_hot[:, :, :, :].rearrange("p k t s -> p (k t) s"),
                                         val[:, :, :, v].rearrange("p k t -> p (k t)").unsqueeze(2).to_broadcast([P, kt, NBLK]),
                                         ALU.mult)
            last.then_inc(table_in, 1)
            for i in range(EXTRA):
                last = dve.tensor_scalar(etab[:, i, :], ebase[0:1, 1, :], float(i), None, ALU.is_le)
            link(last)
            link(dve.tensor_reduce(efin[:, 1:1 + EXTRA], etab[:, :, :], AX.X, ALU.add))
            link(dve.tensor_scalar(efin[:, 1:1 + EXTRA], efin[:, 1:1 + EXTRA], float(EXPERTS - 1), None, ALU.min))
            link(dve.tensor_copy(efin[:, 0:1], ebase[0:1, 1, EXPERTS - 1:EXPERTS]))
            link(dve.tensor_copy(ctl[:, :], efin[:, :]))
            dve.wait_ge(table_made, 1)
            table = banks(2, 0, 3 * NBLK).rearrange("p (v b) -> p v b", v=3)
            link(dve.tensor_scalar(tabf[:, :, :], table[:, 0:2, :], 0.0, EMPTY, ALU.is_equal, ALU.mult))
            link(dve.tensor_tensor(tabf[:, :, :], tabf[:, :, :], table[:, 0:2, :], ALU.add))
            link(dve.tensor_scalar(tabf[:, :, :], tabf[:, :, :], 2.0, half[:, :], ALU.mult, ALU.add))
            link(dve.tensor_copy(wgt[:, :], table[:, 2, :]))
            dve.tensor_copy(idx[:, :, :], tabf[:, :, :]).then_inc(table_out, 1)

            def take_up(e, odd):
                dve.wait_ge(silu_done, e + 1)
                dve.tensor_tensor(hid[:, :], silu[:, :], ps[:, 2 + odd, F // 2:F], ALU.mult).then_inc(hid_done, 1)

            def take_hidden(e, odd):
                dve.wait_ge(hidT_made, e + 1)
                dve.tensor_copy(hidT[:, :, :, :],
                                banks(4 + odd, 0, F // 2).rearrange("p (c h n) -> p c h n", c=KF // 2, h=2)
                                ).then_inc(hidT_out, 1)

            with dve.Fori(0, EXPERTS // 2) as it:
                for odd in range(2):
                    take_up(it * 2 + odd, odd)
                    take_hidden(it * 2 + odd, odd)

            n_extra = dve.value_load(ctl[0:1, 0:1], min_val=0, max_val=EXTRA)
            with dve.If(n_extra > 0):
                with dve.Fori(0, EXTRA) as i:
                    with dve.If(i < n_extra):
                        take_up(i + EXPERTS, 0)
                        take_hidden(i + EXPERTS, 0)

            for t in range(TILES):
                n = TOK_ROWS[t]
                dve.wait_ge(part_loaded[t], 32)
                link(dve.tensor_tensor(h[0:n, t, :], h[0:n, t, :], ring[0:n, t, 0:D], ALU.add))
                dve.tensor_tensor(h[0:n, t, :], h[0:n, t, :], ring[0:n, t, D:2 * D], ALU.add).then_inc(y_done, 1)


_INS = ["x_prompt", "x_sample", "cache_sb_k", "cache_sb_v", "state_pool", "meta_tokens", "norm_mix", "w_in", "q_norm",
        "k_norm", "pool_mix", "pool_scale", "w_pool_out", "w_sb_out", "w_o", "norm_ffn", "w_router_group",
        "b_router_group", "w_router_expert", "b_router_expert", "w_gate", "w_up", "w_down"]


def kernel(**inputs):
    import numpy as _np
    import concourse.bacc as _bacc
    from concourse import mybir as _mybir
    from concourse.bass_utils import run_bass_kernel_spmd as _run

    nc = _bacc.Bacc("TRN2", target_bir_lowering=False, num_devices=1)
    arrays, args = {}, []
    for name in _INS:
        a = _np.ascontiguousarray(inputs[name])
        if name in ("cache_sb_k", "cache_sb_v"):
            a = a.reshape(PAST, W)
        if name == "state_pool":
            a = a.reshape(POOL_STATE, W)
        arrays[f"in_{name}_dram"] = a
        args.append(nc.dram_tensor(f"in_{name}_dram", a.shape, _mybir.dt.from_np(a.dtype), kind="ExternalInput").ap())
    outs = {"y": (TOK, D), "nk_prompt": (META + SEQ, W), "nv_prompt": (META + SEQ, W), "np_prompt": (POOL_STATE, W),
            "nk_sample": (SAMP, W), "nv_sample": (SAMP, W), "np_sample": (POOL_STATE, W)}
    for name, shape in outs.items():
        args.append(nc.dram_tensor(f"out_{name}_dram", shape, F32, kind="ExternalOutput").ap())
    args.append(nc.dram_tensor("hn_dram", (2 * TOK, D // 2), F32, kind="Internal").ap())
    args.append(nc.dram_tensor("part_dram", (2 * TOP * TOK, D // 2), F32, kind="Internal").ap())
    build(nc, *args)
    r = _run(nc, [arrays], core_ids=[0])
    got = {name: r.results[0][f"out_{name}_dram"] for name in outs}
    heads = (HEADS, HD)
    return (got["y"][:SEQ].reshape(1, SEQ, D), got["y"][SEQ:].reshape(1, SAMP, D),
            got["nk_prompt"].reshape(1, 1, META + SEQ, *heads), got["nv_prompt"].reshape(1, 1, META + SEQ, *heads),
            got["np_prompt"].reshape(1, 1, POOL_STATE, W),
            got["nk_sample"].reshape(1, 1, SAMP, *heads), got["nv_sample"].reshape(1, 1, SAMP, *heads),
            got["np_sample"].reshape(1, 1, POOL_STATE, W))
```

```python
from contextlib import ExitStack

import concourse.bass as bass
from concourse import mybir

F32 = mybir.dt.float32
F32R = mybir.dt.float32r
BF16 = mybir.dt.bfloat16
I32 = mybir.dt.int32
U32 = mybir.dt.uint32
ALU = mybir.AluOpType
ACT = mybir.ActivationFunctionType
AX = mybir.AxisListType

P = 128
BANK = 512
D = 1024
KD = D // P
SEQ, META, SAMP, PAST = 512, 16, 64, 512
HEADS, HD = 8, 64
PAIRS = HEADS // 2
W = HEADS * HD
KW = W // P
POOL_STATE = 15
EPS = 1e-6
FRAME_TILES = SEQ // P
TILES = FRAME_TILES + 1
SM = SAMP + META
TOK = SEQ + SAMP
ALL = TOK + META
HALF_D = D // 2
UW = META + SEQ + POOL_STATE + SAMP
GROUPS, PER_GROUP, EXPERTS = 4, 8, 32
TOP = 2
F = 512
KF = F // P
SLOTS = 64
J = -(-TOK // SLOTS)
EXTRA = TOK * TOP // SLOTS
NBLK = EXPERTS + EXTRA
RING = 6
SLOT = KD * BANK
NEG = -1.0e30
DUMP = 2 * TOK

TILE_ROWS = [P] * FRAME_TILES + [SM]
TOK_ROWS = [P] * FRAME_TILES + [SAMP]


FRONT = [("k", 0), ("q", 1), ("v", 0), ("u", 1), (("gate", 0, 0), 0), (("out", 0, 0), 1), (("gate", 0, 1), 3),
         (("out", 0, 1), 5), (("gate", 1, 0), 0), (("out", 1, 0), 1), (("gate", 1, 1), 3), (("out", 1, 1), 5),
         (("wo", 0), 0), (("wo", 1), 1)]
SLOT_OF = dict(FRONT)
COUNT_OF = {name: sum(s == slot for _, s in FRONT[:n + 1]) for n, (name, slot) in enumerate(FRONT)}
LOADS = [sum(s == slot for _, s in FRONT) for slot in range(6)]
HIGH = {"k": 2, "q": 3, "v": 2, "u": 3, ("gate", 0, 0): 2, ("out", 0, 0): 1, ("gate", 0, 1): 4, ("out", 0, 1): 5,
        ("gate", 1, 0): 2, ("out", 1, 0): 1, ("gate", 1, 1): 4, ("out", 1, 1): 5, ("wo", 0): 2, ("wo", 1): 3}
PIECE = SLOT // 4
PIECES = {name: 2 if name[0] == "out" else 4 for name in HIGH}
PIECES_BEFORE = {name: sum(list(PIECES.values())[:n]) for n, name in enumerate(PIECES)}


KINDS = ("gate", "up", "down")


def expert_slot(kind, odd):
    return 3 * odd + KINDS.index(kind)


def expert_count(kind, e, odd):
    first = 0 if kind == "down" else 1
    return (e - odd) * 8 + 16 * (LOADS[expert_slot(kind, odd)] + first)


def attention_units():
    units = []
    for pair in range(PAIRS):
        for block in range(FRAME_TILES):
            units += [(pair, block, 0), (pair, block, 1)]
        units.append((pair, FRAME_TILES, 0))
    return units


UNITS = attention_units()
GROUP_OF = []
for _n, (_pair, _block, _hh) in enumerate(UNITS):
    GROUP_OF.append(GROUP_OF[-1] + (_hh == 0) if _n else 0)
KEYS = [META + P * (b + 1) for b in range(FRAME_TILES)] + [PAST + SAMP]
CW = PAST + SAMP + META
FIRST = [CW - k for k in KEYS]


def build(nc, x_prompt, x_sample, cache_k, cache_v, state_pool, meta, norm_mix, w_in, q_norm, k_norm, pool_mix,
          pool_scale, w_pool_out, w_sb_out, w_o, norm_ffn, w_rg, b_rg, w_re, b_re, w_gate, w_up, w_down,
          y_out, nk_prompt, nv_prompt, np_prompt, nk_sample, nv_sample, np_sample, hn_dram):
    with ExitStack() as ctx:
        def sem(name):
            return ctx.enter_context(nc.semaphore(name))

        arena = ctx.enter_context(nc.sbuf_tensor("arena", [P, 53200], F32))
        del arena
        base = 16512
        place = [base]

        def sb(name, shape, dt=F32):
            n = 4 if dt != BF16 else 2
            for s in shape[1:]:
                n *= s
            off = place[0]
            place[0] += (n + 31) // 32 * 32
            return nc.alloc_sbuf_tensor_at(name, shape, dt, offset=off)

        ring = sb("ring", [P, RING, SLOT])
        ring_r = nc.alloc_sbuf_tensor_at("ring_r", [P, RING, SLOT], F32R, offset=base)
        hn_lo = nc.alloc_sbuf_tensor_at("hn_lo", [P, KD, ALL], F32R, offset=base + 4 * 4 * SLOT)
        ident = sb("ident", [P, P])
        ident_b = sb("ident_b", [P, P], BF16)
        mask_p = sb("mask_p", [P, P], BF16)
        mask_s = sb("mask_s", [P, SAMP], BF16)
        tri = sb("tri", [P, P], BF16)
        ones = sb("ones", [P, P], BF16)
        zeros = sb("zeros", [P, CW])
        gain_mix = sb("gain_mix", [P, KD])
        gain_q = sb("gain_q", [P, HD])
        gain_k = sb("gain_k", [P, HD])
        scale_pool = sb("scale_pool", [P, KW])
        mix = sb("mix", [P, KW, P])
        router = sb("router", [P, KD, GROUPS + EXPERTS])
        router_bias = sb("router_bias", [P, GROUPS + EXPERTS])
        iota_e = sb("iota_e", [P, NBLK])
        iota_r = sb("iota_r", [P, 2 * SLOTS])
        iota_j = sb("iota_j", [P, J - 1])
        token = sb("token", [P, TILES])
        half = sb("half", [P, 1])
        empty = sb("empty", [P, 1])
        stat = sb("stat", [P, 4, 8])
        stat_h = sb("stat_h", [P, 3, TILES * HEADS])
        idx = sb("idx", [P, NBLK], I32)
        wgt = sb("wgt", [P, NBLK])
        in_rows = sb("in_rows", [P, 2, 1], I32)
        out_rows = sb("out_rows", [P, 2, 1], I32)
        out_wgt = sb("out_wgt", [P, 2, 1])
        ctl = sb("ctl", [1, 1 + EXTRA], I32)
        hnT = sb("hnT", [P, KD, ALL])
        hnT_lo = nc.alloc_sbuf_tensor_at("hnT_lo", [P, KD, ALL], F32R, offset=place[0] - 4 * KD * ALL)
        merged_hi = nc.alloc_sbuf_tensor_at("merged_hi", [P, KD, TOK], F32R, offset=place[0] - 4 * KD * ALL)
        u_off = place[0]
        sbT = sb("sbT", [P, KW, TOK])
        sb_lo = nc.alloc_sbuf_tensor_at("sb_lo", [P, KW, TOK], F32R, offset=u_off)
        place[0] = u_off
        U = sb("U", [P, KW, UW])
        mixed_lo = nc.alloc_sbuf_tensor_at("mixed_lo", [P, KW, TOK], F32R, offset=place[0])
        mixedT = sb("mixedT", [P, KW, TOK])
        region = place[0]
        hn_hi = nc.alloc_sbuf_tensor_at("hn_hi", [P, KD, ALL], F32R, offset=region)
        kT = sb("kT", [P, PAIRS, ALL])
        qT = sb("qT", [P, PAIRS, ALL])
        pastkT = sb("pastkT", [P, PAIRS, PAST])
        V = sb("V", [P, TILES, W])
        work = place[0]
        pastV = sb("pastV", [P, PAST // P, W])
        after_pv = place[0]
        place[0] = work
        ptmp = sb("ptmp", [P, 2, UW])
        place[0] = region + 2 * 4 * PAIRS * ALL
        xn = sb("xn", [P, 2, D])
        place[0] = work
        pastk = sb("pastk", [P, PAST // P, W])
        place[0] = work - 4 * TILES * W
        square = sb("square", [P, D])
        state_rows = sb("state_rows", [POOL_STATE, W])
        place[0] = after_pv
        xr = sb("xr", [P, TILES, D])
        top_early = place[0]
        place[0] = after_pv
        krow = sb("krow", [P, TILES, W])
        qrow = sb("qrow", [P, TILES, W])
        place[0] = after_pv
        beta = sb("beta", [P, 3, CW])
        keep = sb("keep", [P, 2, CW + 8])
        AT = sb("AT", [P, 2, TILES, P])
        pool_rows = sb("pool_rows", [32 + POOL_STATE, W])
        top = max(place[0], top_early)
        place[0] = region
        mergedT = sb("mergedT", [P, KD, TOK])
        merged_lo = nc.alloc_sbuf_tensor_at("merged_lo", [P, KD, TOK], F32R, offset=region)
        hnT_hi = nc.alloc_sbuf_tensor_at("hnT_hi", [P, KD, ALL], F32R, offset=place[0])
        h = sb("h", [P, TILES, D])
        mixed_hi = nc.alloc_sbuf_tensor_at("mixed_hi", [P, KW, TOK], F32R, offset=place[0])
        sb_hi = nc.alloc_sbuf_tensor_at("sb_hi", [P, KW, TOK], F32R, offset=place[0] + 4 * KW * TOK)
        hn2 = sb("hn2", [P, 2, D])
        turned = place[0]
        hn2T = sb("hn2T", [P, 2, KD, P])
        gain_ffn = sb("gain_ffn", [P, D])
        behind_gates = place[0]
        square2 = sb("square2", [P, D])
        place[0] = behind_gates
        sg = sb("sg", [P, 2, TOK])
        top = max(top, place[0])
        place[0] = region
        logits = sb("logits", [P, TILES, GROUPS + EXPERTS])
        lg8 = sb("lg8", [P, TILES, 8])
        fm = sb("fm", [P, TILES, EXPERTS])
        best_g = sb("best_g", [P, TILES, 8])
        best_e = sb("best_e", [P, TILES, 8])
        at_g = sb("at_g", [P, TILES, 8], U32)
        at_e = sb("at_e", [P, TILES, 8], U32)
        eg = sb("eg", [P, TILES, GROUPS])
        small = sb("small", [P, 12, TILES])
        pick = sb("pick", [P, TOP, TILES])
        hot = sb("hot", [P, TOP, TILES, EXPERTS])
        hot_b = sb("hot_b", [P, TILES, EXPERTS], BF16)
        cnt = sb("cnt", [P, EXPERTS])
        nb = sb("nb", [P, EXPERTS])
        ebase = sb("ebase", [P, 2, EXPERTS])
        prod = sb("prod", [P, TOP, TILES, EXPERTS])
        rank = sb("rank", [P, TOP, TILES])
        past_first = sb("past_first", [P, TOP, TILES])
        base_of = sb("base_of", [P, TOP, TILES])
        blk = sb("blk", [P, TOP, TILES])
        steps10 = sb("steps10", [P, TOP * TILES, J - 1])
        steps_e = sb("steps_e", [P, EXPERTS, J - 1])
        val = sb("val", [P, TOP, TILES, 2])
        etab = sb("etab", [1, EXTRA, EXPERTS])
        efin = sb("efin", [1, 1 + EXTRA])
        tabf = sb("tabf", [P, NBLK])
        assert place[0] <= region + 4 * KD * TOK
        place[0] = turned
        slot_hot = sb("slot_hot", [P, TOP, TILES, 2 * SLOTS])
        blk_hot = sb("blk_hot", [P, TOP, TILES, NBLK])
        blk_val = sb("blk_val", [P, TOP, TILES, 2, NBLK])
        spare = [nc.alloc_sbuf_tensor_at("spare0", [P, KF, D], F32, offset=u_off),
                 nc.alloc_sbuf_tensor_at("spare1", [P, KF, D], F32, offset=region + 4 * KD * TOK)]
        place[0] = u_off - 4 * KD * ALL
        xg = sb("xg", [P, 2, HALF_D])
        xT = sb("xT", [P, 2, KD // 2, 2, SLOTS])
        silu = sb("silu", [P, F // 2])
        hid = sb("hid", [P, F // 2])
        hidT = sb("hidT", [P, KF // 2, 2, SLOTS])
        yb = sb("yb", [P, 2, HALF_D])
        assert place[0] <= u_off and u_off + 4 * SLOT <= region, (place[0], u_off, region)
        assert top <= 229344, top
        ps = ctx.enter_context(nc.psum_tensor("ps", [P, 8, BANK], F32))
        psf = ps[:, :, :].rearrange("p b n -> p (b n)")

        def banks(b, lo, hi, rows=P, first=0):
            return psf[first:first + rows, b * BANK + lo:b * BANK + hi]

        bank_of = [4, 5, 6, 7, 4, 5, 6, 7, 0, 1, 2, 3, 4, 5, 6]

        slot_loaded = [sem(f"slot_loaded{i}") for i in range(RING)]
        x_loaded = [sem(f"x_loaded{t}") for t in range(TILES)]
        gain_loaded = sem("gain_loaded")
        high_made = sem("matrix_high_parts")
        low_made = sem("matrix_low_parts")
        hn_high = sem("hn_high_parts")
        hn_low = sem("hn_low_parts")
        hnT_high = sem("hnT_high_chunks")
        hnT_low = sem("hnT_low_chunks")
        mixed_low = sem("mixed_low_parts")
        sb_high = sem("sb_high_parts")
        sb_low = sem("sb_low_parts")
        merged_high = sem("merged_high_parts")
        merged_low = sem("merged_low_parts")
        consts_loaded = sem("consts_loaded")
        pastk_loaded = sem("pastk_loaded")
        pastv_loaded = sem("pastv_loaded")
        h_loaded = sem("h_loaded")
        gain_ffn_loaded = sem("gain_ffn_loaded")
        consts_made = sem("consts_made")
        step = sem("vector_step")
        stat_ready = sem("sums_initialised")
        attn_init = sem("attention_initialised")
        k_stored = sem("k_stored")
        v_stored = sem("v_stored")
        state_stored = sem("state_stored")
        pstep = sem("pool_step")
        pool_passed = sem("pool_passed")
        sq_done = sem("x_squares")
        ms_done = sem("x_mean_squares")
        root_done = sem("x_roots")
        xn_ready = sem("xn_ready")
        early_T = sem("early_transposes")
        early_out = sem("early_transposes_read")
        xT_made = sem("x_transposed")
        hnT_ready = sem("hnT_ready")
        rows_made = sem("rows_projected")
        rows_sq = sem("rows_squared")
        rows_out = sem("rows_read")
        qk_ms = sem("qk_mean_squares")
        qk_root = sem("qk_roots")
        qk_ready = sem("qk_rows_ready")
        u_made = sem("u_projected")
        u_out = sem("u_read")
        v_out = sem("v_read")
        qkT_made = sem("qk_transposed")
        kT_out = sem("kT_ready")
        qT_out = sem("qT_ready")
        poolT_made = sem("pool_state_transposed")
        poolT_out = sem("pool_state_read")
        pooled = sem("pooled")
        sums_done = sem("pool_sums")
        mix_made = sem("pool_mixed")
        mix_out = sem("mixedT_ready")
        z_made = sem("scores_ready")
        gates_done = sem("beta_keep_ready")
        a_ready = sem("weights_ready")
        AT_made = sem("weights_transposed")
        AT_out = sem("AT_ready")
        pv_made = sem("attention_output")
        pv_out = sem("sbT_ready")
        g_made = sem("gates_projected")
        g_out = sem("gates_sigmoid")
        p_made = sem("branch_projected")
        merged = sem("merged")
        o_made = sem("mixer_output")
        h_ready = sem("h_ready")
        hsq = sem("h_squares")
        hms = sem("h_mean_squares")
        hroot = sem("h_roots")
        hn2_ready = sem("hn2_ready")
        hn2T_made = sem("hn2_transposed")
        hn2T_out = sem("hn2T_ready")
        logits_made = sem("router_logits")
        route_a = sem("router_differences")
        route_e = sem("router_exponentials")
        hot_ready = sem("choices_ready")
        ranks_made = sem("ranks_counted")
        table_in = sem("table_inputs")
        table_made = sem("table_made")
        table_out = sem("table_ready")
        y_stored = sem("y_stored")
        dump_zeroed = sem("dump_zeroed")
        hn_stored = [sem(f"hn_stored{i}") for i in range(2)]
        ins_ready = sem("block_gather_rows_copied")
        outs_ready = sem("block_scatter_rows_copied")
        gathered = [sem(f"gathered{i}") for i in range(2)]
        xg_init = sem("gather_buffers_initialised")
        eT_made = sem("block_transposed")
        eT_out = sem("block_xT_ready")
        wide_made = sem("block_gate_up")
        silu_done = sem("block_silu")
        hid_done = sem("block_hidden")
        hidT_made = sem("block_hidden_transposed")
        hidT_out = sem("block_hidT_ready")
        down_made = sem("block_down")
        y_ready = sem("block_output")
        scattered = [sem(f"scattered{i}") for i in range(2)]
        spare_loaded = [sem(f"spare_loaded{i}") for i in range(2)]
        extra_loaded = sem("extra_weights_loaded")
        extra_gathered = sem("extra_gathered")
        extra_scattered = sem("extra_scattered")

        def loaded(eng, name):
            eng.wait_ge(slot_loaded[SLOT_OF[name]], 16 * COUNT_OF[name])

        def parts(name):
            if name[0] == "out":
                return slice(0, SLOT // 2), slice(SLOT // 2, SLOT)
            return slice(0, SLOT), slice(0, SLOT)

        def high_low(name):
            own, high = parts(name)
            return (ring_r[:, HIGH[name], high].rearrange("p (k n) -> p k n", n=BANK),
                    ring_r[:, SLOT_OF[name], own].rearrange("p (k n) -> p k n", n=BANK))

        def piece(columns, i):
            return slice(columns.start + i * PIECE, columns.start + (i + 1) * PIECE)

        def split_high(name, pieces):
            own, high = parts(name)
            for i in pieces:
                loaded(nc.scalar, name)
                nc.scalar.activation(ring_r[:, HIGH[name], piece(high, i)], ring[:, SLOT_OF[name], piece(own, i)],
                                     ACT.Copy).then_inc(high_made, 1)

        def split_low(name, pieces):
            own, high = parts(name)
            for i in pieces:
                nc.vector.wait_ge(high_made, PIECES_BEFORE[name] + i + 1)
                nc.vector.tensor_tensor(ring_r[:, SLOT_OF[name], piece(own, i)], ring[:, SLOT_OF[name], piece(own, i)],
                                        ring_r[:, HIGH[name], piece(high, i)].bitcast(F32),
                                        ALU.subtract).then_inc(low_made, 1)

        def split_late(split, m):
            for first, br, j in ((0, 0, 1), (5, 1, 0), (9, 1, 1)):
                if m == first:
                    split(("gate", br, j), (0, 1))
                if m == first + 1:
                    split(("gate", br, j), (2, 3))
                    split(("out", br, j), (0, 1))
            if m in (13, 14):
                split(("wo", 0), (0, 1) if m == 13 else (2, 3))

        block = ctx.enter_context(nc.Block())

        @block.sync
        def _(sp):
            win = w_in[0].rearrange("(k p) n -> p k n", p=P)
            src = {"u": win[:, :, 0:W], "q": win[:, :, W:2 * W], "k": win[:, :, 2 * W:3 * W], "v": win[:, :, 3 * W:4 * W]}
            wo = w_o[0].rearrange("(k p) n -> p k n", p=P)
            for br in range(2):
                for j in range(2):
                    c = 4 * W + br * D + j * BANK
                    src["gate", br, j] = win[:, :, c:c + BANK]
                    src["wo", j] = wo[:, :, j * BANK:(j + 1) * BANK]
            for br, w_out in enumerate((w_pool_out, w_sb_out)):
                for j in range(2):
                    src["out", br, j] = w_out[0].rearrange("(k p) n -> p k n", p=P)[:, :, j * BANK:(j + 1) * BANK]

            k_done, q_done, v_done = [(rows_made, (i + 1) * TILES) for i in range(3)]
            u_done = (u_made, KW)
            after = {"v": k_done, "u": q_done, ("gate", 0, 0): v_done, ("out", 0, 0): u_done, ("gate", 0, 1): u_done,
                     ("out", 0, 1): u_done, ("gate", 1, 0): (g_made, 4), ("out", 1, 0): (p_made, 4),
                     ("gate", 1, 1): (g_made, 8), ("out", 1, 1): (p_made, 8), ("wo", 0): (g_made, 12),
                     ("wo", 1): (p_made, 12)}
            for t in range(0, TILES, 2):
                if t < FRAME_TILES:
                    sp.dma_start(xr[:, t, :], x_prompt[0, t * P:(t + 1) * P, :]).then_inc(x_loaded[t], 16)
                else:
                    sp.dma_start(xr[0:SAMP, t, :], x_sample[0]).then_inc(x_loaded[t], 16)
                    sp.dma_start(xr[SAMP:SM, t, :], meta).then_inc(x_loaded[t], 16)
            for name, slot in FRONT:
                if name in after:
                    sp.wait_ge(*after[name])
                sp.dma_start(ring[:, slot, parts(name)[0]].rearrange("p (k n) -> p k n", n=BANK),
                             src[name]).then_inc(slot_loaded[slot], 16)

            def expert_matrix(kind, e, slot, done):
                source = {"gate": w_gate, "up": w_up, "down": w_down}[kind][0, e].rearrange("(k p) n -> p k n", p=P)
                dst = ring[:, slot, :].rearrange("p (k n) -> p k n", n=D if kind == "down" else F)
                sp.dma_start(dst, source).then_inc(done, 16)

            y_rows = y_out.rearrange("(t h) n -> t (h n)", h=2)
            sp.wait_ge(h_loaded, 16 * TILES)
            for kind, e, done in (("up", 1, (g_made, 2 * KD)), ("down", 3, (p_made, 2 * KD)), ("down", 0, None),
                                  ("gate", 0, (o_made, TILES)), ("up", 0, None), ("gate", 1, None), ("down", 2, None),
                                  ("down", 1, (y_stored, 16 * TILES))):
                if (kind, e) == ("gate", 0):
                    for t in range(TILES):
                        n = TOK_ROWS[t]
                        sp.wait_ge(h_ready, t + 1)
                        sp.dma_start(y_rows[t * P:t * P + n, :], h[0:n, t, :]).then_inc(y_stored, 16)
                if done is not None:
                    sp.wait_ge(*done)
                if kind == "down" and e < 2:
                    sp.dma_start(spare[e][:, :, :],
                                 w_down[0, e].rearrange("(k p) n -> p k n", p=P)).then_inc(spare_loaded[e], 16)
                else:
                    slot = expert_slot(kind, e % 2)
                    expert_matrix(kind, e, slot, slot_loaded[slot])

            def refill(kind, e, odd):
                slot = expert_slot(kind, odd)
                sp.wait_ge(down_made if kind == "down" else wide_made, e - 1)
                expert_matrix(kind, e, slot, slot_loaded[slot])

            for e in (2, 3):
                refill("gate", e, e % 2)
                refill("up", e, e % 2)
            with sp.Fori(2, EXPERTS // 2) as it:
                for odd in range(2):
                    for kind in KINDS:
                        refill(kind, it * 2 + odd, odd)

            sp.wait_ge(table_out, 1)
            n_extra = sp.value_load(ctl[0:1, 0:1], min_val=0, max_val=EXTRA)
            with sp.If(n_extra > 0):
                with sp.Fori(0, EXTRA) as i:
                    with sp.If(i < n_extra):
                        e = sp.value_load(ctl[0:1, bass.ds(i + 1, 1)], min_val=0, max_val=EXPERTS - 1)
                        sp.wait_ge(down_made, i + EXPERTS)
                        for slot, kind in enumerate(KINDS):
                            expert_matrix(kind, e, slot, extra_loaded)

            sp.wait_ge(k_stored, 16 * 6)
            sp.wait_ge(v_stored, 16 * 6)
            sp.wait_ge(state_stored, 32)

        @block.gpsimd
        def _(pool):
            count = [0]

            def link(ins):
                count[0] += 1
                ins.then_inc(pstep, 1)
                pool.wait_ge(pstep, count[0])

            pool.memset(ident[:, :], 0.0)
            pool.memset(ones[:, :], 1.0)
            pool.memset(mask_p[:, :], 0.0)
            pool.memset(mask_s[:, :], 0.0)
            link(pool.memset(ident_b[:, :], 0.0))
            pool.affine_select(out=ident[:, :], in_=ident[:, :], compare_op=ALU.not_equal, fill=1.0, base=0,
                               pattern=[[-1, P]], channel_multiplier=1)
            pool.affine_select(out=ident_b[:, :], in_=ident_b[:, :], compare_op=ALU.not_equal, fill=1.0, base=0,
                               pattern=[[-1, P]], channel_multiplier=1)
            link(pool.affine_select(out=mask_p[:, :], in_=mask_p[:, :], compare_op=ALU.is_gt, fill=NEG, base=0,
                                    pattern=[[-1, P]], channel_multiplier=1))
            for hh in range(2):
                m = mask_s[hh * SAMP:(hh + 1) * SAMP, :]
                link(pool.affine_select(out=m, in_=m, compare_op=ALU.is_gt, fill=NEG, base=0,
                                        pattern=[[-1, SAMP]], channel_multiplier=1))
            pool.affine_select(out=tri[:, :], in_=ones[:, :], compare_op=ALU.is_gt, fill=0.0, base=0,
                               pattern=[[1, P]], channel_multiplier=-1)
            pool.iota(iota_e[:, :], [[1, NBLK]], base=0, channel_multiplier=0,
                      allow_small_or_imprecise_dtypes=True)
            pool.iota(iota_r[:, :], [[0, 2], [1, SLOTS]], base=0, channel_multiplier=0,
                      allow_small_or_imprecise_dtypes=True)
            pool.iota(iota_j[:, :], [[SLOTS, J - 1]], base=SLOTS, channel_multiplier=0,
                      allow_small_or_imprecise_dtypes=True)
            pool.iota(empty[:, :], [[0, 1]], base=DUMP, channel_multiplier=1, allow_small_or_imprecise_dtypes=True)
            pool.iota(token[:, :], [[2 * P, TILES]], base=2, channel_multiplier=2, allow_small_or_imprecise_dtypes=True)
            link(pool.memset(half[0:SLOTS, :], -2.0))
            link(pool.memset(half[SLOTS:P, :], -1.0))
            link(pool.memset(zeros[:, :], 0.0))
            pool.tensor_tensor(empty[:, :], empty[:, :], half[:, :], ALU.subtract).then_inc(consts_made, 1)
            pool.dma_start(y_out[DUMP:DUMP + P, :], zeros[:, 0:HALF_D]).then_inc(dump_zeroed, 16)

            pool.dma_start(gain_k[:, :], k_norm.to_broadcast([P, HD])).then_inc(consts_loaded, 16)
            pool.dma_start(gain_q[:, :], q_norm.to_broadcast([P, HD])).then_inc(consts_loaded, 16)
            pool.dma_start(pastk[:, :, :], cache_k.rearrange("(c p) n -> p c n", p=P)).then_inc(pastk_loaded, 16)
            pool.dma_start(state_rows[:, :], state_pool).then_inc(pastk_loaded, 16)
            with nc.allow_non_contiguous_dma(reason="scale by channel, a few KB"):
                pool.dma_start(scale_pool[:, :], pool_scale.rearrange("a (k p) -> p (a k)", p=P)).then_inc(consts_loaded, 16)
            pool.dma_start(mix[:, :, :], pool_mix[0].rearrange("g c d -> c g d")).then_inc(consts_loaded, 16)
            pool.dma_start(router[:, :, 0:GROUPS], w_rg[0].rearrange("(k p) n -> p k n", p=P)).then_inc(consts_loaded, 16)
            pool.dma_start(router[:, :, GROUPS:], w_re[0].rearrange("(k p) n -> p k n", p=P)).then_inc(consts_loaded, 16)
            pool.dma_start(router_bias[:, 0:GROUPS], b_rg.to_broadcast([P, GROUPS])).then_inc(consts_loaded, 16)
            pool.dma_start(router_bias[:, GROUPS:], b_re.to_broadcast([P, EXPERTS])).then_inc(consts_loaded, 16)

            def store_rows(rows, made, need, prompt, sample, done):
                pool.wait_ge(made, need)
                for t in range(FRAME_TILES):
                    pool.dma_start(prompt[META + t * P:META + (t + 1) * P, :], rows[:, t, :]).then_inc(done, 16)
                pool.dma_start(prompt[0:META, :], rows[SAMP:SM, FRAME_TILES, :]).then_inc(done, 16)
                pool.dma_start(sample, rows[0:SAMP, FRAME_TILES, :]).then_inc(done, 16)

            store_rows(krow, qk_ready, 1, nk_prompt, nk_sample, k_stored)
            for g in range(KW):
                pool.wait_ge(u_out, 3 * (g + 1))
                if g == 0:
                    pool.wait_ge(poolT_out, 1)
                source = U[:, g, :]
                for s in range(g + 1):
                    d = 2 ** s
                    lo = 2 * d - 1
                    dst = ptmp[:, s % 2, :]
                    if s == 0 and g >= 1:
                        pool.wait_ge(pooled, g)
                    ins = pool.tensor_tensor(dst[:, lo:UW], source[:, lo:UW], source[:, lo - d:UW - d], ALU.add)
                    if s < g:
                        link(ins)
                    source = dst
                ins.then_inc(sums_done, 1)

            store_rows(V, v_out, TILES, nv_prompt, nv_sample, v_stored)
            pool.wait_ge(pooled, KW)
            pool.dma_start(pastV[:, :, :], cache_v.rearrange("(c p) n -> p c n", p=P)).then_inc(pastv_loaded, 16)
            pool.wait_ge(poolT_out, 3)
            pool.dma_start(np_prompt, pool_rows[0:POOL_STATE, :]).then_inc(state_stored, 16)
            pool.dma_start(np_sample, pool_rows[32:32 + POOL_STATE, :]).then_inc(state_stored, 16)

            pool.wait_ge(pv_out, GROUP_OF[-1] + 1)
            pool.wait_ge(v_stored, 16 * 6)
            pool.wait_ge(state_stored, 32)
            pool.wait_ge(g_made, 2 * KD)
            for t in range(FRAME_TILES):
                pool.dma_start(h[:, t, :], x_prompt[0, t * P:(t + 1) * P, :]).then_inc(h_loaded, 16)
            pool.dma_start(h[0:SAMP, FRAME_TILES, :], x_sample[0]).then_inc(h_loaded, 16)
            pool.wait_ge(p_made, 2 * KD)
            pool.dma_start(gain_ffn[:, :], norm_ffn.to_broadcast([P, D])).then_inc(gain_ffn_loaded, 16)

            hn_rows = hn_dram.rearrange("(t h) n -> t (h n)", h=2)
            for t in range(TILES):
                n = TOK_ROWS[t]
                pool.wait_ge(hn2_ready, t + 1)
                pool.dma_start(hn_rows[t * P:t * P + n, :], hn2[0:n, t % 2, :]).then_inc(hn_stored[t % 2], 16)

            pool.wait_ge(o_made, TILES)
            pool.memset(xg[:, :, :], 0.0).then_inc(xg_init, 1)
            pool.wait_ge(table_out, 1)
            for i in range(2):
                pool.wait_ge(hn_stored[i], 16 * (-(-(TILES - i) // 2)))
            pool.wait_ge(xg_init, 1)

            last_row, last_dump = pool.to_reg(2 * TOK - 1), pool.to_reg(DUMP + P - 1)

            def reached(semaphore, value):
                pool.wait_ge(semaphore, value)
                pool.sem_inc(pool_passed, 1)

            def gather(e, odd, done):
                pool.tensor_copy(in_rows[:, odd, :], idx[:, bass.ds(e, 1)]).then_inc(ins_ready, 1)
                reached(ins_ready, e + 1)
                pool.indirect_dma_start(out=xg[:, odd, :], out_offset=None, in_=hn_dram,
                                        in_offset=bass.IndirectOffsetOnAxis(ap=in_rows[:, odd, :].bitcast(U32), axis=0),
                                        bounds_check=last_row, oob_is_err=False).then_inc(done, 16)

            def out_columns(e, odd):
                pool.tensor_copy(out_rows[:, odd, :], idx[:, bass.ds(e, 1)])
                pool.tensor_copy(out_wgt[:, odd, :], wgt[:, bass.ds(e, 1)]).then_inc(outs_ready, 1)

            def scatter(e, odd, done):
                reached(outs_ready, e + 1)
                reached(y_ready, e + 1)
                pool.indirect_dma_start(out=y_out, in_=yb[:, odd, :], in_offset=None,
                                        out_offset=bass.IndirectOffsetOnAxis(ap=out_rows[:, odd, :].bitcast(U32), axis=0),
                                        bounds_check=last_dump, oob_is_err=True, compute_op=ALU.add).then_inc(done, 16)

            gather(0, 0, gathered[0])
            gather(1, 1, gathered[1])

            def around(e, odd, fetch=True, first=False):
                if fetch:
                    reached(eT_made, e + 1)
                    gather(e + 2, odd, gathered[odd])
                if not first:
                    reached(scattered[odd], (e - odd) * 8)
                out_columns(e, odd)
                if isinstance(e, int) and e == 1:
                    pool.wait_ge(y_stored, 16 * TILES)
                    pool.wait_ge(dump_zeroed, 16)
                if not (isinstance(e, int) and e == 0):
                    scatter(e - 1, 1 - odd, scattered[1 - odd])

            around(0, 0, first=True)
            around(1, 1, first=True)
            with pool.Fori(0, EXPERTS // 2 - 2) as it:
                for odd in range(2):
                    around(it * 2 + (2 + odd), odd)
            around(EXPERTS - 2, 0, fetch=False)
            around(EXPERTS - 1, 1, fetch=False)
            pool.wait_ge(scattered[0], 16 * (EXPERTS // 2))
            scatter(EXPERTS - 1, 1, scattered[1])
            for odd in range(2):
                pool.wait_ge(scattered[odd], 16 * (EXPERTS // 2))

            n_extra = pool.value_load(ctl[0:1, 0:1], min_val=0, max_val=EXTRA)
            with pool.If(n_extra > 0):
                with pool.Fori(0, EXTRA) as i:
                    with pool.If(i < n_extra):
                        gather(i + EXPERTS, 0, extra_gathered)
                        out_columns(i + EXPERTS, 0)
                        scatter(i + EXPERTS, 0, extra_scattered)
                        reached(extra_scattered, i * 16 + 16)

        @block.scalar
        def _(act):
            with nc.allow_non_contiguous_dma(reason="gains by channel, a few KB"):
                act.dma_start(gain_mix[:, :], norm_mix.rearrange("a (k p) -> p (a k)", p=P)).then_inc(gain_loaded, 16)
                for t in range(1, FRAME_TILES, 2):
                    act.dma_start(xr[:, t, :], x_prompt[0, t * P:(t + 1) * P, :]).then_inc(x_loaded[t], 16)

            def square_x(t):
                act.wait_ge(x_loaded[t], 32 if t == FRAME_TILES else 16)
                if t:
                    act.wait_ge(sq_done, t)
                n = TILE_ROWS[t]
                act.activation(square[0:n, :], xr[0:n, t, :], ACT.Square,
                               accum_out=stat[0:n, 0, t:t + 1]).then_inc(sq_done, 1)
                act.wait_ge(ms_done, t + 1)
                act.activation(stat[0:n, 2, t:t + 1], stat[0:n, 1, t:t + 1], ACT.Sqrt).then_inc(root_done, 1)

            def high_hn(t):
                n, c = TILE_ROWS[t], P * t
                act.wait_ge(hnT_ready, t + 1)
                act.activation(hn_hi[:, :, c:c + n], hnT[:, :, c:c + n], ACT.Copy).then_inc(hn_high, 1)

            act.wait_ge(stat_ready, 2)
            square_x(0)
            square_x(1)
            high_hn(0)
            split_high("k", (0, 1))
            square_x(2)
            high_hn(1)
            split_high("k", (2, 3))
            square_x(3)
            high_hn(2)
            square_x(4)
            high_hn(3)
            high_hn(4)

            def past_keys():
                for c in range(PAST // P):
                    act.wait_ge(early_T, c + 2)
                    act.activation(pastkT[:, :, c * P:(c + 1) * P],
                                   ps[:, c % 3, :].rearrange("p (j n) -> p j n", j=PAIRS),
                                   ACT.Copy).then_inc(early_out, 1)

            for n in range(2 * TILES):
                r = TILE_ROWS[n % TILES]
                act.wait_ge(rows_made, n + 1)
                if n >= 2:
                    act.wait_ge(rows_out, n - 1)
                act.activation(square[0:r, (n % 2) * W:(n % 2 + 1) * W], ps[0:r, bank_of[n], :],
                               ACT.Square).then_inc(rows_sq, 1)
                if n < PIECES["q"]:
                    split_high("q", (n,))
                if n >= TILES + 1:
                    split_high("v", (n - TILES - 1,))
                if n == TILES - 1:
                    past_keys()
                if n % TILES == TILES - 1:
                    i = n // TILES
                    act.wait_ge(qk_ms, i + 1)
                    act.activation(stat_h[:, 2, :], stat_h[:, 1, :], ACT.Sqrt).then_inc(qk_root, 1)
            act.wait_ge(rows_out, 2 * TILES)
            for t in range(TILES):
                n = TILE_ROWS[t]
                act.wait_ge(rows_made, 2 * TILES + t + 1)
                act.activation(V[0:n, t, :], ps[0:n, 2 + t, :], ACT.Copy).then_inc(v_out, 1)
                if t < PIECES["u"]:
                    split_high("u", (t,))
            for mt in range(KW):
                b = 2 * mt
                act.wait_ge(u_made, mt + 1)
                first = BANK - ALL // 2
                act.activation(U[:, mt, META:META + SEQ], banks(b, first, first + SEQ), ACT.Copy).then_inc(u_out, 1)
                act.activation(U[:, mt, 0:META], banks(b, first + TOK, first + ALL), ACT.Copy).then_inc(u_out, 1)
                act.activation(U[:, mt, UW - SAMP:UW], banks(b, first + SEQ, first + TOK), ACT.Copy).then_inc(u_out, 1)
                if mt < 3:
                    split_high(("gate", 0, 0), (mt,))
                if mt == 2:
                    act.activation(stat[:, 2, 7:8], stat[:, 2, 6:7], ACT.Sigmoid)
            for t in range(TILES):
                n, c = TILE_ROWS[t], P * t
                act.wait_ge(qkT_made, TILES + t + 1)
                act.activation(qT[:, :, c:c + n], ps[:, (TILES + t) % 8, :].rearrange("p (j n) -> p j n", j=PAIRS)[:, :, 0:n],
                               ACT.Copy).then_inc(qT_out, 1)
            def sigmoids(n):
                pair, b, _ = UNITS[n]
                lo = BANK - META if b < FRAME_TILES else 0
                z = banks(2 * (n % 2), lo, lo + KEYS[b])
                act.wait_ge(z_made, n + 1)
                if n == 0:
                    act.wait_ge(qkT_made, 2 * TILES)
                    act.wait_ge(attn_init, 2)
                if n >= 3:
                    act.wait_ge(AT_made, n - 2)
                act.activation(beta[:, n % 3, FIRST[b]:CW], z, ACT.Sigmoid, scale=HD ** -0.5)
                if n >= 2:
                    act.wait_ge(a_ready, n - 1)
                act.activation(keep[:, n % 2, FIRST[b]:CW], z, ACT.Sigmoid, scale=-HD ** -0.5).then_inc(gates_done, 1)

            def transposed(n):
                pair, b, _ = UNITS[n]
                act.wait_ge(AT_made, n + 1)
                if n >= 2:
                    act.wait_ge(pv_made, n - 1)
                at = 4 + n % 2
                if b < FRAME_TILES:
                    act.activation(AT[:, n % 2, 0:b + 1, :], banks(at, 0, P * (b + 1)).rearrange("p (c n) -> p c n", n=P),
                                   ACT.Copy)
                    act.activation(AT[SAMP:SM, n % 2, FRAME_TILES, :], banks(6, 0, P, META, SAMP),
                                   ACT.Copy).then_inc(AT_out, 1)
                else:
                    act.activation(AT[:, n % 2, 0:FRAME_TILES, :], banks(at, 0, BANK).rearrange("p (c n) -> p c n", n=P),
                                   ACT.Copy)
                    act.activation(AT[0:SAMP, n % 2, FRAME_TILES, :], banks(6, 0, P, SAMP),
                                   ACT.Copy).then_inc(AT_out, 1)

            for n in range(len(UNITS) + 2):
                if n < len(UNITS):
                    sigmoids(n)
                if n >= 2:
                    transposed(n - 2)
                if n == 0:
                    split_high(("gate", 0, 0), (3,))
                if n in (20, 21):
                    split_high(("out", 0, 0), (n - 20,))

            act.wait_ge(pv_out, GROUP_OF[-1] + 1)
            act.wait_ge(v_stored, 16 * 6)
            act.wait_ge(state_stored, 32)
            act.wait_ge(consts_loaded, 16 * 8)

            def mixed(g):
                act.wait_ge(mix_made, g + 1)
                for dst in (mixed_hi, mixedT):
                    last = act.activation(dst[:, g, :], banks(2 * g, BANK - TOK // 2, BANK + TOK // 2), ACT.Copy,
                                          scale=scale_pool[:, g:g + 1])
                last.then_inc(mix_out, 1)

            mixed(0)
            for k in range(KD):
                act.activation(hnT_hi[:, k, 0:TOK], hnT[:, k, 0:TOK], ACT.Copy).then_inc(hnT_high, 1)
            for g in range(1, KW):
                mixed(g)
            for m in range(2 * KD):
                act.wait_ge(g_made, m + 1)
                if m >= 2:
                    act.wait_ge(merged, m - 1)
                act.activation(sg[:, m % 2, :], banks(4 * (m % 2), BANK - TOK // 2, BANK + TOK // 2),
                               ACT.Sigmoid).then_inc(g_out, 1)
                if m == 1:
                    for k in range(KW):
                        act.activation(sb_hi[:, k, :], sbT[:, k, :], ACT.Copy).then_inc(sb_high, 1)
                split_late(split_high, m)
            act.wait_ge(g_made, 2 * KD)
            for k in range(KD):
                act.wait_ge(merged, KD + k + 1)
                act.activation(merged_hi[:, k, :], mergedT[:, k, :], ACT.Copy).then_inc(merged_high, 1)
                if k == KD - 2:
                    split_high(("wo", 1), (0, 1))
            split_high(("wo", 1), (2, 3))
            for t in range(TILES):
                n = TOK_ROWS[t]
                act.wait_ge(h_ready, t + 1)
                act.activation(square2[0:n, :], h[0:n, t, :], ACT.Square,
                               accum_out=stat[0:n, 0, t:t + 1]).then_inc(hsq, 1)
                act.wait_ge(hms, t + 1)
                act.activation(stat[0:n, 2, t:t + 1], stat[0:n, 1, t:t + 1], ACT.Sqrt).then_inc(hroot, 1)
            act.wait_ge(route_a, 1)
            act.activation(eg[:, :, :], eg[:, :, :], ACT.Exp)
            act.activation(small[:, 1, :], small[:, 0, :], ACT.Exp).then_inc(route_e, 1)

            def take_x(e, odd):
                act.wait_ge(eT_made, e + 1)
                act.activation(xT[:, odd, :, :, :], ps[:, odd, :].rearrange("p (c h n) -> p c h n", c=KD // 2, h=2),
                               ACT.Copy).then_inc(eT_out, 1)

            def take_gate(e, odd):
                act.wait_ge(wide_made, e + 1)
                act.activation(silu[:, :], ps[:, 2 + odd, 0:F // 2], ACT.Silu).then_inc(silu_done, 1)

            def take_down(e, odd):
                act.wait_ge(down_made, e + 1)
                act.wait_ge(outs_ready, e + 1)
                act.activation(yb[:, odd, :], ps[:, 6 + odd, :], ACT.Copy, scale=out_wgt[:, odd, :]).then_inc(y_ready, 1)

            take_x(0, 0)
            with act.Fori(0, EXPERTS // 2 - 1) as it:
                for odd in range(2):
                    take_gate(it * 2 + odd, odd)
                    take_x(it * 2 + (1 + odd), 1 - odd)
                    take_down(it * 2 + odd, odd)
            take_gate(EXPERTS - 2, 0)
            take_x(EXPERTS - 1, 1)
            take_down(EXPERTS - 2, 0)
            take_gate(EXPERTS - 1, 1)
            take_down(EXPERTS - 1, 1)

            act.wait_ge(table_out, 1)
            n_extra = act.value_load(ctl[0:1, 0:1], min_val=0, max_val=EXTRA)
            with act.If(n_extra > 0):
                with act.Fori(0, EXTRA) as i:
                    with act.If(i < n_extra):
                        take_x(i + EXPERTS, 0)
                        take_gate(i + EXPERTS, 0)
                        take_down(i + EXPERTS, 0)

        @block.tensor
        def _(pe):
            pe.wait_ge(consts_made, 1)
            def turn_x_tile(t):
                n = TILE_ROWS[t]
                pe.wait_ge(xn_ready, t + 1)
                if t >= 2:
                    pe.wait_ge(hnT_ready, t - 1)
                for k in range(KD):
                    last = pe.transpose(banks(2 * (t % 2), k * P, k * P + n), xn[0:n, t % 2, k * P:(k + 1) * P],
                                        ident[0:n, 0:n])
                last.then_inc(xT_made, 1)

            def turn_past():
                pe.wait_ge(pastk_loaded, 32)
                for g in range(KW):
                    last = pe.transpose(banks(3, g * POOL_STATE, (g + 1) * POOL_STATE), state_rows[:, g * P:(g + 1) * P],
                                        ident[0:POOL_STATE, 0:POOL_STATE])
                last.then_inc(early_T, 1)
                for c in range(PAST // P):
                    if c == 3:
                        pe.wait_ge(early_out, 1)
                    for j in range(PAIRS):
                        last = pe.transpose(banks(c % 3, j * P, (j + 1) * P), pastk[:, c, j * P:(j + 1) * P],
                                            ident[:, :])
                    last.then_inc(early_T, 1)

            def rows_of(out, x_high, x_low, high, low, k, first, last):
                pe.matmul(out, x_high, high[:, k, :], start=first, stop=False)
                pe.matmul(out, x_high, low[:, k, :], start=False, stop=False)
                return pe.matmul(out, x_low, high[:, k, :], start=False, stop=last)

            def project_tile(name, t, bank):
                n, c = TILE_ROWS[t], P * t
                high, low = high_low(name)
                for k in range(KD):
                    if t == 0 and k % 2 == 0:
                        pe.wait_ge(low_made, PIECES_BEFORE[name] + k // 2 + 1)
                    last = rows_of(ps[0:n, bank, :], hn_hi[:, k, c:c + n], hn_lo[:, k, c:c + n], high, low, k, k == 0,
                                   k == KD - 1)
                last.then_inc(rows_made, 1)

            def columns(bank, name, m, x_high, x_low, chunks, cols, ready=None):
                high, low = high_low(name)
                pe.wait_ge(low_made, PIECES_BEFORE[name] + PIECES[name])
                for k in range(chunks):
                    if ready is not None:
                        pe.wait_ge(ready, k + 1)
                    for part, (w, x) in enumerate(((high, x_high), (high, x_low), (low, x_high))):
                        for j in range(2):
                            out = banks(bank, BANK - cols // 2, BANK) if j == 0 else banks(bank + 1, 0, cols // 2)
                            last = pe.matmul(out, w[:, k, m * P:(m + 1) * P], x[:, k, j * cols // 2:(j + 1) * cols // 2],
                                             start=(k + part == 0), stop=(k == chunks - 1 and part == 2))
                return last

            turn_x_tile(0)
            turn_x_tile(1)
            for t in range(TILES):
                pe.wait_ge(hn_low, t + 1)
                if t == TILES - 1:
                    pe.wait_ge(rows_out, 1)
                project_tile("k", t, bank_of[t])
                if t + 2 < TILES:
                    turn_x_tile(t + 2)
            turn_past()
            for t in range(TILES):
                if t < 3:
                    pe.wait_ge(rows_out, t + 2)
                else:
                    pe.wait_ge(early_out, PAST // P)
                project_tile("q", t, bank_of[TILES + t])
            for t in range(TILES):
                if t == 1:
                    pe.wait_ge(poolT_out, 1)
                if t >= 2:
                    pe.wait_ge(rows_out, (0, 0, TILES, TILES + 1, TILES + 2)[t])
                project_tile("v", t, bank_of[2 * TILES + t])
            for mt in range(KW):
                if mt == 0:
                    pe.wait_ge(rows_out, 2 * TILES)
                else:
                    pe.wait_ge(v_out, min(2 * mt, TILES))
                columns(2 * mt, "u", mt, hn_hi, hn_lo, KD, ALL).then_inc(u_made, 1)

            for i in range(2 * TILES):
                rows, t = (krow, qrow)[i // TILES], i % TILES
                n, b = TILE_ROWS[t], i % 8
                if t == 0:
                    pe.wait_ge(qk_ready, i // TILES + 1)
                if i < 8:
                    pe.wait_ge(u_out, 3 * (b // 2 + 1))
                else:
                    pe.wait_ge(kT_out, i - 7)
                for j in range(PAIRS):
                    last = pe.transpose(banks(b, j * P, j * P + n), rows[0:n, t, j * P:(j + 1) * P], ident[0:n, 0:n])
                last.then_inc(qkT_made, 1)
            pe.wait_ge(qT_out, 3)
            for grp, lo in ((0, META + SEQ - POOL_STATE), (1, UW - POOL_STATE)):
                for g in range(KW):
                    last = pe.transpose(banks(6 + grp, g * P, (g + 1) * P, POOL_STATE), U[:, g, lo:lo + POOL_STATE],
                                        ident[:, :])
            last.then_inc(poolT_made, 1)
            def scores(n):
                pair, b, hh = UNITS[n]
                z = 2 * (n % 2)
                if n >= 2:
                    pe.wait_ge(gates_done, n - 1)
                if n == 0:
                    pe.wait_ge(kT_out, TILES)
                    pe.wait_ge(qT_out, TILES)
                if b < FRAME_TILES:
                    rows = slice(hh * HD, (hh + 1) * HD)
                    q = qT[rows, pair, b * P:(b + 1) * P]
                    pe.matmul(banks(z, BANK - META, BANK), q, kT[rows, pair, TOK:ALL], start=True, stop=True)
                    pe.matmul(banks(z + 1, 0, P * (b + 1)), q, kT[rows, pair, 0:P * (b + 1)], start=True,
                              stop=True)
                    pe.matmul(banks(z + 1, P * b, P * (b + 1)), ident_b[:, :], mask_p[:, :], start=False,
                              stop=True, skip_group_check=True).then_inc(z_made, 1)
                else:
                    for s in range(2):
                        rows = slice(s * HD, (s + 1) * HD)
                        q = qT[rows, pair, SEQ:TOK]
                        pe.matmul(banks(z, 0, PAST, SAMP, s * SAMP), q, pastkT[rows, pair, :], start=True, stop=True,
                                  skip_group_check=True)
                        pe.matmul(banks(z + 1, 0, SAMP, SAMP, s * SAMP), q, kT[rows, pair, SEQ:TOK], start=True, stop=False,
                                  skip_group_check=True)
                    pe.matmul(banks(z + 1, 0, SAMP), ident_b[:, :], mask_s[:, :], start=False, stop=True,
                              skip_group_check=True).then_inc(z_made, 1)

            def turn(n):
                pair, b, hh = UNITS[n]
                at = 4 + n % 2
                pe.wait_ge(a_ready, n + 1)
                if n == 0:
                    pe.wait_ge(poolT_out, 3)
                if n >= 2:
                    pe.wait_ge(AT_out, n - 1)
                w = beta[:, n % 3, :]
                if b < FRAME_TILES:
                    lo = FIRST[b]
                    for c in range(b + 1):
                        pe.transpose(banks(at, c * P, (c + 1) * P), w[:, lo + META + c * P:lo + META + (c + 1) * P],
                                     ident[:, :])
                    if n >= 1:
                        pe.wait_ge(AT_out, n)
                    pe.transpose(banks(6, 0, P, SM), w[:, lo - SAMP:lo + META], ident[:, :]).then_inc(AT_made, 1)
                else:
                    lo = FIRST[b]
                    for c in range(PAST // P):
                        pe.transpose(banks(at, c * P, (c + 1) * P), w[:, lo + c * P:lo + (c + 1) * P], ident[:, :])
                    pe.wait_ge(AT_out, n)
                    pe.transpose(banks(6, 0, P, SAMP), w[:, lo + PAST:CW], ident[:, :]).then_inc(AT_made, 1)

            def values(n):
                pair, b, hh = UNITS[n]
                group = GROUP_OF[n]
                pe.wait_ge(AT_out, n + 1)
                if group >= 1 and hh == 0:
                    pe.wait_ge(pv_out, group)
                if b < FRAME_TILES:
                    out = banks(7, BANK - P, BANK, HD, hh * HD)
                    cols = slice((2 * pair + hh) * HD, (2 * pair + hh + 1) * HD)
                    for c in range(b + 1):
                        pe.matmul(out, V[:, c, cols], AT[:, n % 2, c, :], start=(c == 0), stop=False,
                                  skip_group_check=True)
                    pe.matmul(out, V[SAMP:SM, FRAME_TILES, cols], AT[SAMP:SM, n % 2, FRAME_TILES, :], start=False,
                              stop=True, skip_group_check=True).then_inc(pv_made, 1)
                else:
                    if pair == 0:
                        pe.wait_ge(pastv_loaded, 16)
                    for s in range(2):
                        out = banks(7, BANK - P, BANK - P + SAMP, HD, s * HD)
                        cols = slice((2 * pair + s) * HD, (2 * pair + s + 1) * HD)
                        q = slice(s * SAMP, (s + 1) * SAMP)
                        for c in range(PAST // P):
                            pe.matmul(out, pastV[:, c, cols], AT[:, n % 2, c, q], start=(c == 0), stop=False,
                                      skip_group_check=True)
                        last = pe.matmul(out, V[0:SAMP, FRAME_TILES, cols], AT[0:SAMP, n % 2, FRAME_TILES, q],
                                         start=False, stop=True, skip_group_check=True)
                    last.then_inc(pv_made, 1)

            for n in range(len(UNITS) + 3):
                if n < len(UNITS):
                    scores(n)
                if 2 <= n < len(UNITS) + 2:
                    turn(n - 2)
                if n >= 3:
                    values(n - 3)

            pe.wait_ge(pv_out, GROUP_OF[-1] + 1)
            for g in range(KW):
                pe.wait_ge(pooled, g + 1)
                if g == 0:
                    pe.wait_ge(consts_loaded, 16 * 8)
                pe.matmul(banks(2 * g, BANK - TOK // 2, BANK), mix[:, g, :], mixedT[:, g, 0:TOK // 2], start=True, stop=True)
                pe.matmul(banks(2 * g + 1, 0, TOK // 2), mix[:, g, :], mixedT[:, g, TOK // 2:TOK], start=True,
                          stop=True).then_inc(mix_made, 1)
            pe.wait_ge(mix_out, 1)
            for m in range(2 * KD):
                br, mt = m // KD, m % KD
                bank = 4 * (m % 2)
                if m >= 2:
                    pe.wait_ge(merged, m - 1)
                if m == 1:
                    pe.wait_ge(mix_out, KW)
                columns(bank, ("gate", br, mt // 4), mt % 4, hnT_hi, hnT_lo, KD, TOK,
                        hnT_low if m == 0 else None).then_inc(g_made, 1)
                if m == 0:
                    pe.wait_ge(mixed_low, KW)
                if m == KD:
                    pe.wait_ge(sb_low, KW)
                x_high, x_low = ((mixed_hi, mixed_lo), (sb_hi, sb_lo))[br]
                columns(bank + 2, ("out", br, mt // 4), mt % 4, x_high, x_low, KW, TOK).then_inc(p_made, 1)

            def turn_tile(t):
                n = TOK_ROWS[t]
                pe.wait_ge(hn2_ready, t + 1)
                if t >= 1:
                    pe.wait_ge(hn2T_out, t)
                for k in range(KD):
                    last = pe.transpose(banks(4, k * P, k * P + n), hn2[0:n, t % 2, k * P:(k + 1) * P], ident[0:n, 0:n])
                last.then_inc(hn2T_made, 1)

            def route_tile(t):
                n = TOK_ROWS[t]
                pe.wait_ge(hn2T_out, t + 1)
                width = GROUPS + EXPERTS
                for k in range(KD):
                    last = pe.matmul(banks(6, t * width, (t + 1) * width, n), hn2T[:, t % 2, k, 0:n], router[:, k, :],
                                     start=(k == 0), stop=(k == KD - 1), skip_group_check=True)
                last.then_inc(logits_made, 1)

            for t in range(TILES):
                n, c = TOK_ROWS[t], P * t
                if t >= 2:
                    pe.wait_ge(h_ready, t - 1)
                for j in range(2):
                    high, low = high_low(("wo", j))
                    for k in range(KD):
                        if t + j == 0:
                            pe.wait_ge(merged_low, k + 1)
                        if t == 0 and k % 2 == 0:
                            pe.wait_ge(low_made, PIECES_BEFORE["wo", j] + k // 2 + 1)
                        last = rows_of(banks(2 * (t % 2) + j, 0, BANK, n), merged_hi[:, k, c:c + n],
                                       merged_lo[:, k, c:c + n], high, low, k, k == 0, k == KD - 1)
                    if j == 0 and t >= 1:
                        turn_tile(t - 1)
                last.then_inc(o_made, 1)
                if t >= 1:
                    route_tile(t - 1)
            turn_tile(TILES - 1)
            route_tile(TILES - 1)

            pe.wait_ge(hot_ready, 1)
            for t in range(TILES):
                n = TOK_ROWS[t]
                out = banks(0, t * EXPERTS, (t + 1) * EXPERTS)
                for s in range(t):
                    pe.matmul(out, ones[:, :], hot_b[:, s, :], start=(s == 0), stop=False, skip_group_check=True)
                pe.matmul(out, tri[0:n, :], hot_b[0:n, t, :], start=(t == 0), stop=True, skip_group_check=True)
            for t in range(TILES):
                n = TOK_ROWS[t]
                last = pe.matmul(banks(1, 0, EXPERTS), ones[0:n, :], hot_b[0:n, t, :], start=(t == 0), stop=(t == TILES - 1))
            last.then_inc(ranks_made, 1)
            pe.wait_ge(table_in, 1)
            for k in range(TOP):
                for t in range(TILES):
                    n = TOK_ROWS[t]
                    last = pe.matmul(banks(2, 0, 2 * NBLK), slot_hot[0:n, k, t, :],
                                     blk_val[0:n, k, t, :, :].rearrange("p v b -> p (v b)"),
                                     start=(k + t == 0), stop=(k == TOP - 1 and t == TILES - 1))
            last.then_inc(table_made, 1)

            def turn_x(odd):
                for c in range(KD // 2):
                    last = pe.transpose(banks(odd, c * P, (c + 1) * P), xg[:, odd, c * P:(c + 1) * P], ident[:, :])
                last.then_inc(eT_made, 1)

            def wide(e, odd, slot):
                pe.wait_ge(eT_out, e + 1)
                w = ring[:, slot:slot + 2, :].rearrange("p m (k n) -> p k m n", n=F)
                for k in range(KD):
                    for s in range(2):
                        out = banks(2 + odd, 0, BANK, SLOTS, s * SLOTS).rearrange("p (m n) -> p m n", m=2)
                        last = pe.matmul(out, xT[:, odd, k % (KD // 2), k // (KD // 2), :],
                                         w[:, k, :, s * F // 2:(s + 1) * F // 2], start=(k == 0), stop=(k == KD - 1),
                                         skip_group_check=True)
                last.then_inc(wide_made, 1)

            def turn_hidden(e, odd):
                pe.wait_ge(hid_done, e + 1)
                for c in range(KF // 2):
                    last = pe.transpose(banks(4 + odd, c * P, (c + 1) * P), hid[:, c * P:(c + 1) * P], ident[:, :])
                last.then_inc(hidT_made, 1)

            def down(e, odd, slot, first=False):
                pe.wait_ge(hidT_out, e + 1)
                if not first:
                    pe.wait_ge(y_ready, e)
                w = spare[odd][:, :, :] if slot is None else ring[:, slot, :].rearrange("p (k n) -> p k n", n=D)
                for k in range(KF):
                    for s in range(2):
                        last = pe.matmul(banks(6 + odd, 0, BANK, SLOTS, s * SLOTS),
                                         hidT[:, k % (KF // 2), k // (KF // 2), :],
                                         w[:, k, s * HALF_D:(s + 1) * HALF_D], start=(k == 0), stop=(k == KF - 1),
                                         skip_group_check=True)
                last.then_inc(down_made, 1)

            def around(e, odd, first=False, last=False, spare_down=False):
                for kind in ("gate", "up"):
                    pe.wait_ge(slot_loaded[expert_slot(kind, odd)], expert_count(kind, e, odd))
                wide(e, odd, expert_slot("gate", odd))
                if not last:
                    pe.wait_ge(gathered[1 - odd], (e + (odd - 1) + 1) * 8 + 16)
                    turn_x(1 - odd)
                turn_hidden(e, odd)
                if spare_down:
                    pe.wait_ge(spare_loaded[odd], 16)
                    down(e, odd, None, first)
                else:
                    pe.wait_ge(slot_loaded[expert_slot("down", odd)], expert_count("down", e, odd))
                    down(e, odd, expert_slot("down", odd))

            pe.wait_ge(table_out, 1)
            pe.wait_ge(gathered[0], 16)
            turn_x(0)
            around(0, 0, first=True, spare_down=True)
            around(1, 1, spare_down=True)
            with pe.Fori(1, EXPERTS // 2 - 1) as it:
                for odd in range(2):
                    around(it * 2 + odd, odd)
            around(EXPERTS - 2, 0)
            around(EXPERTS - 1, 1, last=True)

            pe.wait_ge(table_out, 1)
            n_extra = pe.value_load(ctl[0:1, 0:1], min_val=0, max_val=EXTRA)
            with pe.If(n_extra > 0):
                with pe.Fori(0, EXTRA) as i:
                    with pe.If(i < n_extra):
                        pe.wait_ge(extra_gathered, i * 16 + 16)
                        turn_x(0)
                        pe.wait_ge(extra_loaded, i * 48 + 48)
                        wide(i + EXPERTS, 0, 0)
                        turn_hidden(i + EXPERTS, 0)
                        down(i + EXPERTS, 0, 2)

        @block.vector
        def _(dve):
            count = [0]

            def link(ins):
                count[0] += 1
                ins.then_inc(step, 1)
                dve.wait_ge(step, count[0])

            dve.memset(stat[:, :, :], 1.0).then_inc(stat_ready, 1)
            dve.memset(stat_h[:, :, :], 1.0).then_inc(stat_ready, 1)
            def norm_x(t):
                n = TILE_ROWS[t]
                dve.wait_ge(sq_done, t + 1)
                if t == 0:
                    dve.wait_ge(stat_ready, 1)
                dve.tensor_scalar(stat[0:n, 1, t:t + 1], stat[0:n, 0, t:t + 1], 1.0 / D, EPS, ALU.mult,
                                  ALU.add).then_inc(ms_done, 1)
                dve.wait_ge(root_done, t + 1)
                link(dve.reciprocal(stat[0:n, 3, t:t + 1], stat[0:n, 2, t:t + 1]))
                if t >= 2:
                    dve.wait_ge(xT_made, t - 1)
                dve.tensor_scalar(xn[0:n, t % 2, :], xr[0:n, t, :], stat[0:n, 3, t:t + 1], None, ALU.mult).then_inc(xn_ready, 1)

            def take_hn(t):
                n, c = TILE_ROWS[t], P * t
                dve.wait_ge(xT_made, t + 1)
                src = banks(2 * (t % 2), 0, 2 * BANK).rearrange("p (k n) -> p k n", k=KD)[:, :, 0:n]
                dve.tensor_tensor(hnT[:, :, c:c + n], src,
                                  gain_mix[:, :].unsqueeze(2).to_broadcast([P, KD, n]), ALU.mult).then_inc(hnT_ready, 1)

            def low_hn(t):
                n, c = TILE_ROWS[t], P * t
                dve.wait_ge(hn_high, t + 1)
                dve.tensor_tensor(hn_lo[:, :, c:c + n], hnT[:, :, c:c + n], hn_hi[:, :, c:c + n].bitcast(F32),
                                  ALU.subtract).then_inc(hn_low, 1)

            norm_x(0)
            norm_x(1)
            dve.wait_ge(gain_loaded, 16)
            take_hn(0)
            low_hn(0)
            split_low("k", (0, 1))
            norm_x(2)
            take_hn(1)
            low_hn(1)
            split_low("k", (2, 3))
            norm_x(3)
            take_hn(2)
            low_hn(2)
            norm_x(4)
            for t in (3, 4):
                take_hn(t)
                low_hn(t)

            dve.wait_ge(stat_ready, 2)
            dve.wait_ge(consts_loaded, 16 * 8)
            for i, (rows, gain) in enumerate(((krow, gain_k), (qrow, gain_q))):
                for t in range(TILES):
                    u = i * TILES + t
                    n = TILE_ROWS[t]
                    dve.wait_ge(rows_made, u + 1)
                    if u == 0:
                        dve.wait_ge(xT_made, TILES)
                    dve.wait_ge(rows_sq, u + 1)
                    dve.tensor_tensor(rows[0:n, t, :].rearrange("p (h d) -> p h d", h=HEADS),
                                      ps[0:n, bank_of[u], :].rearrange("p (h d) -> p h d", h=HEADS),
                                      gain[0:n, :].unsqueeze(1).to_broadcast([n, HEADS, HD]), ALU.mult)
                    dve.tensor_reduce(stat_h[0:n, 0, t * HEADS:(t + 1) * HEADS],
                                      square[0:n, (u % 2) * W:(u % 2 + 1) * W].rearrange("p (h d) -> p h d", h=HEADS),
                                      AX.X, ALU.add).then_inc(rows_out, 1)
                    if i == 0 and t < PIECES["q"]:
                        split_low("q", (t,))
                    if i == 1 and t >= 1:
                        split_low("v", (t - 1,))
                if i == 0:
                    dve.wait_ge(early_T, 1)
                    dve.tensor_copy(U[:, :, META + SEQ:META + SEQ + POOL_STATE],
                                    banks(3, 0, KW * POOL_STATE).rearrange("p (g n) -> p g n", g=KW)).then_inc(poolT_out, 1)
                dve.wait_ge(rows_out, (i + 1) * TILES)
                dve.tensor_scalar(stat_h[:, 1, :], stat_h[:, 0, :], 1.0 / HD, EPS, ALU.mult, ALU.add).then_inc(qk_ms, 1)
                dve.wait_ge(qk_root, i + 1)
                link(dve.reciprocal(stat_h[:, 0, :], stat_h[:, 2, :]))
                for t in range(TILES):
                    n = TILE_ROWS[t]
                    r = rows[0:n, t, :].rearrange("p (h d) -> p h d", h=HEADS)
                    inv = stat_h[0:n, 0, t * HEADS:(t + 1) * HEADS].unsqueeze(2).to_broadcast([n, HEADS, HD])
                    last = dve.tensor_tensor(r, r, inv, ALU.mult)
                last.then_inc(qk_ready, 1)
                dve.wait_ge(qk_ready, i + 1)

            def pool_group(g):
                dve.wait_ge(sums_done, g + 1)
                sums = ptmp[:, g % 2, :]
                for dst, lo, n in ((0, META, SEQ), (SEQ, UW - SAMP, SAMP)):
                    last = dve.scalar_tensor_tensor(out=mixedT[:, g, dst:dst + n], in0=sums[:, lo:lo + n],
                                                    scalar=1.0 / 2 ** (g + 1), in1=U[:, g, lo:lo + n],
                                                    op0=ALU.mult, op1=ALU.subtract)
                last.then_inc(pooled, 1)

            split_low("u", range(PIECES["u"]))
            for g in range(2):
                pool_group(g)
                split_low(("gate", 0, 0), (g,))
            for t in range(TILES):
                n, c = TILE_ROWS[t], P * t
                dve.wait_ge(qkT_made, t + 1)
                dve.tensor_copy(kT[:, :, c:c + n],
                                ps[:, t, :].rearrange("p (j n) -> p j n", j=PAIRS)[:, :, 0:n]).then_inc(kT_out, 1)
            dve.wait_ge(poolT_made, 1)
            for i in range(2):
                dve.tensor_copy(pool_rows[32 * i:32 * i + POOL_STATE, :], ps[0:POOL_STATE, 6 + i, :]).then_inc(poolT_out, 1)

            dve.wait_ge(qkT_made, 2 * TILES)
            dve.wait_ge(k_stored, 16 * 6)
            dve.memset(beta[:, :, :], 0.0).then_inc(attn_init, 1)
            dve.memset(keep[:, :, CW:CW + 1], 1.0).then_inc(attn_init, 1)
            dve.wait_ge(attn_init, 2)
            dve.wait_ge(consts_made, 1)

            def weigh(n):
                pair, b, hh = UNITS[n]
                lo = FIRST[b]
                kp = keep[:, n % 2, :]
                dve.wait_ge(gates_done, n + 1)
                count[0] += 1
                dve.tensor_tensor_scan(kp[:, lo:CW][:, ::-1], kp[:, lo:CW][:, ::-1], zeros[:, lo:CW], 1.0, ALU.mult,
                                       ALU.add).then_inc(step, 1)
                dve.wait_ge(step, count[0])
                dve.tensor_tensor(beta[:, n % 3, lo:CW], beta[:, n % 3, lo:CW], kp[:, lo + 1:CW + 1],
                                  ALU.mult).then_inc(a_ready, 1)

            def take_output(n):
                pair, b, hh = UNITS[n]
                if b < FRAME_TILES and hh == 0:
                    return
                group = GROUP_OF[n]
                dve.wait_ge(pv_made, n + 1)
                if group == 0:
                    dve.wait_ge(poolT_made, 1)
                if b < FRAME_TILES:
                    dve.tensor_copy(sbT[:, pair, b * P:(b + 1) * P],
                                    banks(7, BANK - P, BANK)).then_inc(pv_out, 1)
                else:
                    dve.tensor_copy(sbT[:, pair, SEQ:TOK], banks(7, BANK - P, BANK - P + SAMP)).then_inc(pv_out, 1)

            for n in range(len(UNITS) + 4):
                if n >= 4:
                    take_output(n - 4)
                if n < len(UNITS):
                    weigh(n)
                if n == 0:
                    pool_group(2)
                if n == 3:
                    pool_group(3)
                if n in (1, 2):
                    split_low(("gate", 0, 0), (n + 1,))
                if n in (20, 21):
                    split_low(("out", 0, 0), (n - 20,))

            for k in range(KD):
                dve.wait_ge(hnT_high, k + 1)
                dve.tensor_tensor(hnT_lo[:, k, 0:TOK], hnT[:, k, 0:TOK], hnT_hi[:, k, 0:TOK].bitcast(F32),
                                  ALU.subtract).then_inc(hnT_low, 1)
            for g in range(KW):
                dve.wait_ge(mix_out, g + 1)
                dve.tensor_tensor(mixed_lo[:, g, :], mixedT[:, g, :], mixed_hi[:, g, :].bitcast(F32),
                                  ALU.subtract).then_inc(mixed_low, 1)
            def merged_chunk(k):
                dve.wait_ge(merged_high, k + 1)
                dve.tensor_tensor(merged_lo[:, k, :], mergedT[:, k, :], merged_hi[:, k, :].bitcast(F32),
                                  ALU.subtract).then_inc(merged_low, 1)

            for m in range(2 * KD):
                br, mt = m // KD, m % KD
                proj = banks(4 * (m % 2) + 2, BANK - TOK // 2, BANK + TOK // 2)
                dve.wait_ge(g_out, m + 1)
                if m < 2 * KD - 1:
                    dve.wait_ge(p_made, m + 1)
                if m == 2 * KD - 1:
                    for k in range(KD - 3):
                        merged_chunk(k)
                    dve.wait_ge(p_made, m + 1)
                if br == 0:
                    dve.tensor_tensor(mergedT[:, mt, :], sg[:, m % 2, :], proj, ALU.mult).then_inc(merged, 1)
                else:
                    link(dve.tensor_tensor(sg[:, m % 2, :], sg[:, m % 2, :], proj, ALU.mult))
                    dve.tensor_tensor(mergedT[:, mt, :], mergedT[:, mt, :], sg[:, m % 2, :], ALU.add).then_inc(merged, 1)
                if m == 1:
                    for k in range(KW):
                        dve.wait_ge(sb_high, k + 1)
                        dve.tensor_tensor(sb_lo[:, k, :], sbT[:, k, :], sb_hi[:, k, :].bitcast(F32),
                                          ALU.subtract).then_inc(sb_low, 1)
                split_late(split_low, m)
            merged_chunk(KD - 3)
            merged_chunk(KD - 2)
            merged_chunk(KD - 1)
            split_low(("wo", 1), range(4))

            dve.wait_ge(h_loaded, 16 * TILES)
            dve.wait_ge(gain_ffn_loaded, 16)
            for t in range(TILES):
                n = TOK_ROWS[t]
                dve.wait_ge(o_made, t + 1)
                dve.tensor_tensor(h[0:n, t, :], h[0:n, t, :], banks(2 * (t % 2), 0, 2 * BANK, n), ALU.add).then_inc(h_ready, 1)
                dve.wait_ge(hsq, t + 1)
                dve.tensor_scalar(stat[0:n, 1, t:t + 1], stat[0:n, 0, t:t + 1], 1.0 / D, EPS, ALU.mult,
                                  ALU.add).then_inc(hms, 1)
                dve.wait_ge(hroot, t + 1)
                link(dve.reciprocal(stat[0:n, 3, t:t + 1], stat[0:n, 2, t:t + 1]))
                if t >= 2:
                    dve.wait_ge(hn_stored[t % 2], 16 * (t // 2))
                dve.scalar_tensor_tensor(out=hn2[0:n, t % 2, :], in0=h[0:n, t, :], scalar=stat[0:n, 3, t:t + 1],
                                         in1=gain_ffn[0:n, :], op0=ALU.mult, op1=ALU.mult).then_inc(hn2_ready, 1)
                dve.wait_ge(hn2T_made, t + 1)
                if t >= 2:
                    dve.wait_ge(logits_made, t - 1)
                dve.tensor_copy(hn2T[:, t % 2, :, 0:n],
                                banks(4, 0, 2 * BANK).rearrange("p (k n) -> p k n", k=KD)[:, :, 0:n]).then_inc(hn2T_out, 1)

            width = GROUPS + EXPERTS
            dve.wait_ge(logits_made, TILES)
            dve.memset(logits[:, :, :], 0.0)
            link(dve.memset(lg8[:, :, :], NEG))
            for t in range(TILES):
                n = TOK_ROWS[t]
                last = dve.tensor_tensor(logits[0:n, t, :], banks(6, t * width, (t + 1) * width, n), router_bias[0:n, :],
                                         ALU.add)
            link(last)
            link(dve.tensor_copy(lg8[:, :, 0:GROUPS], logits[:, :, 0:GROUPS]))
            for t in range(TILES):
                last = dve.max(best_g[:, t, :], lg8[:, t, :])
            link(last)
            for t in range(TILES):
                last = dve.max_index(at_g[:, t, :], best_g[:, t, :], lg8[:, t, :])
            link(last)
            wide3 = [P, TILES, EXPERTS]

            def over_e(ap):
                return ap.unsqueeze(2).to_broadcast(wide3)

            group_of = small[:, 2, :]
            link(dve.tensor_copy(group_of, at_g[:, :, 0:1].rearrange("p t a -> p (t a)")))
            wide4 = [P, TILES, GROUPS, PER_GROUP]
            at_group = [P, TILES, GROUPS]
            link(dve.tensor_tensor(eg[:, :, :], iota_e[:, 0:GROUPS].unsqueeze(1).to_broadcast(at_group),
                                   group_of.unsqueeze(2).to_broadcast(at_group), ALU.is_equal))
            link(dve.tensor_scalar(eg[:, :, :], eg[:, :, :], -NEG, NEG, ALU.mult, ALU.add))
            link(dve.tensor_tensor(fm[:, :, :].rearrange("p t (g e) -> p t g e", g=GROUPS),
                                   logits[:, :, GROUPS:].rearrange("p t (g e) -> p t g e", g=GROUPS),
                                   eg[:, :, :].unsqueeze(3).to_broadcast(wide4), ALU.add))
            for t in range(TILES):
                last = dve.max(best_e[:, t, :], fm[:, t, :])
            link(last)
            for t in range(TILES):
                last = dve.max_index(at_e[:, t, :], best_e[:, t, :], fm[:, t, :])
            link(last)
            dve.tensor_tensor(eg[:, :, :], logits[:, :, 0:GROUPS],
                              best_g[:, :, 0:1].to_broadcast([P, TILES, GROUPS]), ALU.subtract)
            dve.tensor_tensor(small[:, 0, :], best_e[:, :, 1:2].rearrange("p t a -> p (t a)"),
                              best_e[:, :, 0:1].rearrange("p t a -> p (t a)"), ALU.subtract).then_inc(route_a, 1)
            for k in range(TOP):
                last = dve.tensor_copy(pick[:, k, :], at_e[:, :, k:k + 1].rearrange("p t a -> p (t a)"))
            link(last)
            for k in range(TOP):
                last = dve.tensor_tensor(hot[:, k, :, :], iota_e[:, 0:EXPERTS].unsqueeze(1).to_broadcast(wide3),
                                         over_e(pick[:, k, :]), ALU.is_equal)
            link(last)
            dve.tensor_tensor(hot_b[:, :, :], hot[:, 0, :, :], hot[:, 1, :, :], ALU.add).then_inc(hot_ready, 1)
            dve.wait_ge(route_e, 1)
            link(dve.tensor_reduce(small[:, 4, :], eg[:, :, :], AX.X, ALU.add))
            link(dve.tensor_scalar(small[:, 5, :], small[:, 1, :], 1.0, None, ALU.add))
            link(dve.tensor_tensor(small[:, 6, :], small[:, 4, :], small[:, 5, :], ALU.mult))
            link(dve.reciprocal(small[:, 7, :], small[:, 6, :]))
            dve.tensor_copy(val[:, 0, :, 1], small[:, 7, :])
            dve.tensor_tensor(val[:, 1, :, 1], small[:, 7, :], small[:, 1, :], ALU.mult)
            dve.tensor_copy(val[:, 0, :, 0], token[:, :])
            link(dve.tensor_copy(val[:, 1, :, 0], token[:, :]))

            dve.wait_ge(ranks_made, 1)
            link(dve.tensor_copy(cnt[:, :], banks(1, 0, EXPERTS)))
            over = [P, EXPERTS, J - 1]
            link(dve.tensor_tensor(steps_e[:, :, :], cnt[:, :].unsqueeze(2).to_broadcast(over),
                                   iota_j[:, :].unsqueeze(1).to_broadcast(over), ALU.is_gt))
            link(dve.tensor_reduce(nb[:, :], steps_e[:, :, :], AX.X, ALU.add))
            link(dve.tensor_tensor_scan(ebase[:, 1, :], zeros[:, 0:EXPERTS], nb[:, :], 0.0, ALU.add, ALU.add))
            link(dve.tensor_tensor(ebase[:, 0, :], ebase[:, 1, :], nb[:, :], ALU.subtract))
            for k in range(TOP):
                last = dve.tensor_tensor(prod[:, k, :, :], hot[:, k, :, :],
                                         banks(0, 0, TILES * EXPERTS).rearrange("p (t e) -> p t e", t=TILES), ALU.mult)
            link(last)
            link(dve.tensor_reduce(rank[:, :, :], prod[:, :, :, :], AX.X, ALU.add))
            link(dve.tensor_tensor(prod[:, :, :, :].rearrange("p k t e -> p (k t) e"),
                                   hot[:, :, :, :].rearrange("p k t e -> p (k t) e"),
                                   ebase[:, 0, :].unsqueeze(1).to_broadcast([P, TOP * TILES, EXPERTS]), ALU.mult))
            link(dve.tensor_reduce(base_of[:, :, :], prod[:, :, :, :], AX.X, ALU.add))
            over = [P, TOP * TILES, J - 1]
            dve.tensor_scalar(past_first[:, :, :], rank[:, :, :], float(SLOTS), None, ALU.is_ge)
            link(dve.tensor_tensor(steps10[:, :, :], rank[:, :, :].rearrange("p k t -> p (k t)").unsqueeze(2).to_broadcast(over),
                                   iota_j[:, :].unsqueeze(1).to_broadcast(over), ALU.is_ge))
            link(dve.tensor_reduce(blk[:, :, :], steps10[:, :, :].rearrange("p (k t) j -> p k t j", k=TOP), AX.X, ALU.add))
            link(dve.scalar_tensor_tensor(out=rank[:, :, :], in0=blk[:, :, :], scalar=-float(SLOTS), in1=rank[:, :, :],
                                          op0=ALU.mult, op1=ALU.add))
            link(dve.tensor_tensor(blk[:, :, :], blk[:, :, :], base_of[:, :, :], ALU.add))
            link(dve.tensor_scalar(blk[:, :, :], blk[:, :, :], float(EXPERTS - 1), None, ALU.add))
            link(dve.tensor_tensor(blk[:, :, :], blk[:, :, :], pick[:, :, :], ALU.subtract))
            link(dve.tensor_tensor(blk[:, :, :], blk[:, :, :], past_first[:, :, :], ALU.mult))
            link(dve.tensor_tensor(blk[:, :, :], blk[:, :, :], pick[:, :, :], ALU.add))
            kt = TOP * TILES
            dve.tensor_tensor(slot_hot[:, :, :, :].rearrange("p k t s -> p (k t) s"),
                              iota_r[:, :].unsqueeze(1).to_broadcast([P, kt, 2 * SLOTS]),
                              rank[:, :, :].rearrange("p k t -> p (k t)").unsqueeze(2).to_broadcast([P, kt, 2 * SLOTS]),
                              ALU.is_equal)
            link(dve.tensor_tensor(blk_hot[:, :, :, :].rearrange("p k t s -> p (k t) s"),
                                   iota_e[:, :].unsqueeze(1).to_broadcast([P, kt, NBLK]),
                                   blk[:, :, :].rearrange("p k t -> p (k t)").unsqueeze(2).to_broadcast([P, kt, NBLK]),
                                   ALU.is_equal))
            for v in range(2):
                last = dve.tensor_tensor(blk_val[:, :, :, v, :].rearrange("p k t s -> p (k t) s"),
                                         blk_hot[:, :, :, :].rearrange("p k t s -> p (k t) s"),
                                         val[:, :, :, v].rearrange("p k t -> p (k t)").unsqueeze(2).to_broadcast([P, kt, NBLK]),
                                         ALU.mult)
            last.then_inc(table_in, 1)
            for i in range(EXTRA):
                last = dve.tensor_scalar(etab[:, i, :], ebase[0:1, 1, :], float(i), None, ALU.is_le)
            link(last)
            link(dve.tensor_reduce(efin[:, 1:1 + EXTRA], etab[:, :, :], AX.X, ALU.add))
            link(dve.tensor_scalar(efin[:, 1:1 + EXTRA], efin[:, 1:1 + EXTRA], float(EXPERTS - 1), None, ALU.min))
            link(dve.tensor_copy(efin[:, 0:1], ebase[0:1, 1, EXPERTS - 1:EXPERTS]))
            link(dve.tensor_copy(ctl[:, :], efin[:, :]))
            dve.wait_ge(table_made, 1)
            table = banks(2, 0, 2 * NBLK).rearrange("p (v b) -> p v b", v=2)
            link(dve.tensor_scalar(tabf[:, :], table[:, 0, :], 0.0, empty[:, :], ALU.is_equal, ALU.mult))
            link(dve.tensor_tensor(tabf[:, :], tabf[:, :], table[:, 0, :], ALU.add))
            link(dve.tensor_scalar(tabf[:, :], tabf[:, :], half[:, :], None, ALU.add))
            dve.tensor_copy(wgt[:, :], table[:, 1, :])
            dve.tensor_copy(idx[:, :], tabf[:, :]).then_inc(table_out, 1)

            def take_up(e, odd):
                dve.wait_ge(silu_done, e + 1)
                dve.tensor_tensor(hid[:, :], silu[:, :], ps[:, 2 + odd, F // 2:F], ALU.mult).then_inc(hid_done, 1)

            def take_hidden(e, odd):
                dve.wait_ge(hidT_made, e + 1)
                dve.tensor_copy(hidT[:, :, :, :],
                                banks(4 + odd, 0, F // 2).rearrange("p (c h n) -> p c h n", c=KF // 2, h=2)
                                ).then_inc(hidT_out, 1)

            with dve.Fori(0, EXPERTS // 2) as it:
                for odd in range(2):
                    take_up(it * 2 + odd, odd)
                    take_hidden(it * 2 + odd, odd)

            n_extra = dve.value_load(ctl[0:1, 0:1], min_val=0, max_val=EXTRA)
            with dve.If(n_extra > 0):
                with dve.Fori(0, EXTRA) as i:
                    with dve.If(i < n_extra):
                        take_up(i + EXPERTS, 0)
                        take_hidden(i + EXPERTS, 0)


_INS = ["x_prompt", "x_sample", "cache_sb_k", "cache_sb_v", "state_pool", "meta_tokens", "norm_mix", "w_in", "q_norm",
        "k_norm", "pool_mix", "pool_scale", "w_pool_out", "w_sb_out", "w_o", "norm_ffn", "w_router_group",
        "b_router_group", "w_router_expert", "b_router_expert", "w_gate", "w_up", "w_down"]


def kernel(**inputs):
    import numpy as _np
    import concourse.bacc as _bacc
    from concourse import mybir as _mybir
    from concourse.bass_utils import run_bass_kernel_spmd as _run

    nc = _bacc.Bacc("TRN2", target_bir_lowering=False, num_devices=1)
    arrays, args = {}, []
    for name in _INS:
        a = _np.ascontiguousarray(inputs[name])
        if name in ("cache_sb_k", "cache_sb_v"):
            a = a.reshape(PAST, W)
        if name == "state_pool":
            a = a.reshape(POOL_STATE, W)
        arrays[f"in_{name}_dram"] = a
        args.append(nc.dram_tensor(f"in_{name}_dram", a.shape, _mybir.dt.from_np(a.dtype), kind="ExternalInput").ap())
    outs = {"y": (DUMP + P, HALF_D), "nk_prompt": (META + SEQ, W), "nv_prompt": (META + SEQ, W), "np_prompt": (POOL_STATE, W),
            "nk_sample": (SAMP, W), "nv_sample": (SAMP, W), "np_sample": (POOL_STATE, W)}
    for name, shape in outs.items():
        args.append(nc.dram_tensor(f"out_{name}_dram", shape, F32, kind="ExternalOutput").ap())
    args.append(nc.dram_tensor("hn_dram", (2 * TOK, D // 2), F32, kind="Internal").ap())
    build(nc, *args)
    r = _run(nc, [arrays], core_ids=[0])
    got = {name: r.results[0][f"out_{name}_dram"] for name in outs}
    heads = (HEADS, HD)
    return (got["y"][:2 * SEQ].reshape(1, SEQ, D), got["y"][2 * SEQ:DUMP].reshape(1, SAMP, D),
            got["nk_prompt"].reshape(1, 1, META + SEQ, *heads), got["nv_prompt"].reshape(1, 1, META + SEQ, *heads),
            got["np_prompt"].reshape(1, 1, POOL_STATE, W),
            got["nk_sample"].reshape(1, 1, SAMP, *heads), got["nv_sample"].reshape(1, 1, SAMP, *heads),
            got["np_sample"].reshape(1, 1, POOL_STATE, W))
```
